# Optimizing a Trainium2 kernel written in Bass

```python
import jax
import jax.numpy as jnp
from jax import lax
import numpy as np
import math
import jax, jax.numpy as jnp

D_MODEL = 1024
BATCH = 1
SEQ = 256
DEPTH = 2

CTX_LEN = 256
GRID_W = 64
HEAD_DIM = D_MODEL // 16
N_FOURIER_GROUPS = 4
N_NA_HEADS = 4
N_GLA_HEADS = 4
N_GQA_HEADS = 4
N_GQA_KV_HEADS = 2
GQA_GROUP = N_GQA_HEADS // N_GQA_KV_HEADS
GLA_DK = HEAD_DIM // 2
GLA_DV = HEAD_DIM
GLA_GATE_RANK = 16
GLA_TAU = 16.0
GLA_CHUNK = 64
NA_ROWS = 8
NA_COLS = 16
Q_BLOCK = 128
D_FF = 256 * ((8 * D_MODEL // 3 + 255) // 256)
ROPE_THETA = 10000.0
EPS = 1e-6
N_MOD = 9

W_FOURIER = N_FOURIER_GROUPS * HEAD_DIM
W_NA = N_NA_HEADS * HEAD_DIM
W_GLA = N_GLA_HEADS * GLA_DV
W_GQA = N_GQA_HEADS * HEAD_DIM
D_MIX = W_FOURIER + W_NA + W_GLA + W_GQA

IN_LAYOUT = (
    ('fourier', W_FOURIER),
    ('na_q', W_NA), ('na_k', W_NA), ('na_v', W_NA),
    ('gla_q', N_GLA_HEADS * GLA_DK), ('gla_k', N_GLA_HEADS * GLA_DK),
    ('gla_v', W_GLA), ('gla_r', W_GLA),
    ('gla_gf', GLA_GATE_RANK), ('gla_gb', GLA_GATE_RANK),
    ('gqa_q', W_GQA), ('gqa_k', N_GQA_KV_HEADS * HEAD_DIM), ('gqa_v', N_GQA_KV_HEADS * HEAD_DIM),
)
D_IN = sum(w for _, w in IN_LAYOUT)


def rms_norm(x, gain=None):
    xf = x.astype(jnp.float32)
    y = xf * lax.rsqrt(jnp.mean(xf * xf, axis=-1, keepdims=True) + EPS)
    if gain is not None:
        y = y * gain.astype(jnp.float32)
    return y.astype(x.dtype)

def modulate(h, shift, scale):
    return h * (1.0 + scale) + shift

def swiglu(h, w1, w3, w2):
    return (jax.nn.silu(h @ w1) * (h @ w3)) @ w2

def heads(t, n, d):
    return t.reshape(t.shape[:-1] + (n, d))

def split_in(h):
    offsets = np.cumsum([w for _, w in IN_LAYOUT])[:-1].tolist()
    parts = jnp.split(h, offsets, axis=-1)
    return {name: part for (name, _), part in zip(IN_LAYOUT, parts)}

def axial_rope(n_tokens):
    t = jnp.arange(n_tokens, dtype=jnp.int32)
    row = (t // GRID_W).astype(jnp.float32)
    col = (t % GRID_W).astype(jnp.float32)
    n_freq = HEAD_DIM // 4
    inv_freq = ROPE_THETA ** (-jnp.arange(n_freq, dtype=jnp.float32) / n_freq)
    ang = jnp.concatenate([row[:, None] * inv_freq, col[:, None] * inv_freq], axis=-1)
    return jnp.cos(ang)[:, None, :], jnp.sin(ang)[:, None, :]

def apply_rope(x, cos, sin):
    xf = x.astype(jnp.float32)
    x1, x2 = jnp.split(xf, 2, axis=-1)
    return jnp.concatenate([x1 * cos - x2 * sin, x1 * sin + x2 * cos], axis=-1).astype(x.dtype)

def fourier_mix(u):
    b_, l_, _ = u.shape
    uf = u.astype(jnp.float32).reshape(b_, l_, N_FOURIER_GROUPS, HEAD_DIM)
    y = jnp.fft.fft2(uf, axes=(1, 3), norm='ortho').real
    return y.reshape(b_, l_, W_FOURIER).astype(u.dtype)

def block_attention(q, k, v):
    b_, lq, hk, g, dh = q.shape
    nb = lq // Q_BLOCK
    qb = (q * dh ** -0.5).reshape(b_, nb, Q_BLOCK, hk, g, dh).swapaxes(0, 1)

    def one_block(q_blk):
        s = jnp.einsum('bqhgd,bkhd->bhgqk', q_blk, k).astype(jnp.float32)
        p = jax.nn.softmax(s, axis=-1).astype(v.dtype)
        return jnp.einsum('bhgqk,bkhd->bqhgd', p, v)

    o = lax.map(one_block, qb)
    return o.swapaxes(0, 1).reshape(b_, lq, hk * g * dh)

def neighborhood_attention(q, k, v, k_ctx, v_ctx, rpb):
    b_, s_, h_, dh = q.shape
    rows = s_ // GRID_W
    kr = min(NA_ROWS, rows)
    kg = k.reshape(b_, rows, GRID_W, h_, dh)
    vg = v.reshape(b_, rows, GRID_W, h_, dh)
    qg = q.reshape(b_, rows, GRID_W, h_, dh).transpose(1, 0, 2, 3, 4)
    r_pos = jnp.arange(rows)
    c_pos = jnp.arange(GRID_W)
    row_start = jnp.clip(r_pos - kr // 2, 0, rows - kr)
    rel_row = row_start[:, None] + jnp.arange(kr)[None, :] - r_pos[:, None]
    col_start = jnp.clip(c_pos - NA_COLS // 2, 0, GRID_W - NA_COLS)
    col_idx = col_start[:, None] + jnp.arange(NA_COLS)[None, :]
    rel_col = col_idx - c_pos[:, None]
    bias_col = rpb.astype(jnp.float32)[:, :, rel_col + NA_COLS - 1]
    scale = dh ** -0.5
    n_win = kr * NA_COLS

    def row_block(args):
        q_r, rs, rr = args
        k_blk = lax.dynamic_slice_in_dim(kg, rs, kr, axis=1)[:, :, col_idx]
        v_blk = lax.dynamic_slice_in_dim(vg, rs, kr, axis=1)[:, :, col_idx]
        bias = bias_col[:, rr + NA_ROWS - 1].transpose(0, 2, 1, 3)
        s_win = jnp.einsum('bchd,brckhd->bhcrk', q_r, k_blk).astype(jnp.float32) * scale + bias[None]
        s_ctx = jnp.einsum('bchd,bjhd->bhcj', q_r, k_ctx).astype(jnp.float32) * scale
        s = jnp.concatenate([s_win.reshape(b_, h_, GRID_W, n_win), s_ctx], axis=-1)
        p = jax.nn.softmax(s, axis=-1).astype(v.dtype)
        p_win = p[..., :n_win].reshape(b_, h_, GRID_W, kr, NA_COLS)
        p_ctx = p[..., n_win:]
        return (jnp.einsum('bhcrk,brckhd->bchd', p_win, v_blk)
                + jnp.einsum('bhcj,bjhd->bchd', p_ctx, v_ctx))

    out = lax.map(row_block, (qg, row_start, rel_row))
    return out.transpose(1, 0, 2, 3, 4).reshape(b_, s_, h_ * dh)

def gla_scan(q, k, v, log_a, s0):
    b_, h_, l_, _ = q.shape
    dv = v.shape[-1]
    n_chunks = l_ // GLA_CHUNK

    def chunks(t):
        return t.reshape(b_, h_, n_chunks, GLA_CHUNK, t.shape[-1]).transpose(2, 0, 1, 3, 4)

    lower_tri = jnp.tril(jnp.ones((GLA_CHUNK, GLA_CHUNK), dtype=bool))[None, None, :, :, None]

    def step(s, inp):
        qc, kc, vc, ac = inp
        qf, kf, vf = (t.astype(jnp.float32) for t in (qc, kc, vc))
        b = jnp.cumsum(ac.astype(jnp.float32), axis=2)
        rel = b[:, :, :, None, :] - b[:, :, None, :, :]
        decay = jnp.where(lower_tri, jnp.exp(jnp.minimum(rel, 0.0)), 0.0)
        scores = jnp.einsum('bhid,bhjd,bhijd->bhij', qf, kf, decay)
        o = (jnp.einsum('bhcd,bhde->bhce', qf * jnp.exp(b), s)
             + jnp.einsum('bhij,bhje->bhie', scores, vf))
        b_last = b[:, :, -1:, :]
        s_new = (jnp.exp(b_last[:, :, 0, :])[..., None] * s
                 + jnp.einsum('bhcd,bhce->bhde', kf * jnp.exp(b_last - b), vf))
        return s_new, o.astype(v.dtype)

    s_final, o = lax.scan(step, s0, (chunks(q), chunks(k), chunks(v), chunks(log_a)))
    return o.transpose(1, 2, 0, 3, 4).reshape(b_, h_, l_, dv), s_final

def bidir_gla(q, k, v, a_f, a_b, s0_f, s0_b):
    flip = lambda t: jnp.flip(t, axis=2)
    o_f, s_f = gla_scan(q, k, v, a_f, s0_f)
    o_b, s_b = gla_scan(flip(q), flip(k), flip(v), flip(a_b), s0_b)
    return o_f + flip(o_b), s_f, s_b

def gla_prepare(p, w_gf, b_gf, w_gb, b_gb):
    to_bhld = lambda t, d: heads(t, N_GLA_HEADS, d).transpose(0, 2, 1, 3)
    q = to_bhld(p['gla_q'] * GLA_DK ** -0.5, GLA_DK)
    k = to_bhld(p['gla_k'], GLA_DK)
    v = to_bhld(p['gla_v'], GLA_DV)
    a_f = to_bhld(jax.nn.log_sigmoid((p['gla_gf'] @ w_gf + b_gf).astype(jnp.float32)) / GLA_TAU, GLA_DK)
    a_b = to_bhld(jax.nn.log_sigmoid((p['gla_gb'] @ w_gb + b_gb).astype(jnp.float32)) / GLA_TAU, GLA_DK)
    return q, k, v, a_f, a_b

def gla_output(o, r, gain):
    b_, _, l_, _ = o.shape
    o = rms_norm(o.transpose(0, 2, 1, 3), gain).reshape(b_, l_, W_GLA)
    return o * jax.nn.silu(r)

def token_mixing(hx, hz, cos, sin, na_q_norm, na_k_norm, na_rpb, gla_w_gate_f, gla_b_gate_f,
                 gla_w_gate_b, gla_b_gate_b, gla_norm, gqa_q_norm, gqa_k_norm, with_ctx_out):
    px, pz = split_in(hx), split_in(hz)
    b_, s_ = hx.shape[0], hx.shape[1]
    lc = hz.shape[1]
    a_x = fourier_mix(px['fourier'])
    na_q = lambda p: rms_norm(heads(p['na_q'], N_NA_HEADS, HEAD_DIM), na_q_norm)
    na_k = lambda p: rms_norm(heads(p['na_k'], N_NA_HEADS, HEAD_DIM), na_k_norm)
    na_v = lambda p: heads(p['na_v'], N_NA_HEADS, HEAD_DIM)
    kz_na, vz_na = na_k(pz), na_v(pz)
    b_x = neighborhood_attention(na_q(px), na_k(px), na_v(px), kz_na, vz_na, na_rpb)
    gates = (gla_w_gate_f, gla_b_gate_f, gla_w_gate_b, gla_b_gate_b)
    s0 = jnp.zeros((b_, N_GLA_HEADS, GLA_DK, GLA_DV), jnp.float32)
    oz_gla, s_f, s_b = bidir_gla(*gla_prepare(pz, *gates), s0, s0)
    ox_gla, _, _ = bidir_gla(*gla_prepare(px, *gates), s_f, s_b)
    c_x = gla_output(ox_gla, px['gla_r'], gla_norm)
    gqa_q = lambda p: rms_norm(heads(p['gqa_q'], N_GQA_HEADS, HEAD_DIM), gqa_q_norm)
    gqa_k = lambda p: rms_norm(heads(p['gqa_k'], N_GQA_KV_HEADS, HEAD_DIM), gqa_k_norm)
    gqa_v = lambda p: heads(p['gqa_v'], N_GQA_KV_HEADS, HEAD_DIM)
    kz_gqa, vz_gqa = gqa_k(pz), gqa_v(pz)
    qx_gqa = apply_rope(gqa_q(px), cos, sin).reshape(b_, s_, N_GQA_KV_HEADS, GQA_GROUP, HEAD_DIM)
    kx_gqa = apply_rope(gqa_k(px), cos, sin)
    d_x = block_attention(qx_gqa, jnp.concatenate([kx_gqa, kz_gqa], axis=1),
                          jnp.concatenate([gqa_v(px), vz_gqa], axis=1))
    out_x = jnp.concatenate([a_x, b_x, c_x, d_x], axis=-1)
    if not with_ctx_out:
        return out_x, None
    a_z = fourier_mix(pz['fourier'])
    b_z = block_attention(na_q(pz)[:, :, :, None, :], kz_na, vz_na)
    c_z = gla_output(oz_gla, pz['gla_r'], gla_norm)
    d_z = block_attention(gqa_q(pz).reshape(b_, lc, N_GQA_KV_HEADS, GQA_GROUP, HEAD_DIM), kz_gqa, vz_gqa)
    return out_x, jnp.concatenate([a_z, b_z, c_z, d_z], axis=-1)

def first_inputs(seed: int = 0) -> dict:
    key = jax.random.key(seed)
    ks = iter(jax.random.split(key, 32))
    f32 = jnp.float32

    def nrm(shape, std):
        return jax.random.normal(next(ks), shape, f32) * std

    L, D = DEPTH, D_MODEL
    return {
        'x': nrm((BATCH, SEQ, D), 1.0),
        'c': nrm((BATCH, D), 1.0),
        'ctx': nrm((BATCH, CTX_LEN, D), 1.0),
        'c_ctx': nrm((D,), 1.0),
        'w_mod': nrm((L, D, N_MOD * D), 0.5 * D ** -0.5),
        'b_mod': nrm((L, N_MOD * D), 0.02),
        'ffn1_w1': nrm((L, D, D_FF), D ** -0.5),
        'ffn1_w3': nrm((L, D, D_FF), D ** -0.5),
        'ffn1_w2': nrm((L, D_FF, D), D_FF ** -0.5),
        'w_in': nrm((L, D, D_IN), D ** -0.5),
        'na_q_norm': 1.0 + nrm((L, HEAD_DIM), 0.1),
        'na_k_norm': 1.0 + nrm((L, HEAD_DIM), 0.1),
        'na_rpb': nrm((L, N_NA_HEADS, 2 * NA_ROWS - 1, 2 * NA_COLS - 1), 0.1),
        'gla_w_gate_f': nrm((L, GLA_GATE_RANK, N_GLA_HEADS * GLA_DK), GLA_GATE_RANK ** -0.5),
        'gla_b_gate_f': nrm((L, N_GLA_HEADS * GLA_DK), 0.1),
        'gla_w_gate_b': nrm((L, GLA_GATE_RANK, N_GLA_HEADS * GLA_DK), GLA_GATE_RANK ** -0.5),
        'gla_b_gate_b': nrm((L, N_GLA_HEADS * GLA_DK), 0.1),
        'gla_norm': 1.0 + nrm((L, GLA_DV), 0.1),
        'gqa_q_norm': 1.0 + nrm((L, HEAD_DIM), 0.1),
        'gqa_k_norm': 1.0 + nrm((L, HEAD_DIM), 0.1),
        'w_out': nrm((L, D_MIX, D), D_MIX ** -0.5),
        'ffn2_w1': nrm((L, D, D_FF), D ** -0.5),
        'ffn2_w3': nrm((L, D, D_FF), D ** -0.5),
        'ffn2_w2': nrm((L, D_FF, D), D_FF ** -0.5),
    }

def first_block(x, c, ctx, c_ctx, w_mod, b_mod, ffn1_w1, ffn1_w3, ffn1_w2, w_in,
              na_q_norm, na_k_norm, na_rpb, gla_w_gate_f, gla_b_gate_f, gla_w_gate_b, gla_b_gate_b,
              gla_norm, gqa_q_norm, gqa_k_norm, w_out, ffn2_w1, ffn2_w3, ffn2_w2):
    cos, sin = axial_rope(x.shape[1])
    z = ctx
    for l in range(DEPTH):
        last = l == DEPTH - 1
        mx = jnp.split((jax.nn.silu(c) @ w_mod[l] + b_mod[l])[:, None, :], N_MOD, axis=-1)
        mz = jnp.split(jax.nn.silu(c_ctx) @ w_mod[l] + b_mod[l], N_MOD, axis=-1)
        x = x + 0.5 * mx[2] * swiglu(modulate(rms_norm(x), mx[0], mx[1]), ffn1_w1[l], ffn1_w3[l], ffn1_w2[l])
        z = z + 0.5 * mz[2] * swiglu(modulate(rms_norm(z), mz[0], mz[1]), ffn1_w1[l], ffn1_w3[l], ffn1_w2[l])
        hx = modulate(rms_norm(x), mx[3], mx[4]) @ w_in[l]
        hz = modulate(rms_norm(z), mz[3], mz[4]) @ w_in[l]
        mix_x, mix_z = token_mixing(hx, hz, cos, sin, na_q_norm[l], na_k_norm[l], na_rpb[l],
                                    gla_w_gate_f[l], gla_b_gate_f[l], gla_w_gate_b[l], gla_b_gate_b[l],
                                    gla_norm[l], gqa_q_norm[l], gqa_k_norm[l], not last)
        x = x + mx[5] * (mix_x @ w_out[l])
        x = x + 0.5 * mx[8] * swiglu(modulate(rms_norm(x), mx[6], mx[7]), ffn2_w1[l], ffn2_w3[l], ffn2_w2[l])
        if not last:
            z = z + mz[5] * (mix_z @ w_out[l])
            z = z + 0.5 * mz[8] * swiglu(modulate(rms_norm(z), mz[6], mz[7]), ffn2_w1[l], ffn2_w3[l], ffn2_w2[l])
    return x


MEM_LEN = 256
ROPE_THETA_2 = 500000.0
MLA_HEADS = 8
MLA_NOPE = 64
MLA_ROPE = 32
MLA_V = 64
MLA_Q_LORA = 384
MLA_KV_LORA = 256
DIFF_HEADS = 8
DIFF_D = 64
DIFF_ROT = DIFF_D // 4
MEM_HEADS = 4
MEM_HD = 128
N_BRANCH = 3
D_FF_2 = 4 * D_MODEL
DEEPNORM_ALPHA = (2 * DEPTH) ** 0.25
DEEPNORM_BETA = (8 * DEPTH) ** -0.25
LN_EPS = 1e-5

MLA_OUT = MLA_HEADS * MLA_V
DIFF_QK = DIFF_HEADS * 2 * DIFF_D
DIFF_OUT = DIFF_HEADS * 2 * DIFF_D
MEM_OUT = MEM_HEADS * MEM_HD
BRANCH_W = MLA_OUT + DIFF_OUT + MEM_OUT
IN_SIZES = (MLA_Q_LORA, MLA_KV_LORA, MLA_ROPE, DIFF_QK, DIFF_QK, DIFF_OUT, MEM_OUT, N_BRANCH * D_MODEL)
N_IN = sum(IN_SIZES)


def _split_points():
    pts, acc = [], 0
    for s in IN_SIZES[:-1]:
        acc += s
        pts.append(acc)
    return pts

def _rms(x, g, eps=1e-6):
    xf = x.astype(jnp.float32)
    y = xf * lax.rsqrt(jnp.mean(xf * xf, axis=-1, keepdims=True) + eps)
    return (y * g.astype(jnp.float32)).astype(x.dtype)

def _layernorm(x, g, b):
    xf = x.astype(jnp.float32)
    mu = jnp.mean(xf, axis=-1, keepdims=True)
    var = jnp.mean(jnp.square(xf - mu), axis=-1, keepdims=True)
    y = (xf - mu) * lax.rsqrt(var + LN_EPS) * g.astype(jnp.float32) + b.astype(jnp.float32)
    return y.astype(x.dtype)

def _rope_tables(positions, rot_dim, dtype):
    inv = ROPE_THETA_2 ** (-jnp.arange(0, rot_dim, 2, dtype=jnp.float32) / rot_dim)
    ang = positions.astype(jnp.float32)[..., None] * inv
    return jnp.cos(ang).astype(dtype), jnp.sin(ang).astype(dtype)

def _apply_rope(x, cos, sin):
    half = cos.shape[-1]
    shape = cos.shape[:2] + (1,) * (x.ndim - 3) + (half,)
    c, s = cos.reshape(shape), sin.reshape(shape)
    x1, x2, rest = x[..., :half], x[..., half:2 * half], x[..., 2 * half:]
    return jnp.concatenate([x1 * c - x2 * s, x2 * c + x1 * s, rest], axis=-1)

def _sweep_query_blocks(fn, q):
    b, s = q.shape[0], q.shape[1]
    nb = s // Q_BLOCK
    qb = jnp.moveaxis(q.reshape((b, nb, Q_BLOCK) + q.shape[2:]), 1, 0)
    out = jnp.moveaxis(lax.map(fn, qb), 0, 1)
    return out.reshape((b, s) + out.shape[3:])

def _mla_branch(c_q, c_kv, k_pe, q_norm, kv_norm, w_uq, w_ukv, cos, sin):
    b, s, _ = c_q.shape
    q = (_rms(c_q, q_norm) @ w_uq).reshape(b, s, MLA_HEADS, MLA_NOPE + MLA_ROPE)
    q = jnp.concatenate([q[..., :MLA_NOPE], _apply_rope(q[..., MLA_NOPE:], cos, sin)], axis=-1)
    kv = (_rms(c_kv, kv_norm) @ w_ukv).reshape(b, s, MLA_HEADS, MLA_NOPE + MLA_V)
    k_nope, v = kv[..., :MLA_NOPE], kv[..., MLA_NOPE:]
    k_pe = _apply_rope(k_pe, cos, sin)
    scale = (MLA_NOPE + MLA_ROPE) ** -0.5

    def attend(qblk):
        qn, qp = qblk[..., :MLA_NOPE], qblk[..., MLA_NOPE:]
        sc = jnp.einsum('bqhn,bkhn->bhqk', qn, k_nope) + jnp.einsum('bqhr,bkr->bhqk', qp, k_pe)
        p = jax.nn.softmax(sc.astype(jnp.float32) * scale, axis=-1).astype(v.dtype)
        return jnp.einsum('bhqk,bkhv->bqhv', p, v)

    return _sweep_query_blocks(attend, q).reshape(b, s, MLA_OUT)

def _diff_branch(q, k, v, lam, subln, lambda_init, cos, sin):
    b, s, _ = q.shape
    q = _apply_rope(q.reshape(b, s, DIFF_HEADS, 2, DIFF_D), cos, sin)
    k = _apply_rope(k.reshape(b, s, DIFF_HEADS, 2, DIFF_D), cos, sin)
    v = v.reshape(b, s, DIFF_HEADS, 2 * DIFF_D)
    lf = lam.astype(jnp.float32)
    lambda_full = jnp.exp(jnp.sum(lf[0] * lf[1])) - jnp.exp(jnp.sum(lf[2] * lf[3])) + lambda_init
    scale = DIFF_D ** -0.5

    def attend(qblk):
        sc = jnp.einsum('bqhcd,bkhcd->bhcqk', qblk, k).astype(jnp.float32) * scale
        p = jax.nn.softmax(sc, axis=-1)
        w = (p[:, :, 0] - lambda_full * p[:, :, 1]).astype(v.dtype)
        return jnp.einsum('bhqk,bkhe->bqhe', w, v)

    o = _sweep_query_blocks(attend, q)
    o = _rms(o, subln, 1e-5) * (1.0 - lambda_init)
    return o.reshape(b, s, DIFF_OUT)

def _mem_branch(q, mem, w_kv):
    b, s, _ = q.shape
    q = q.reshape(b, s, MEM_HEADS, MEM_HD)
    kv = (mem @ w_kv).reshape(b, mem.shape[1], 2, MEM_HEADS, MEM_HD)
    k, v = kv[:, :, 0], kv[:, :, 1]
    sc = jnp.einsum('bqhd,bmhd->bhqm', q, k).astype(jnp.float32) * (MEM_HD ** -0.5)
    p = jax.nn.softmax(sc, axis=-1).astype(v.dtype)
    return jnp.einsum('bhqm,bmhd->bqhd', p, v).reshape(b, s, MEM_OUT)

def second_inputs(seed: int = 0) -> dict:
    key = jax.random.key(seed)
    ks = jax.random.split(key, 24)
    f32 = jnp.float32
    L, D = DEPTH, D_MODEL

    def w(k, shape, fan_in, gain=1.0):
        return jax.random.normal(k, shape, f32) * (gain * fan_in ** -0.5)

    def gain(k, shape):
        return 1.0 + 0.02 * jax.random.normal(k, shape, f32)

    def bias(k, shape):
        return 0.02 * jax.random.normal(k, shape, f32)

    x = jax.random.normal(ks[0], (BATCH, SEQ, D), f32)
    mem = jax.random.normal(ks[1], (BATCH, MEM_LEN, D), f32)
    offset = jax.random.randint(ks[2], (BATCH, 1), 0, SEQ, dtype=jnp.int32)
    positions = (jnp.arange(SEQ, dtype=jnp.int32)[None, :] + offset).astype(jnp.int32)
    return {
        'x': x,
        'mem': mem,
        'positions': positions,
        'w_in': w(ks[3], (L, D, N_IN), D),
        'b_gate': bias(ks[4], (L, N_BRANCH, D)),
        'mla_q_norm': gain(ks[5], (L, MLA_Q_LORA)),
        'mla_kv_norm': gain(ks[6], (L, MLA_KV_LORA)),
        'mla_w_uq': w(ks[7], (L, MLA_Q_LORA, MLA_HEADS * (MLA_NOPE + MLA_ROPE)), MLA_Q_LORA),
        'mla_w_ukv': w(ks[8], (L, MLA_KV_LORA, MLA_HEADS * (MLA_NOPE + MLA_V)), MLA_KV_LORA),
        'diff_lambda': 0.1 * jax.random.normal(ks[9], (L, 4, DIFF_D), f32),
        'diff_subln': gain(ks[10], (L, 2 * DIFF_D)),
        'mem_w_kv': w(ks[11], (L, D, 2 * MEM_OUT), D),
        'w_branch': w(ks[12], (L, BRANCH_W, D), BRANCH_W // N_BRANCH),
        'w_out': w(ks[13], (L, D, D), D, DEEPNORM_BETA),
        'ln1_g': gain(ks[14], (L, D)),
        'ln1_b': bias(ks[15], (L, D)),
        'mlp_w1': w(ks[16], (L, D, D_FF_2), D),
        'mlp_w2': w(ks[17], (L, D_FF_2, D), D_FF_2, DEEPNORM_BETA),
        'ln2_g': gain(ks[18], (L, D)),
        'ln2_b': bias(ks[19], (L, D)),
    }

def second_block(x, mem, positions, w_in, b_gate, mla_q_norm, mla_kv_norm, mla_w_uq, mla_w_ukv,
              diff_lambda, diff_subln, mem_w_kv, w_branch, w_out, ln1_g, ln1_b,
              mlp_w1, mlp_w2, ln2_g, ln2_b):
    b, s, d = x.shape
    cos_m, sin_m = _rope_tables(positions, MLA_ROPE, x.dtype)
    cos_d, sin_d = _rope_tables(positions, DIFF_ROT, x.dtype)
    splits = _split_points()
    for l in range(DEPTH):
        lambda_init = 0.8 - 0.6 * math.exp(-0.3 * l)
        h = x @ w_in[l]
        c_q, c_kv, k_pe, dq, dk, dv, mq, gate_pre = jnp.split(h, splits, axis=-1)
        o_mla = _mla_branch(c_q, c_kv, k_pe, mla_q_norm[l], mla_kv_norm[l], mla_w_uq[l], mla_w_ukv[l], cos_m, sin_m)
        o_diff = _diff_branch(dq, dk, dv, diff_lambda[l], diff_subln[l], lambda_init, cos_d, sin_d)
        o_mem = _mem_branch(mq, mem, mem_w_kv[l])
        g = jax.nn.sigmoid(gate_pre.reshape(b, s, N_BRANCH, d) + b_gate[l])
        wb = w_branch[l]
        merged = (g[:, :, 0] * (o_mla @ wb[:MLA_OUT])
                  + g[:, :, 1] * (o_diff @ wb[MLA_OUT:MLA_OUT + DIFF_OUT])
                  + g[:, :, 2] * (o_mem @ wb[MLA_OUT + DIFF_OUT:]))
        x = _layernorm(DEEPNORM_ALPHA * x + merged @ w_out[l], ln1_g[l], ln1_b[l])
        f = jnp.square(jax.nn.relu(x @ mlp_w1[l])) @ mlp_w2[l]
        x = _layernorm(DEEPNORM_ALPHA * x + f, ln2_g[l], ln2_b[l])
    return x


def setup_inputs(seed=0):
    out = dict(first_inputs(seed))
    for name, value in second_inputs(seed + 1).items():
        if name != "x":
            out[name + "_2"] = value
    return out


def reference(
    x, c, ctx, c_ctx, w_mod, b_mod, ffn1_w1, ffn1_w3, ffn1_w2, w_in, na_q_norm, na_k_norm,
    na_rpb, gla_w_gate_f, gla_b_gate_f, gla_w_gate_b, gla_b_gate_b, gla_norm, gqa_q_norm,
    gqa_k_norm, w_out, ffn2_w1, ffn2_w3, ffn2_w2, mem_2, positions_2, w_in_2, b_gate_2,
    mla_q_norm_2, mla_kv_norm_2, mla_w_uq_2, mla_w_ukv_2, diff_lambda_2, diff_subln_2,
    mem_w_kv_2, w_branch_2, w_out_2, ln1_g_2, ln1_b_2, mlp_w1_2, mlp_w2_2, ln2_g_2, ln2_b_2,
):
    x = first_block(
        x, c, ctx, c_ctx, w_mod, b_mod, ffn1_w1, ffn1_w3, ffn1_w2, w_in, na_q_norm, na_k_norm,
        na_rpb, gla_w_gate_f, gla_b_gate_f, gla_w_gate_b, gla_b_gate_b, gla_norm, gqa_q_norm,
        gqa_k_norm, w_out, ffn2_w1, ffn2_w3, ffn2_w2,
    )
    return second_block(
        x, mem_2, positions_2, w_in_2, b_gate_2, mla_q_norm_2, mla_kv_norm_2, mla_w_uq_2,
        mla_w_ukv_2, diff_lambda_2, diff_subln_2, mem_w_kv_2, w_branch_2, w_out_2, ln1_g_2,
        ln1_b_2, mlp_w1_2, mlp_w2_2, ln2_g_2, ln2_b_2,
    )


_drawn_inputs = setup_inputs


def setup_inputs(seed=0):
    import zlib

    import numpy as np

    out = dict(_drawn_inputs(seed))
    spreads = {}
    factors = {'na_q_norm': 8.0,
     'na_k_norm': 8.0,
     'na_rpb': 8.0,
     'gla_w_gate_f': 3.041,
     'gla_b_gate_f': 8.0,
     'gla_w_gate_b': 3.152,
     'gla_b_gate_b': 8.0,
     'gla_norm': 3.786,
     'gqa_q_norm': 8.0,
     'gqa_k_norm': 8.0,
     'b_gate_2': 8.0,
     'mla_q_norm_2': 8.0,
     'mla_kv_norm_2': 8.0,
     'diff_subln_2': 8.0}
    for name, (base, spread) in spreads.items():
        noise = np.random.default_rng([zlib.crc32(name.encode()), seed]).standard_normal(out[name].shape)
        drawn = base * np.exp(spread * noise) if base else spread * noise
        out[name] = jnp.asarray(drawn.astype(out[name].dtype))
    for name, factor in factors.items():
        out[name] = (out[name] * factor).astype(out[name].dtype)
    return out
```

```python
import math
from contextlib import ExitStack

import numpy as np

import concourse.bass as bass
from concourse import mybir

F32 = mybir.dt.float32
F32R = mybir.dt.float32r
I32 = mybir.dt.int32
ACT = mybir.ActivationFunctionType
ALU = mybir.AluOpType
AX = mybir.AxisListType.X

P = 128
D = 1024
KT = D // P
LAYERS = 2
TOK = 256
CHUNK = 2048
SLOTS = 3

D_FF = 2816
HD = 64
NA_HEADS = 4
GLA_HEADS = 4
GLA_DK = 32
GLA_LEVELS = 7
OFF = dict(fourier=0, na_q=256, na_k=512, na_v=768, gla_q=1024, gla_k=1152, gla_v=1280, gla_r=1536,
           gla_g=1792, gqa_q=1824, gqa_k=2080, gqa_v=2208)
D_IN = 2336
GRID_W = 64
NA_COLS = 16
RPB_ROWS, RPB_COLS = 15, 31
EPS = 1e-6

MLA_HEADS, MLA_NOPE, MLA_ROPE, MLA_V = 8, 64, 32, 64
MLA_QK = MLA_NOPE + MLA_ROPE
Q_LORA, KV_LORA = 384, 256
DIFF_HEADS, DIFF_D, DIFF_ROT = 8, 64, 16
MEM_HEADS, MEM_HD = 4, 128
OFF2 = dict(cq=0, ckv=384, kpe=640, dq=672, dk=1696, dv=2720, mq=3744, gate=4256)
N_IN = 7328
D_FF_2 = 4096
ALPHA = (2 * LAYERS) ** 0.25
LN_EPS = 1e-5
BRANCH_ROWS = (0, 512, 1536, 2048)


def shape_constants():
    t = np.arange(TOK)
    ang = 2 * np.pi * np.outer(t, t) / TOK
    dft_tok = np.concatenate([np.cos(ang), np.sin(ang)], 1) / math.sqrt(TOK)
    e = np.arange(HD)
    a2 = 2 * np.pi * np.outer(e, e) / HD
    eye2 = np.eye(2)
    dft_ch = np.stack([np.kron(eye2, np.cos(a2)), -np.kron(eye2, np.sin(a2))], 1) / math.sqrt(HD)

    c = np.arange(GRID_W)
    start = np.clip(c - NA_COLS // 2, 0, GRID_W - NA_COLS)
    seen = (c[None, :] >= start[:, None]) & (c[None, :] < start[:, None] + NA_COLS)
    na_mask = np.zeros((P, 2 * TOK))
    na_mask[:, :TOK] = np.where(np.tile(seen, (2, 4)), 0.0, -1e30)
    flip = np.zeros((P, P))
    for r in range(2):
        for i in range(GRID_W):
            flip[r * GRID_W + GRID_W - 1 - i, r * GRID_W + i] = math.sqrt(HD)

    i = np.arange(P)
    T_, I_ = i[:, None], i[None, :]
    dec = []
    for back in (False, True):
        for lv in range(GLA_LEVELS):
            s = 2 ** lv
            lo = (I_ // s) * s
            end = lo + s - 1
            late = (I_ // s) % 2 == 1
            if not back:
                m = np.where(late, (T_ >= lo) & (T_ <= I_), (T_ > I_) & (T_ <= end))
            else:
                m = np.where(late, (T_ >= lo) & (T_ < I_), (T_ >= I_) & (T_ <= end))
            dec.append(m)
    dec += [T_ <= I_, T_ > I_, T_ < I_, T_ >= I_, np.ones((P, P), bool)]
    dec = np.stack(dec, 1).astype(np.float64) / 16.0
    J_ = T_
    masks = []
    for back in (False, True):
        for lv in range(GLA_LEVELS):
            bj, bi = J_ >> lv, I_ >> lv
            masks.append((bj % 2 == 0) & (bi == bj + 1) if not back else (bj % 2 == 1) & (bi == bj - 1))
    masks = np.stack(masks, 1).astype(np.int32)

    row, col = (t // GRID_W).astype(np.float32), (t % GRID_W).astype(np.float32)
    inv = np.float32(10000.0) ** (-np.arange(16, dtype=np.float32) / np.float32(16))
    an = np.concatenate([row[:, None] * inv, col[:, None] * inv], -1)
    rope = np.stack([np.cos(an), np.sin(an)], 1).reshape(2, P, 2, 32).transpose(1, 0, 2, 3)
    inv_m = np.float32(500000.0) ** (-np.arange(0, MLA_ROPE, 2, dtype=np.float32) / np.float32(MLA_ROPE))
    inv_d = np.float32(500000.0) ** (-np.arange(0, DIFF_ROT, 2, dtype=np.float32) / np.float32(DIFF_ROT))
    inv2 = np.tile(np.concatenate([inv_m, inv_d])[None], (P, 1))
    f = lambda a: np.ascontiguousarray(a, dtype=np.float32)
    return dict(k_dft_tok=f(dft_tok.reshape(2, P, 2 * TOK).transpose(1, 0, 2)), k_dft_ch=f(dft_ch),
                k_na_mask=f(na_mask), k_flip=f(flip), k_decay=f(dec), k_levels=np.ascontiguousarray(masks),
                k_rope=f(rope), k_inv=f(inv2), k_eye=f(np.eye(P)))


TAB = dict(le=14, gt=15, lt=16, ge=17, ones=18)


class Signal:

    def __init__(self, sem, unit=1):
        self.sem, self.unit, self.base = sem, unit, 0

    def at(self, n):
        return (self.base + n) * self.unit

    def passed(self, n):
        self.base += n


def loop(eng, first, last, body):
    if last - first == 1:
        body(first)
    elif last > first:
        with eng.Fori(first, last) as i:
            body(i)


def split_product(pe, out, a, b, first, last):
    pe.matmul(out, a[0], b[0], start=first, stop=False)
    pe.matmul(out, a[0], b[1], start=False, stop=False)
    return pe.matmul(out, a[1], b[0], start=False, stop=last)


class Core:

    def __init__(self, nc, ctx):
        self.nc, self.ctx = nc, ctx
        self.serial = 0
        self.ps = ctx.enter_context(nc.psum_tensor("psum", [P, 8, 512], F32))
        self.raw = ctx.enter_context(nc.sbuf_tensor("w_raw", [P, SLOTS, CHUNK], F32))
        self.w_hi = ctx.enter_context(nc.sbuf_tensor("w_hi", [P, SLOTS, CHUNK], F32R))
        self.w_lo = ctx.enter_context(nc.sbuf_tensor("w_lo", [P, SLOTS, CHUNK], F32R))
        self.loaded = [self.counter(f"w_loaded{s}", 16) for s in range(SLOTS)]
        self.hi_done = [self.counter(f"w_hi_done{s}") for s in range(SLOTS)]
        self.split = [self.counter(f"w_split{s}") for s in range(SLOTS)]
        self.minus_half = None
        self.heads = []
        self.next_heads = 0
        self.counters = {}

    def counter(self, name, unit=1):
        return Signal(self.ctx.enter_context(self.nc.semaphore(name)), unit)

    def sig(self, name, unit=1):
        if name not in self.counters:
            self.counters[name] = self.counter(name, unit)
        return self.counters[name]

    def sb(self, stack, name, shape, dt=F32):
        self.serial += 1
        return stack.enter_context(self.nc.sbuf_tensor(f"{name}_{self.serial}", shape, dt))

    def load(self, sp, slot, used, src):
        if not isinstance(used, int) or self.split[slot].base + used > 0:
            sp.wait_ge(self.split[slot].sem, self.split[slot].at(used))
        a, b = src.shape[1], src.shape[2]
        dst = self.raw[:, slot, 0:a * b].rearrange("p (a b) -> p a b", b=b)
        sp.dma_start(dst, src).then_inc(self.loaded[slot].sem, 16)

    def load_heads(self, sp, used):
        self.next_heads += 1
        if self.next_heads <= len(self.heads):
            for slot, src in self.heads[self.next_heads - 1]:
                self.load(sp, slot, used[slot], src)

    def hi(self, act, slot, u, n=CHUNK):
        act.wait_ge(self.loaded[slot].sem, self.loaded[slot].at(u + 1))
        act.activation(self.w_hi[:, slot, 0:n], self.raw[:, slot, 0:n], ACT.Copy).then_inc(self.hi_done[slot].sem, 1)

    def lo(self, dve, slot, u, n=CHUNK):
        dve.wait_ge(self.hi_done[slot].sem, self.hi_done[slot].at(u + 1))
        dve.tensor_tensor(self.w_lo[:, slot, 0:n], self.raw[:, slot, 0:n], self.w_hi[:, slot, 0:n].bitcast(F32),
                          ALU.subtract).then_inc(self.split[slot].sem, 1)

    def ready(self, pe, slot, u):
        pe.wait_ge(self.split[slot].sem, self.split[slot].at(u + 1))

    def w(self, slot, nk, cw):
        return [t[:, slot, 0:nk * cw].rearrange("p (k c) -> p k c", c=cw) for t in (self.w_hi, self.w_lo)]

    def weights_passed(self, used):
        for s in range(SLOTS):
            self.loaded[s].passed(used[s])
            self.hi_done[s].passed(used[s])
            self.split[s].passed(used[s])


def block(c):
    return c.nc.Block(no_gpsimd_drain=True)


def chunk_of(w2d, r0, nk, c0, cw):
    cols = w2d[r0:r0 + nk * P, c0:c0 + cw] if isinstance(c0, int) else w2d[r0:r0 + nk * P, bass.ds(c0, cw)]
    return cols.rearrange("(k p) n -> p k n", p=P)


def rows_of(w2d, i, nk):
    rows = w2d[i * nk * P:(i + 1) * nk * P, :] if isinstance(i, int) else w2d[bass.ds(i * (nk * P), nk * P), :]
    return rows.rearrange("(k p) n -> p k n", p=P)


class Chain:

    def __init__(self, eng, count):
        self.eng, self.count, self.n = eng, count, 0

    def __call__(self, ins):
        ins.then_inc(self.count.sem, 1)
        self.n += 1
        self.eng.wait_ge(self.count.sem, self.count.at(self.n))

    def close(self):
        self.count.passed(self.n)


def on_vector(c, steps):
    with block(c) as b:
        @b.vector
        def _(dve):
            link = Chain(dve, c.sig("dve_step"))
            steps(dve, link)
            link.close()


def on_scalar(c, steps):
    with block(c) as b:
        @b.scalar
        def _(act):
            link = Chain(act, c.sig("act_step"))
            steps(act, link)
            link.close()


def inverse_root(c, ss, scale, eps):
    squared, rooted = c.sig("mean_ready"), c.sig("root_ready")
    with block(c) as b:
        @b.vector
        def _(dve):
            dve.tensor_scalar(ss, ss, scale, eps, ALU.mult, ALU.add).then_inc(squared.sem, 1)
            dve.wait_ge(rooted.sem, rooted.at(1))

        @b.gpsimd
        def _(pool):
            pool.wait_ge(squared.sem, squared.at(1))
            pool.tensor_tensor(ss, ss, c.minus_half[:, 0:ss.shape[1]], ALU.pow).then_inc(rooted.sem, 1)
    squared.passed(1)
    rooted.passed(1)


def turn(c, src, dst, nk, ntt, w, eye, scale=None, split=True, cols=None, side=1.0):
    nt = ntt * P
    banks = 4
    turned, moved, highs = c.sig("turned"), c.sig("turn_moved"), c.sig("turn_hi")
    lows = c.sig("turn_lo")
    with ExitStack() as st:
        tmp = c.sb(st, "turn_tmp", [P, 2, nt]) if split else None
        with block(c) as b:
            @b.tensor
            def _(pe):
                for k in range(nk):
                    if k >= banks:
                        pe.wait_ge(moved.sem, moved.at(k - banks + 1))
                    for t in range(ntt):
                        last = pe.transpose(c.ps[0:w, k % banks, t * P:(t + 1) * P], src(t, k), eye)
                    last.then_inc(turned.sem, 1)

            if not split:
                @b.scalar
                def _(act):
                    for k in range(nk):
                        act.wait_ge(turned.sem, turned.at(k + 1))
                        act.activation(dst[0:w, k, :], c.ps[0:w, k % banks, 0:nt], ACT.Copy,
                                       scale=side).then_inc(moved.sem, 1)
            else:
                @b.vector
                def _(dve):
                    def low(k):
                        dve.wait_ge(highs.sem, highs.at(k + 1))
                        dve.tensor_tensor(dst[1][0:w, k, :], tmp[0:w, k % 2, :], dst[0][0:w, k, :].bitcast(F32),
                                          ALU.subtract).then_inc(lows.sem, 1)

                    for k in range(nk):
                        dve.wait_ge(turned.sem, turned.at(k + 1))
                        if k >= 2:
                            dve.wait_ge(lows.sem, lows.at(k - 1))
                        parts = cols(k) if cols else [(0, nt, None, None)]
                        for t0, t1, sc, sh in parts:
                            o, s = tmp[0:w, k % 2, t0:t1], c.ps[0:w, k % banks, t0:t1]
                            if sc is None:
                                last = dve.tensor_copy(o, s)
                            elif sh is None:
                                last = dve.tensor_scalar(o, s, sc, None, ALU.mult)
                            else:
                                last = dve.tensor_scalar(o, s, sc, sh, ALU.mult, ALU.add)
                        last.then_inc(moved.sem, 1)
                        if k >= 1:
                            low(k - 1)
                    low(nk - 1)

                @b.scalar
                def _(act):
                    for k in range(nk):
                        act.wait_ge(moved.sem, moved.at(k + 1))
                        act.activation(dst[0][0:w, k, :], tmp[0:w, k % 2, :], ACT.Copy).then_inc(highs.sem, 1)
    turned.passed(nk)
    moved.passed(nk)
    if split:
        highs.passed(nk)
        lows.passed(nk)


def rms_rows(c, x, ntt, xs):
    with ExitStack() as st:
        ss = c.sb(st, "ss", [P, ntt])
        on_scalar(c, lambda act, link: [link(act.activation(xs[:, t, :], x[:, t, :], ACT.Square,
                                                            accum_out=ss[:, t:t + 1])) for t in range(ntt)])
        inverse_root(c, ss[:, :], 1.0 / D, EPS)
        with block(c) as b:
            @b.scalar
            def _(act):
                for t in range(0, ntt, 2):
                    act.activation(xs[:, t, :], x[:, t, :], ACT.Copy, scale=ss[:, t:t + 1])

            @b.vector
            def _(dve):
                for t in range(1, ntt, 2):
                    dve.tensor_scalar(xs[:, t, :], x[:, t, :], ss[:, t:t + 1], None, ALU.mult)


def chunks_of(w2d, r0, nk, col0, ncols):
    cw = min(CHUNK // nk, 512)
    out, at = [], 0
    while at < ncols:
        out.append((w2d, r0, nk, col0 + at, min(cw, ncols - at)))
        at += cw
    return out


def project_heads(chunks):
    return [(n, chunk_of(*chunks[n])) for n in range(min(SLOTS, len(chunks)))]


def project(c, chunks, lhs, ntt, evac, on_act=True):
    n_all = len(chunks)
    nk, cw = chunks[0][2], chunks[0][4]
    full = n_all if chunks[-1][4] == cw else n_all - 1
    per_bank = 512 // cw
    banks = (ntt + per_bank - 1) // per_bank
    out_ready, out_read = c.sig("proj_ready"), c.sig("proj_read")
    used = [len(range(s, n_all, SLOTS)) for s in range(SLOTS)]

    def view(slot, width):
        v = c.ps[:, 2 * slot:2 * slot + banks, :].rearrange("p b (t n) -> p (b t) n", n=cw)
        return v[:, 0:ntt, 0:width]

    def width(n):
        return chunks[n][4] if isinstance(n, int) else cw

    turns = max(0, (full - 1) // SLOTS) if full == n_all else max(0, (full - 1) // SLOTS)

    with block(c) as b:
        @b.sync
        def _(sp):
            whole = max(0, full // SLOTS)

            def three(i):
                for j in range(SLOTS):
                    w2d, r0, k_, c0, _ = chunks[0]
                    c.load(sp, j, i, chunk_of(w2d, r0, k_, c0 + (i * SLOTS + j) * cw, cw))

            regular = all(ch[:3] == chunks[0][:3] for ch in chunks) if n_all > 2 * SLOTS else False
            if regular:
                loop(sp, 1, whole, three)
                rest = range(max(1, whole) * SLOTS, n_all)
            else:
                rest = range(SLOTS, n_all)
            for n in rest:
                c.load(sp, n % SLOTS, n // SLOTS, chunk_of(*chunks[n]))
            c.load_heads(sp, used)

        @b.scalar
        def _(act):
            def high(n, i, j, wd):
                if not isinstance(n, int) or n >= SLOTS:
                    act.wait_ge(out_ready.sem, out_ready.at(n - SLOTS + 1))
                c.hi(act, j, i, nk * wd)

            def one(n, i, j, ahead):
                if ahead:
                    jn = (j + 1) % SLOTS
                    high(n + 1, i + (j + 1) // SLOTS, jn, width(n + 1))
                if on_act:
                    act.wait_ge(out_ready.sem, out_ready.at(n + 1))
                    evac(act, n, view(j, width(n))).then_inc(out_read.sem, 1)

            high(0, 0, 0, width(0))
            for n in range(min(SLOTS, n_all)):
                one(n, 0, n, n + 1 < n_all)
            loop(act, 1, turns, lambda i: [one(i * SLOTS + j, i, j, True) for j in range(SLOTS)])
            for n in range(max(1, turns) * SLOTS, n_all):
                one(n, n // SLOTS, n % SLOTS, n + 1 < n_all)

        @b.vector
        def _(dve):
            def one(n, i, j, ahead):
                if ahead:
                    c.lo(dve, (j + 1) % SLOTS, i + (j + 1) // SLOTS, nk * width(n + 1))
                if not on_act:
                    dve.wait_ge(out_ready.sem, out_ready.at(n + 1))
                    evac(dve, n, view(j, width(n))).then_inc(out_read.sem, 1)

            c.lo(dve, 0, 0, nk * width(0))
            for n in range(min(SLOTS, n_all)):
                one(n, 0, n, n + 1 < n_all)
            loop(dve, 1, turns, lambda i: [one(i * SLOTS + j, i, j, True) for j in range(SLOTS)])
            for n in range(max(1, turns) * SLOTS, n_all):
                one(n, n // SLOTS, n % SLOTS, n + 1 < n_all)

        @b.tensor
        def _(pe):
            def one(n, i, j):
                wd = width(n)
                c.ready(pe, j, i)
                if not isinstance(n, int) or n >= SLOTS:
                    pe.wait_ge(out_read.sem, out_read.at(n - SLOTS + 1))
                w = c.w(j, nk, wd)
                v = view(j, wd)
                for t in range(ntt):
                    for k in range(nk):
                        last = split_product(pe, v[:, t, :], [a(n, k)[:, t * P:(t + 1) * P] for a in lhs],
                                             [x[:, k, :] for x in w], k == 0, k == nk - 1)
                last.then_inc(out_ready.sem, 1)

            for n in range(min(SLOTS, n_all)):
                one(n, 0, n)
            loop(pe, 1, turns, lambda i: [one(i * SLOTS + j, i, j) for j in range(SLOTS)])
            for n in range(max(1, turns) * SLOTS, n_all):
                one(n, n // SLOTS, n % SLOTS)
    out_ready.passed(n_all)
    out_read.passed(n_all)
    c.weights_passed(used)


def lhs_of(pair):
    return [lambda n, k, a=a: a[:, k, :] for a in pair]


def into(dst, cw):
    def evac(eng, n, v):
        wd = v.shape[2]
        cols = slice(n * cw, n * cw + wd) if isinstance(n, int) else bass.ds(n * cw, cw)
        return eng.activation(dst[:, :, cols], v, ACT.Copy)
    return evac


def ffn_heads(w1, w3, w2):
    return [(0, chunk_of(w1, 0, KT, 0, 2 * P)), (2, chunk_of(w3, 0, KT, 0, 2 * P)), (1, rows_of(w2, 0, 2))]


def swiglu(c, w1, w3, w2, xt, ntt, y):
    nt = ntt * P
    n = D_FF // (2 * P)
    h1_ready, h3_ready, silu_ready = c.sig("h1_ready"), c.sig("h3_ready"), c.sig("silu_ready")
    g_ready, ghi_ready, glo_ready = c.sig("g_ready"), c.sig("ghi_ready"), c.sig("glo_ready")
    y_ready, y_added, y_clear = c.sig("y_ready"), c.sig("y_added"), c.sig("y_clear")
    ny = 2 * ntt
    with ExitStack() as st:
        s1 = c.sb(st, "silu", [P, 2, nt])
        g = c.sb(st, "gated", [P, 2, nt])
        gh = c.sb(st, "gated_hi", [P, 2, nt], F32R)
        gl = c.sb(st, "gated_lo", [P, 2, nt], F32R)
        with block(c) as b:
            @b.gpsimd
            def _(pool):
                pool.memset(y[:, 0:ntt, :], 0.0).then_inc(y_clear.sem, 1)

            @b.sync
            def _(sp):
                up = lambda w, i: chunk_of(w, 0, KT, i * (2 * P), 2 * P)
                c.load(sp, 0, 1, up(w1, 1))
                c.load(sp, 2, 1, up(w3, 1))
                c.load(sp, 0, 2, up(w1, 2))

                def body(i):
                    c.load(sp, 1, i, rows_of(w2, i, 2))
                    c.load(sp, 2, i + 1, up(w3, i + 1))
                    c.load(sp, 0, i + 2, up(w1, i + 2))
                loop(sp, 1, n - 2, body)
                c.load(sp, 1, n - 2, rows_of(w2, n - 2, 2))
                c.load(sp, 2, n - 1, up(w3, n - 1))
                c.load(sp, 1, n - 1, rows_of(w2, n - 1, 2))
                c.load_heads(sp, [n, n, n])

            @b.tensor
            def _(pe):
                def up(i, slot, bank, ready, held, per):
                    c.ready(pe, slot, i)
                    w = c.w(slot, KT, 2 * P)
                    for f in range(2):
                        if not isinstance(i, int) or i > 0:
                            pe.wait_ge(held.sem, held.at((i - 1) * 2 + f + 1))
                        for k in range(KT):
                            last = split_product(pe, c.ps[:, bank + f, 0:nt], [x[:, k, f * P:(f + 1) * P] for x in w],
                                                 [x[:, k, :] for x in xt], k == 0, k == KT - 1)
                        last.then_inc(ready.sem, 1)

                def down(i):
                    c.ready(pe, 1, i)
                    w = c.w(1, 2, D)
                    pe.wait_ge(glo_ready.sem, glo_ready.at((i + 1) * 2))
                    for m in range(ny):
                        t, half = m // 2, m % 2
                        if not (isinstance(i, int) and i * ny + m < 4):
                            pe.wait_ge(y_added.sem, y_added.at(i * ny + (m - 3)))
                        for f in range(2):
                            last = split_product(pe, c.ps[:, 4 + m % 4, :], [x[:, f, t * P:(t + 1) * P] for x in (gh, gl)],
                                                 [x[:, f, half * 512:(half + 1) * 512] for x in w], f == 0, f == 1)
                        last.then_inc(y_ready.sem, 1)

                def body(i):
                    up(i, 0, 0, h1_ready, silu_ready, 2)
                    down(i - 1)
                    up(i, 2, 2, h3_ready, g_ready, 2)
                up(0, 0, 0, h1_ready, silu_ready, 2)
                up(0, 2, 2, h3_ready, g_ready, 2)
                body(1)
                loop(pe, 2, n, body)
                down(n - 1)

            @b.scalar
            def _(act):
                def gate_hi(i):
                    if not isinstance(i, int) or i > 0:
                        act.wait_ge(y_ready.sem, y_ready.at(i * ny))
                    for f in range(2):
                        act.wait_ge(g_ready.sem, g_ready.at(i * 2 + f + 1))
                        act.activation(gh[:, f, :], g[:, f, :], ACT.Copy).then_inc(ghi_ready.sem, 1)

                def silu(i):
                    for f in range(2):
                        act.wait_ge(h1_ready.sem, h1_ready.at(i * 2 + f + 1))
                        if not isinstance(i, int) or i > 0:
                            act.wait_ge(g_ready.sem, g_ready.at((i - 1) * 2 + f + 1))
                        act.activation(s1[:, f, :], c.ps[:, f, 0:nt], ACT.Silu).then_inc(silu_ready.sem, 1)

                def w3_hi(i):
                    if not isinstance(i, int) or i > 0:
                        act.wait_ge(h3_ready.sem, h3_ready.at(i * 2))
                    c.hi(act, 2, i)

                def w1_hi(i):
                    if not isinstance(i, int) or i > 0:
                        act.wait_ge(h1_ready.sem, h1_ready.at(i * 2))
                    c.hi(act, 0, i)

                def w2_hi(i):
                    c.hi(act, 1, i)

                def body(i):
                    gate_hi(i - 1)
                    w2_hi(i - 1)
                    w3_hi(i)
                    silu(i)
                    w1_hi(i + 1)
                w1_hi(0)
                w3_hi(0)
                silu(0)
                w1_hi(1)
                loop(act, 1, n - 1, body)
                gate_hi(n - 2)
                w2_hi(n - 2)
                w3_hi(n - 1)
                silu(n - 1)
                gate_hi(n - 1)
                w2_hi(n - 1)

            @b.vector
            def _(dve):
                def gate(i):
                    for f in range(2):
                        dve.wait_ge(h3_ready.sem, h3_ready.at(i * 2 + f + 1))
                        dve.wait_ge(silu_ready.sem, silu_ready.at(i * 2 + f + 1))
                        if not isinstance(i, int) or i > 0:
                            dve.wait_ge(glo_ready.sem, glo_ready.at((i - 1) * 2 + f + 1))
                        dve.tensor_tensor(g[:, f, :], s1[:, f, :], c.ps[:, 2 + f, 0:nt], ALU.mult).then_inc(g_ready.sem, 1)
                    for f in range(2):
                        dve.wait_ge(ghi_ready.sem, ghi_ready.at(i * 2 + f + 1))
                        dve.tensor_tensor(gl[:, f, :], g[:, f, :], gh[:, f, :].bitcast(F32),
                                          ALU.subtract).then_inc(glo_ready.sem, 1)

                def add(i):
                    for m in range(ny):
                        t, half = m // 2, m % 2
                        dve.wait_ge(y_ready.sem, y_ready.at(i * ny + m + 1))
                        if not isinstance(i, int) or i > 0:
                            dve.wait_ge(y_added.sem, y_added.at((i - 1) * ny + m + 1))
                        yv = y[:, t, half * 512:(half + 1) * 512]
                        dve.tensor_tensor(yv, c.ps[:, 4 + m % 4, :], yv, ALU.add).then_inc(y_added.sem, 1)

                def body(i):
                    gate(i - 1)
                    c.lo(dve, 1, i - 1)
                    c.lo(dve, 2, i)
                    c.lo(dve, 0, i + 1)
                    add(i - 1)
                c.lo(dve, 0, 0)
                c.lo(dve, 2, 0)
                c.lo(dve, 0, 1)
                dve.wait_ge(y_clear.sem, y_clear.at(1))
                gate(0)
                c.lo(dve, 1, 0)
                c.lo(dve, 2, 1)
                c.lo(dve, 0, 2)
                add(0)
                loop(dve, 2, n - 1, body)
                gate(n - 2)
                c.lo(dve, 1, n - 2)
                c.lo(dve, 2, n - 1)
                add(n - 2)
                gate(n - 1)
                c.lo(dve, 1, n - 1)
                add(n - 1)
    for s in (h1_ready, h3_ready, silu_ready, g_ready, ghi_ready, glo_ready):
        s.passed(2 * n)
    y_ready.passed(ny * n)
    y_added.passed(ny * n)
    y_clear.passed(1)
    c.weights_passed([n, n, n])


def mlp_heads(w1, w2):
    return [(0, chunk_of(w1, 0, KT, 0, 2 * P)), (2, chunk_of(w1, 0, KT, 2 * P, 2 * P)), (1, rows_of(w2, 0, 2))]


def relu_squared_mlp(c, w1, w2, xt, y):
    ntt, nt = 2, 2 * P
    n = D_FF_2 // (2 * P)
    h_ready, relu_ready, g_ready = c.sig("h1_ready"), c.sig("silu_ready"), c.sig("g_ready")
    ghi_ready, glo_ready = c.sig("ghi_ready"), c.sig("glo_ready")
    y_ready, y_added, y_clear = c.sig("y_ready"), c.sig("y_added"), c.sig("y_clear")
    ny = 2 * ntt
    turns = n // 2
    with ExitStack() as st:
        s1 = c.sb(st, "relu", [P, 2, 2, nt])
        g = c.sb(st, "squared", [P, 2, 2, nt])
        gh = c.sb(st, "squared_hi", [P, 2, 2, nt], F32R)
        gl = c.sb(st, "squared_lo", [P, 2, 2, nt], F32R)
        slot_of = (0, 2)
        started = lambda i: not isinstance(i, int) or i > 0
        with block(c) as b:
            @b.gpsimd
            def _(pool):
                pool.memset(y[:, 0:ntt, :], 0.0).then_inc(y_clear.sem, 1)

            @b.sync
            def _(sp):
                up = lambda i, a: chunk_of(w1, 0, KT, i * (4 * P) + a * 2 * P, 2 * P)

                def body(i):
                    c.load(sp, 0, i, up(i, 0))
                    c.load(sp, 1, 2 * i - 1, rows_of(w2, 2 * i - 1, 2))
                    c.load(sp, 2, i, up(i, 1))
                    c.load(sp, 1, 2 * i, rows_of(w2, 2 * i, 2))
                loop(sp, 1, turns, body)
                c.load(sp, 1, n - 1, rows_of(w2, n - 1, 2))
                c.load_heads(sp, [turns, n, turns])

            @b.tensor
            def _(pe):
                def up(i, a):
                    c.ready(pe, slot_of[a], i)
                    w = c.w(slot_of[a], KT, 2 * P)
                    if started(i):
                        pe.wait_ge(relu_ready.sem, relu_ready.at((i - 1) * 2 + a + 1))
                    for f in range(2):
                        for k in range(KT):
                            last = split_product(pe, c.ps[:, a, f * nt:(f + 1) * nt], [x[:, k, f * P:(f + 1) * P] for x in w],
                                                 [x[:, k, :] for x in xt], k == 0, k == KT - 1)
                    last.then_inc(h_ready.sem, 1)

                def down(i, a):
                    q = i * 2 + a
                    c.ready(pe, 1, q)
                    pe.wait_ge(glo_ready.sem, glo_ready.at(q + 1))
                    w = c.w(1, 2, D)
                    for m in range(ny):
                        t, half = m // 2, m % 2
                        if not (isinstance(q, int) and q == 0):
                            pe.wait_ge(y_added.sem, y_added.at((q - 1) * ny + m + 1))
                        for f in range(2):
                            last = split_product(pe, c.ps[:, 4 + m, :], [x[:, a, f, t * P:(t + 1) * P] for x in (gh, gl)],
                                                 [x[:, f, half * 512:(half + 1) * 512] for x in w], f == 0, f == 1)
                        last.then_inc(y_ready.sem, 1)

                def body(i):
                    up(i, 0)
                    down(i - 1, 1)
                    up(i, 1)
                    down(i, 0)
                up(0, 0)
                up(0, 1)
                down(0, 0)
                loop(pe, 1, turns, body)
                down(turns - 1, 1)

            @b.scalar
            def _(act):
                def w1_hi(i, a):
                    if started(i):
                        act.wait_ge(h_ready.sem, h_ready.at((i - 1) * 2 + a + 1))
                    c.hi(act, slot_of[a], i)

                def w2_hi(i, a):
                    q = i * 2 + a
                    if started(q):
                        act.wait_ge(y_ready.sem, y_ready.at(q * ny))
                    c.hi(act, 1, q)

                def relu(i, a):
                    act.wait_ge(h_ready.sem, h_ready.at(i * 2 + a + 1))
                    if started(i):
                        act.wait_ge(g_ready.sem, g_ready.at((i - 1) * 2 + a + 1))
                    act.activation(s1[:, a, :, :].rearrange("p f n -> p (f n)"), c.ps[:, a, :], ACT.Relu).then_inc(relu_ready.sem, 1)

                def g_hi(i, a):
                    q = i * 2 + a
                    act.wait_ge(g_ready.sem, g_ready.at(q + 1))
                    if not isinstance(q, int) or q >= 2:
                        act.wait_ge(y_ready.sem, y_ready.at((q - 1) * ny))
                    act.activation(gh[:, a, :, :], g[:, a, :, :], ACT.Copy).then_inc(ghi_ready.sem, 1)

                def body(i):
                    w1_hi(i, 0)
                    w2_hi(i - 1, 1)
                    relu(i, 0)
                    g_hi(i, 0)
                    w1_hi(i, 1)
                    w2_hi(i, 0)
                    relu(i, 1)
                    g_hi(i, 1)
                w1_hi(0, 0)
                w1_hi(0, 1)
                w2_hi(0, 0)
                relu(0, 0)
                g_hi(0, 0)
                relu(0, 1)
                g_hi(0, 1)
                loop(act, 1, turns, body)
                w2_hi(turns - 1, 1)

            @b.vector
            def _(dve):
                def gate(i, a):
                    q = i * 2 + a
                    dve.wait_ge(relu_ready.sem, relu_ready.at(q + 1))
                    if started(i):
                        dve.wait_ge(glo_ready.sem, glo_ready.at(q - 1))
                    dve.tensor_tensor(g[:, a, :, :], s1[:, a, :, :], s1[:, a, :, :], ALU.mult).then_inc(g_ready.sem, 1)
                    dve.wait_ge(ghi_ready.sem, ghi_ready.at(q + 1))
                    dve.tensor_tensor(gl[:, a, :, :], g[:, a, :, :], gh[:, a, :, :].bitcast(F32),
                                      ALU.subtract).then_inc(glo_ready.sem, 1)

                def add(i, a):
                    q = i * 2 + a
                    for m in range(ny):
                        t, half = m // 2, m % 2
                        dve.wait_ge(y_ready.sem, y_ready.at(q * ny + m + 1))
                        if started(q):
                            dve.wait_ge(y_added.sem, y_added.at((q - 1) * ny + m + 1))
                        yv = y[:, t, half * 512:(half + 1) * 512]
                        dve.tensor_tensor(yv, c.ps[:, 4 + m, :], yv, ALU.add).then_inc(y_added.sem, 1)

                def body(i):
                    c.lo(dve, 0, i)
                    c.lo(dve, 1, i * 2 - 1)
                    gate(i, 0)
                    add(i - 1, 1)
                    c.lo(dve, 2, i)
                    c.lo(dve, 1, i * 2)
                    gate(i, 1)
                    add(i, 0)
                c.lo(dve, 0, 0)
                c.lo(dve, 2, 0)
                c.lo(dve, 1, 0)
                dve.wait_ge(y_clear.sem, y_clear.at(1))
                gate(0, 0)
                gate(0, 1)
                add(0, 0)
                loop(dve, 1, turns, body)
                c.lo(dve, 1, n - 1)
                add(turns - 1, 1)
    for s in (h_ready, relu_ready, g_ready, ghi_ready, glo_ready):
        s.passed(n)
    y_ready.passed(ny * n)
    y_added.passed(ny * n)
    y_clear.passed(1)
    c.weights_passed([turns, n, turns])


def modulation_heads(w):
    return [(j, chunk_of(w, 0, KT, j * 2 * P, 2 * P)) for j in range(SLOTS)]


def modulation(c, w, silu4, bias_t, mod, comb):
    n = w.shape[1] // (2 * P)
    turns = n // SLOTS
    row_ready, row_moved = c.sig("mod_row_ready"), c.sig("mod_row_moved")
    col_ready, col_moved = c.sig("mod_col_ready"), c.sig("mod_col_moved")
    with ExitStack() as st:
        rows = c.sb(st, "mod_rows", [4, SLOTS, 2 * P])
        with block(c) as b:
            @b.sync
            def _(sp):
                loop(sp, 1, turns, lambda i: [c.load(sp, j, i, chunk_of(w, 0, KT, i * (SLOTS * 2 * P) + j * 2 * P, 2 * P))
                                              for j in range(SLOTS)])
                c.load_heads(sp, [turns] * SLOTS)

            @b.scalar
            def _(act):
                def body(i, first=False):
                    for j in range(SLOTS):
                        if not first:
                            act.wait_ge(row_ready.sem, row_ready.at(i * SLOTS + j - 2))
                        c.hi(act, j, i)
                body(0, True)
                loop(act, 1, turns, body)

            @b.vector
            def _(dve):
                def body(i):
                    for j in range(SLOTS):
                        c.lo(dve, j, i)
                        dve.wait_ge(row_ready.sem, row_ready.at(i * SLOTS + j + 1))
                        if not isinstance(i, int):
                            dve.wait_ge(col_ready.sem, col_ready.at(i * SLOTS + j - 2))
                        dve.tensor_copy(rows[:, j, :], c.ps[0:4, j, 0:2 * P]).then_inc(row_moved.sem, 1)
                        dve.wait_ge(col_ready.sem, col_ready.at(i * SLOTS + j + 1))
                        q = i * SLOTS + j
                        o = mod[:, 2 * q:2 * q + 2, :] if isinstance(i, int) else mod[:, bass.ds(q * 2, 2), :]
                        bt = bias_t[:, 2 * q:2 * q + 2] if isinstance(i, int) else bias_t[:, bass.ds(q * 2, 2)]
                        dve.tensor_tensor(o, c.ps[:, 3 + j, 0:4].rearrange("p (f v) -> p f v", v=2),
                                          bt.unsqueeze(2).to_broadcast([P, 2, 2]), ALU.add).then_inc(col_moved.sem, 1)
                body(0)
                loop(dve, 1, turns, body)

            @b.tensor
            def _(pe):
                def body(i):
                    for j in range(SLOTS):
                        c.ready(pe, j, i)
                        if not isinstance(i, int):
                            pe.wait_ge(row_moved.sem, row_moved.at(i * SLOTS + j - 2))
                        wv = c.w(j, KT, 2 * P)
                        for h in range(2):
                            for k in range(KT):
                                last = pe.matmul(c.ps[0:4, j, 0:2 * P], silu4[:, k, :], wv[h][:, k, :],
                                                 start=(h + k == 0), stop=(h == 1 and k == KT - 1))
                        last.then_inc(row_ready.sem, 1)
                        pe.wait_ge(row_moved.sem, row_moved.at(i * SLOTS + j + 1))
                        if not isinstance(i, int):
                            pe.wait_ge(col_moved.sem, col_moved.at(i * SLOTS + j - 2))
                        for f in range(2):
                            last = pe.matmul(c.ps[:, 3 + j, 2 * f:2 * f + 2], rows[:, j, f * P:(f + 1) * P], comb,
                                             start=True, stop=True)
                        last.then_inc(col_ready.sem, 1)
                body(0)
                loop(pe, 1, turns, body)
    for s in (row_ready, row_moved, col_ready, col_moved):
        s.passed(n)
    c.weights_passed([turns] * SLOTS)
    m = mod[:, :, :].rearrange("p (j k) v -> p j (k v)", k=KT)

    def finish(dve, link):
        for j in (1, 4, 7):
            link(dve.tensor_scalar(m[:, j, :], m[:, j, :], 1.0, None, ALU.add))
        for j in (2, 8):
            link(dve.tensor_scalar(m[:, j, :], m[:, j, :], 0.5, None, ALU.mult))
    on_vector(c, finish)


def residual(c, x, y, ntt, mod, j, eye):
    spread, scaled = c.sig("gate_spread"), c.sig("gated_rows")
    nv = ntt // 2
    with block(c) as b:
        @b.tensor
        def _(pe):
            for v in range(nv):
                for k in range(KT):
                    col = mod[:, j * KT + k, v:v + 1].to_broadcast([P, P])
                    last = pe.matmul(c.ps[:, 2 * v + k // 4, (k % 4) * P:(k % 4 + 1) * P], col, eye, start=True, stop=True)
                last.then_inc(spread.sem, 1)

        @b.vector
        def _(dve):
            for t in range(ntt):
                dve.wait_ge(spread.sem, spread.at(t // 2 + 1))
                g = c.ps[:, 2 * (t // 2):2 * (t // 2) + 2, :].rearrange("p b n -> p (b n)")
                dve.tensor_tensor(y[:, t, :], y[:, t, :], g, ALU.mult).then_inc(scaled.sem, 1)
            for t in range(ntt):
                dve.wait_ge(scaled.sem, scaled.at(t + 1))
                dve.tensor_tensor(x[:, t, :], x[:, t, :], y[:, t, :], ALU.add)
    spread.passed(nv)
    scaled.passed(ntt)


def attention(c, units, scale, eye, mask=None, pair=None):
    s_ready, neg_ready, p_ready = c.sig("s_ready"), c.sig("negmax_ready"), c.sig("p_ready")
    w_ready, pt_ready, pt_moved = c.sig("w_ready"), c.sig("pt_ready"), c.sig("pt_moved")
    o_ready, o_moved, step = c.sig("o_ready"), c.sig("o_moved"), c.sig("dve_step")
    n = len(units)
    nk = [sum(k.shape[-1] for k in u["keys"]) for u in units]
    top = max(nk)
    maps = 2 if pair is not None else 1
    with ExitStack() as st:
        sm = c.sb(st, "scores", [P, 2, top]) if mask is not None else None
        p = c.sb(st, "probs", [P, 2, top])
        w = c.sb(st, "mixed", [P, 2, top // 2]) if maps == 2 else None
        pt = c.sb(st, "probs_t", [P, 2, 512])
        neg = c.sb(st, "negmax", [P, 2, 2])
        sums = c.sb(st, "sums", [P, 2, 2])
        inv = c.sb(st, "inv", [P, 2, 2])
        with block(c) as b:
            @b.tensor
            def _(pe):
                def score(u):
                    if u >= 2:
                        pe.wait_ge(p_ready.sem, p_ready.at(u - 1))
                    at, un, bank = 0, units[u], 2 * (u % 2)
                    for i, (q, k) in enumerate(zip(un["q"], un["keys"])):
                        m = k.shape[-1]
                        biased = un.get("bias") is not None and i == 0
                        last = pe.matmul(c.ps[:, bank, at:at + m], q, k, start=True, stop=not biased)
                        if biased:
                            last = pe.matmul(c.ps[:, bank, at:at + m], un["bias"][0], un["bias"][1], start=False, stop=True)
                        if maps == 2:
                            bank += 1
                        else:
                            at += m
                    last.then_inc(s_ready.sem, 1)

                def turns(u):
                    if maps == 2:
                        pe.wait_ge(w_ready.sem, w_ready.at(u + 1))
                    else:
                        pe.wait_ge(p_ready.sem, p_ready.at(u + 1))
                    if u >= 2:
                        pe.wait_ge(pt_moved.sem, pt_moved.at(u - 1))
                    src = w if maps == 2 else p
                    for i in range(nk[u] // maps // P):
                        last = pe.transpose(c.ps[:, 4 + u % 2, i * P:(i + 1) * P], src[:, u % 2, i * P:(i + 1) * P], eye)
                    last.then_inc(pt_ready.sem, 1)

                def values(u):
                    pe.wait_ge(pt_moved.sem, pt_moved.at(u + 1))
                    if u >= 2:
                        pe.wait_ge(o_moved.sem, o_moved.at(u - 1))
                    nv = nk[u] // maps // P
                    dv = units[u]["out"].shape[-1]
                    for i in range(nv):
                        last = pe.matmul(c.ps[:, 6 + u % 2, 0:dv], pt[:, u % 2, i * P:(i + 1) * P], units[u]["v"][i],
                                         start=(i == 0), stop=(i == nv - 1))
                    last.then_inc(o_ready.sem, 1)

                for u in range(n + 2):
                    if u < n:
                        score(u)
                    if 0 <= u - 1 < n:
                        turns(u - 1)
                    if 0 <= u - 2 < n:
                        values(u - 2)

            @b.scalar
            def _(act):
                def exps(u):
                    act.wait_ge(neg_ready.sem, neg_ready.at(u + 1))
                    if u >= 2:
                        if maps == 2:
                            act.wait_ge(w_ready.sem, w_ready.at(u - 1))
                        else:
                            act.wait_ge(pt_ready.sem, pt_ready.at(u - 1))
                    m = nk[u] // maps
                    for i in range(maps):
                        src = c.ps[:, 2 * (u % 2) + i, 0:m] if mask is None else sm[:, u % 2, 0:m]
                        last = act.activation(p[:, u % 2, i * m:(i + 1) * m], src, ACT.Exp, bias=neg[:, u % 2, i:i + 1],
                                              scale=scale if mask is None else 1.0, accum_out=sums[:, u % 2, i:i + 1])
                    last.then_inc(p_ready.sem, 1)

                def move(u):
                    act.wait_ge(pt_ready.sem, pt_ready.at(u + 1))
                    if u >= 2:
                        act.wait_ge(o_ready.sem, o_ready.at(u - 1))
                    m = nk[u] // maps
                    act.activation(pt[:, u % 2, 0:m], c.ps[:, 4 + u % 2, 0:m], ACT.Copy).then_inc(pt_moved.sem, 1)

                for u in range(n + 1):
                    if u < n:
                        exps(u)
                    if u >= 1:
                        move(u - 1)

            @b.vector
            def _(dve):
                link = Chain(dve, step)

                def top_of(u):
                    dve.wait_ge(s_ready.sem, s_ready.at(u + 1))
                    if u >= 2:
                        dve.wait_ge(p_ready.sem, p_ready.at(u - 1))
                    m = nk[u] // maps
                    src = c.ps[:, 2 * (u % 2):2 * (u % 2) + maps, 0:m]
                    if mask is not None:
                        link(dve.scalar_tensor_tensor(out=sm[:, u % 2, 0:m], in0=src[:, 0, :], scalar=scale, in1=mask[:, 0:m],
                                                      op0=ALU.mult, op1=ALU.add))
                        src = sm[:, u % 2:u % 2 + 1, 0:m]
                    link(dve.tensor_reduce(neg[:, u % 2, 0:maps], src, AX, ALU.max))
                    dve.tensor_scalar(neg[:, u % 2, 0:maps], neg[:, u % 2, 0:maps], -1.0 if mask is not None else -scale, None,
                                      ALU.mult).then_inc(neg_ready.sem, 1)

                def mix(u):
                    dve.wait_ge(p_ready.sem, p_ready.at(u + 1))
                    if u >= 2:
                        dve.wait_ge(pt_ready.sem, pt_ready.at(u - 1))
                    m = nk[u] // 2
                    link(dve.reciprocal(inv[:, u % 2, :], sums[:, u % 2, :]))
                    link(dve.tensor_scalar(inv[:, u % 2, 1:2], inv[:, u % 2, 1:2], pair, None, ALU.mult))
                    link(dve.tensor_scalar(w[:, u % 2, :], p[:, u % 2, 0:m], inv[:, u % 2, 0:1], None, ALU.mult))
                    dve.scalar_tensor_tensor(out=w[:, u % 2, :], in0=p[:, u % 2, m:2 * m], scalar=inv[:, u % 2, 1:2],
                                             in1=w[:, u % 2, :], op0=ALU.mult, op1=ALU.add).then_inc(w_ready.sem, 1)

                def recip(u):
                    dve.wait_ge(p_ready.sem, p_ready.at(u + 1))
                    link(dve.reciprocal(inv[:, u % 2, 0:1], sums[:, u % 2, 0:1]))

                def out(u):
                    dve.wait_ge(o_ready.sem, o_ready.at(u + 1))
                    dv = units[u]["out"].shape[-1]
                    src = c.ps[:, 6 + u % 2, 0:dv]
                    if maps == 2:
                        dve.tensor_copy(units[u]["out"], src).then_inc(o_moved.sem, 1)
                    else:
                        dve.tensor_scalar(units[u]["out"], src, inv[:, u % 2, 0:1], None, ALU.mult).then_inc(o_moved.sem, 1)

                for u in range(n + 2):
                    if maps == 2:
                        if u < n:
                            top_of(u)
                        if 0 <= u - 1 < n:
                            mix(u - 1)
                        if 0 <= u - 2 < n:
                            out(u - 2)
                    else:
                        if u < n:
                            top_of(u)
                        if 0 <= u - 2 < n:
                            out(u - 2)
                        if 0 <= u - 1 < n:
                            if u >= 3:
                                dve.wait_ge(o_moved.sem, o_moved.at(u - 2))
                            recip(u - 1)
                link.close()
    for s in (s_ready, neg_ready, p_ready, pt_ready, pt_moved, o_ready, o_moved):
        s.passed(n)
    if maps == 2:
        w_ready.passed(n)


def head_rms(c, v, ntt, h, d, gain, eps, extra=1.0):
    with ExitStack() as st:
        sq = c.sb(st, "sq", [P, ntt, h * d])
        ss = c.sb(st, "ss", [P, ntt, h])
        on_scalar(c, lambda act, link: act.activation(sq[:, :, :], v, ACT.Square))
        on_vector(c, lambda dve, link: [dve.tensor_reduce(ss[:, t, :], sq[:, t, :].rearrange("p (h d) -> p h d", d=d),
                                                          AX, ALU.add) for t in range(ntt)])
        inverse_root(c, ss[:, :, :].rearrange("p t h -> p (t h)"), 1.0 / d, eps)

        def steps(dve, link):
            for t in range(ntt):
                a = v[:, t, :].rearrange("p (h d) -> p h d", d=d)
                ins = dve.tensor_tensor(a, a, ss[:, t, :].unsqueeze(2).to_broadcast([P, h, d]), ALU.mult)
                link(ins) if t == ntt - 1 else None
            if gain is not None:
                for t in range(ntt):
                    a = v[:, t, :]
                    if extra == 1.0:
                        dve.tensor_tensor(a, a, gain, ALU.mult)
                    else:
                        dve.scalar_tensor_tensor(out=a, in0=a, scalar=extra, in1=gain, op0=ALU.mult, op1=ALU.mult)
        on_vector(c, steps)


def rotate(c, groups, half):
    hmax = max(g[0].shape[1] for g in groups)
    with ExitStack() as st:
        t = c.sb(st, "rot", [P, len(groups), 4, hmax, half])

        def products(dve, link):
            for i, (x1, x2, co, si) in enumerate(groups):
                h = x1.shape[1]
                cb, sb_ = (a.unsqueeze(1).to_broadcast([P, h, half]) for a in (co, si))
                for m, (a, bb) in enumerate(((x1, cb), (x2, sb_), (x1, sb_), (x2, cb))):
                    dve.tensor_tensor(t[:, i, m, 0:h, :], a, bb, ALU.mult)

        def sums(dve, link):
            for i, (x1, x2, co, si) in enumerate(groups):
                h = x1.shape[1]
                dve.tensor_tensor(x1, t[:, i, 0, 0:h, :], t[:, i, 1, 0:h, :], ALU.subtract)
                dve.tensor_tensor(x2, t[:, i, 2, 0:h, :], t[:, i, 3, 0:h, :], ALU.add)
        on_vector(c, products)
        on_vector(c, sums)


def fourier(c, u, out, tok, ch):
    with ExitStack() as st:
        a = c.sb(st, "dft", [P, 2, 512])
        with block(c) as b:
            @b.tensor
            def _(pe):
                for fg in range(2):
                    for l in range(2):
                        pe.matmul(c.ps[:, fg, :], u[:, l, fg * P:(fg + 1) * P], tok[:, l, :], start=(l == 0), stop=(l == 1))
        with block(c) as b:
            @b.scalar
            def _(act):
                act.activation(a[:, 0, :], c.ps[:, 0, :], ACT.Copy)

            @b.vector
            def _(dve):
                dve.tensor_copy(a[:, 1, :], c.ps[:, 1, :])
        with block(c) as b:
            @b.tensor
            def _(pe):
                for t in range(2):
                    for fg in range(2):
                        for part in range(2):
                            pe.matmul(c.ps[:, 2, t * 256 + fg * P:t * 256 + (fg + 1) * P],
                                      a[:, fg, part * 256 + t * P:part * 256 + (t + 1) * P], ch[:, part, :],
                                      start=(part == 0), stop=(part == 1))
        with block(c) as b:
            @b.vector
            def _(dve):
                dve.tensor_copy(out, c.ps[:, 2, :].rearrange("p (t n) -> p t n", t=2))


def gla_decay(c, g, gate_w, gate_b, a, ones, eye):
    with ExitStack() as st:
        gt = c.sb(st, "gate_t", [32, 1, TOK])
        turn(c, lambda t, k: g[:, t, :], gt, 1, 2, 32, eye, split=False)
        pre = c.sb(st, "pre", [P, 2, 256])
        e = c.sb(st, "gate_e", [P, 2, 256])
        with block(c) as b:
            @b.tensor
            def _(pe):
                for t in range(2):
                    o = c.ps[:, 0, t * 256:(t + 1) * 256]
                    pe.matmul(o, gt[:, 0, t * P:(t + 1) * P], gate_w, start=True, stop=False)
                    pe.matmul(o, ones, gate_b, start=False, stop=True)
        on_vector(c, lambda dve, link: dve.tensor_copy(pre[:, :, :], c.ps[:, 0, :].rearrange("p (t n) -> p t n", t=2)))

        def steps(act, link):
            link(act.activation(e[:, :, :], pre[:, :, :], ACT.Abs))
            link(act.activation(e[:, :, :], e[:, :, :], ACT.Exp, scale=-1.0))
            link(act.activation(e[:, :, :], e[:, :, :], ACT.Ln, bias=1.0))
        on_scalar(c, steps)
        on_vector(c, lambda dve, link: dve.scalar_tensor_tensor(
            out=a[:, :, :].rearrange("p t n -> p (t n)"), in0=pre[:, :, :].rearrange("p t n -> p (t n)"), scalar=0.0,
            in1=e[:, :, :].rearrange("p t n -> p (t n)"), op0=ALU.min, op1=ALU.subtract))


def decay_sums(pe, ps, a, dec, parts):
    for n, (t, d, tab) in enumerate(parts):
        last = pe.matmul(ps, a[:, t, d * P:(d + 1) * P], dec[:, tab, :], start=(n == 0), stop=(n == len(parts) - 1))
    return last


def gla_state(c, k, v, a, dec, state):
    f = TAB
    with ExitStack() as st:
        e = c.sb(st, "end_decay", [P, 2, 2, P])
        kd = c.sb(st, "k_decayed", [P, 2, 2, P])
        parts = [[[(0, f["gt"]), (1, f["ones"])], [(1, f["gt"])]], [[(0, f["lt"])], [(1, f["lt"]), (0, f["ones"])]]]
        with block(c) as b:
            @b.tensor
            def _(pe):
                for d in range(2):
                    for t in range(2):
                        pp = parts[d][t]
                        for n, (src, tab) in enumerate(pp):
                            pe.matmul(c.ps[:, d, t * P:(t + 1) * P], dec[:, tab, :], a[:, src, d * P:(d + 1) * P],
                                      start=(n == 0), stop=(n == len(pp) - 1))

            @b.vector
            def _(dve):
                dve.memset(state[:, :, :], 0.0)
        on_scalar(c, lambda act, link: [act.activation(e[:, d, :, :].rearrange("p t n -> p (t n)"), c.ps[:, d, 0:256], ACT.Exp)
                                        for d in range(2)])
        on_vector(c, lambda dve, link: [dve.tensor_tensor(kd[:, d, :, :], e[:, d, :, :], k, ALU.mult) for d in range(2)])
        with block(c) as b:
            @b.tensor
            def _(pe):
                for d in range(2):
                    for t in range(2):
                        pe.matmul(c.ps[:, d, 0:256], kd[:, d, t, :], v[:, t, :], start=(t == 0), stop=(t == 1))
        on_vector(c, lambda dve, link: [dve.tensor_copy(state[32 * h:32 * h + 32, d, 64 * h:64 * h + 64],
                                                        c.ps[32 * h:32 * h + 32, d, 64 * h:64 * h + 64])
                                        for d in range(2) for h in range(GLA_HEADS)])


def gla_output(c, qk, v, a, dec, levels, state, out):
    f = TAB
    e_ready, e_exp, qk_ready = c.sig("decay_ready"), c.sig("decay_exp"), c.sig("qk_ready")
    sc_ready, sc_taken = c.sig("level_ready"), c.sig("level_taken")
    n = 2 * GLA_LEVELS
    with ExitStack() as st:
        near = c.sb(st, "scores_near", [P, GLA_HEADS, 2, P])
        far = c.sb(st, "scores_far", [P, GLA_HEADS, 2, P])
        ex = c.sb(st, "decays", [P, 2, 256])
        dq = c.sb(st, "decayed", [P, 2, 2, 256])
        with block(c) as b:
            @b.tensor
            def _(pe):
                for t in range(2):
                    for h in range(GLA_HEADS):
                        r = slice(32 * h, 32 * h + 32)
                        pe.matmul(c.ps[:, h, t * P:(t + 1) * P], qk[r, 1, t * P:(t + 1) * P], qk[r, 0, t * P:(t + 1) * P],
                                  start=True, stop=True)
        with block(c) as b:
            @b.vector
            def _(dve):
                dve.tensor_scalar(near[:, :, :, :].rearrange("p h t n -> p h (t n)"), c.ps[:, 0:4, 0:2 * P], 2.0, None, ALU.mult)
        with block(c) as b:
            @b.tensor
            def _(pe):
                def sums(m):
                    d = m // GLA_LEVELS
                    if m >= 2:
                        pe.wait_ge(e_exp.sem, e_exp.at(m - 1))
                    for t in range(2):
                        last = decay_sums(pe, c.ps[:, m % 2, t * P:(t + 1) * P], a, dec, [(t, d, m)])
                    last.then_inc(e_ready.sem, 1)

                def scores(m):
                    pe.wait_ge(qk_ready.sem, qk_ready.at(m + 1))
                    for pair in range(2):
                        u = 2 * m + pair
                        if u >= 3:
                            pe.wait_ge(sc_taken.sem, sc_taken.at(u - 2))
                        for t in range(2):
                            for i in range(2):
                                h = 2 * pair + i
                                r = slice(32 * h, 32 * h + 32)
                                last = pe.matmul(c.ps[:, 2 + 2 * (u % 3) + i, t * P:(t + 1) * P],
                                                 dq[r, m % 2, 1, t * P:(t + 1) * P],
                                                 dq[r, m % 2, 0, t * P:(t + 1) * P], start=True, stop=True)
                        last.then_inc(sc_ready.sem, 1)
                sums(0)
                for m in range(n):
                    if m + 1 < n:
                        sums(m + 1)
                    scores(m)

            @b.scalar
            def _(act):
                for m in range(n):
                    act.wait_ge(e_ready.sem, e_ready.at(m + 1))
                    if m >= 2:
                        act.wait_ge(qk_ready.sem, qk_ready.at(m - 1))
                    act.activation(ex[:, m % 2, :], c.ps[:, m % 2, 0:256], ACT.Exp).then_inc(e_exp.sem, 1)

            @b.vector
            def _(dve):
                def decayed(m):
                    dve.wait_ge(e_exp.sem, e_exp.at(m + 1))
                    if m >= 2:
                        dve.wait_ge(sc_ready.sem, sc_ready.at(2 * (m - 1)))
                    dve.tensor_tensor(dq[:, m % 2, :, :], qk[:, :, :], ex[:, m % 2, :].unsqueeze(1).to_broadcast([P, 2, 256]),
                                      ALU.mult).then_inc(qk_ready.sem, 1)

                def take(m):
                    for pair in range(2):
                        u = 2 * m + pair
                        dve.wait_ge(sc_ready.sem, sc_ready.at(u + 1))
                        if u >= 2:
                            dve.wait_ge(sc_taken.sem, sc_taken.at(u - 1))
                        b0 = 2 + 2 * (u % 3)
                        for i in range(2):
                            last = dve.copy_predicated(near[:, 2 * pair + i, :, :],
                                                       levels[:, m, :].unsqueeze(1).to_broadcast([P, 2, P]),
                                                       c.ps[:, b0 + i, 0:2 * P].rearrange("p (t n) -> p t n", t=2))
                        last.then_inc(sc_taken.sem, 1)
                decayed(0)
                for m in range(n):
                    if m + 1 < n:
                        decayed(m + 1)
                    take(m)
        for s in (e_ready, e_exp, qk_ready):
            s.passed(n)
        sc_ready.passed(2 * n)
        sc_taken.passed(2 * n)
        with block(c) as b:
            @b.tensor
            def _(pe):
                for d, (t0, t1) in enumerate(((f["gt"], f["le"]), (f["ge"], f["lt"]))):
                    decay_sums(pe, c.ps[:, d, 0:P], a, dec, [(0, d, t0)])
                    decay_sums(pe, c.ps[:, d, P:2 * P], a, dec, [(1, d, t1)])
                decay_sums(pe, c.ps[:, 2, 0:P], a, dec, [(0, 0, f["le"])])
                decay_sums(pe, c.ps[:, 2, P:2 * P], a, dec, [(1, 0, f["le"]), (0, 0, f["ones"])])
                decay_sums(pe, c.ps[:, 3, 0:P], a, dec, [(0, 1, f["ge"]), (1, 1, f["ones"])])
                decay_sums(pe, c.ps[:, 3, P:2 * P], a, dec, [(1, 1, f["ge"])])
        on_scalar(c, lambda act, link: [act.activation(ex[:, d, :], c.ps[:, d, 0:256], ACT.Exp) for d in range(2)])
        on_vector(c, lambda dve, link: [dve.tensor_tensor(dq[:, d, :, :], qk[:, :, :],
                                                          ex[:, d, :].unsqueeze(1).to_broadcast([P, 2, 256]), ALU.mult)
                                        for d in range(2)])
        with block(c) as b:
            @b.tensor
            def _(pe):
                for d, (jt, it) in enumerate(((0, 1), (1, 0))):
                    for h in range(GLA_HEADS):
                        r = slice(32 * h, 32 * h + 32)
                        pe.matmul(c.ps[:, 4 + h, d * P:(d + 1) * P], dq[r, d, 1, jt * P:(jt + 1) * P],
                                  dq[r, d, 0, it * P:(it + 1) * P], start=True, stop=True)

            @b.scalar
            def _(act):
                for d in range(2):
                    act.activation(ex[:, d, :], c.ps[:, 2 + d, 0:256], ACT.Exp)
        with block(c) as b:
            @b.vector
            def _(dve):
                dve.tensor_copy(far[:, :, :, :].rearrange("p h t n -> p h (t n)"), c.ps[:, 4:8, 0:2 * P])
                if state is not None:
                    for d in range(2):
                        dve.tensor_tensor(dq[:, d, 0, :], qk[:, 0, :], ex[:, d, :], ALU.mult)
        with block(c) as b:
            @b.tensor
            def _(pe):
                for it in range(2):
                    for h in range(GLA_HEADS):
                        if state is not None:
                            for d in range(2):
                                pe.matmul(c.ps[:, 6 + it, 64 * h:64 * h + 64], dq[:, d, 0, it * P:(it + 1) * P],
                                          state[:, d, 64 * h:64 * h + 64], start=(d == 0), stop=False)
                        for jt in range(2):
                            s_t = near[:, h, it, :] if it == jt else far[:, h, jt, :]
                            pe.matmul(c.ps[:, 6 + it, 64 * h:64 * h + 64], s_t, v[:, jt, 64 * h:64 * h + 64],
                                      start=(state is None and jt == 0), stop=(jt == 1))
        on_vector(c, lambda dve, link: [dve.tensor_copy(out[:, it, :], c.ps[:, 6 + it, 0:256]) for it in range(2)])


def encoder_program(nc, A, out, stop=None):
    with ExitStack() as ctx:
        c = Core(nc, ctx)
        sb = lambda name, shape, dt=F32: ctx.enter_context(nc.sbuf_tensor(name, shape, dt))
        dma_in = c.sig("dma_in", 16)

        x = sb("x", [P, 4, D])
        eye = sb("eye", [P, P])
        rope = sb("rope", [P, 2, 2, 32])
        mod = sb("mod", [P, 9 * KT, 2])
        silu4 = sb("silu4", [P, KT, 4], F32R)
        comb = sb("comb", [4, 2])
        ones = sb("ones", [1, P])
        c.minus_half = sb("minus_half", [P, 32])
        angles = sb("angles", [P, 2, 2, 24])

        win = [chunks_of(A["w_in"][l], 0, KT, 0, D_IN) for l in range(LAYERS)]
        wout = [chunks_of(A["w_out"][l], 0, KT, 0, D) for l in range(LAYERS)]
        for l in range(LAYERS):
            c.heads.append(modulation_heads(A["w_mod"][l]))
            c.heads.append(ffn_heads(A["ffn1_w1"][l], A["ffn1_w3"][l], A["ffn1_w2"][l]))
            c.heads.append(project_heads(win[l]))
            c.heads.append(project_heads(wout[l]))
            c.heads.append(ffn_heads(A["ffn2_w1"][l], A["ffn2_w3"][l], A["ffn2_w2"][l]))
        second = []
        for l in range(LAYERS):
            s = dict(
                main=chunks_of(A["w_in_2"][l], 0, KT, 0, OFF2["gate"]),
                uq=chunks_of(A["mla_w_uq_2"][l], 0, 3, 0, MLA_HEADS * MLA_QK),
                ukv=chunks_of(A["mla_w_ukv_2"][l], 0, 2, 0, MLA_HEADS * 2 * MLA_NOPE),
                memkv=chunks_of(A["mem_w_kv_2"][l], 0, KT, 0, 2 * MEM_HEADS * MEM_HD),
                gate=chunks_of(A["w_in_2"][l], 0, KT, OFF2["gate"], 3 * D),
                b0=chunks_of(A["w_branch_2"][l], 0, 4, 0, D),
                b1=chunks_of(A["w_branch_2"][l], 512, 8, 0, D),
                b2=chunks_of(A["w_branch_2"][l], 1536, 4, 0, D),
                out=chunks_of(A["w_out_2"][l], 0, KT, 0, D))
            second.append(s)
            c.heads += [project_heads(s[k]) for k in ("main", "uq", "ukv", "memkv", "gate", "b0", "b1", "b2", "out")]
            c.heads.append(mlp_heads(A["mlp_w1_2"][l], A["mlp_w2_2"][l]))

        def load_all(pairs):
            with block(c) as b:
                @b.sync
                def _(sp):
                    with nc.allow_non_contiguous_dma(reason="small vectors"):
                        for dst, src in pairs:
                            sp.dma_start(dst, src).then_inc(dma_in.sem, 16)
                    sp.wait_ge(dma_in.sem, dma_in.at(len(pairs)))
            dma_in.passed(len(pairs))

        with ExitStack() as st:
            cond = c.sb(st, "cond", [16, P])
            cond_t = c.sb(st, "cond_t", [P, 1, P])
            with block(c) as b:
                @b.sync
                def _(sp):
                    small = [(cond[0:8, :], A["c"].rearrange("o (k p) -> (o k) p", p=P)),
                             (cond[8:16, :], A["c_ctx"].rearrange("(k p) -> k p", p=P)),
                             (eye[:, :], A["k_eye"]), (rope[:, :, :, :], A["k_rope"]),
                             (comb[0:2, :], A["k_eye"][0:2, 0:2]), (comb[2:4, :], A["k_eye"][0:2, 0:2])]
                    for dst, src in small:
                        with nc.allow_non_contiguous_dma(reason="small vectors"):
                            sp.dma_start(dst, src).then_inc(dma_in.sem, 16)
                    c.load_heads(sp, [0] * SLOTS)
                    sp.dma_start(x[:, 0:2, :], A["x"][0].rearrange("(t p) d -> p t d", p=P)).then_inc(dma_in.sem, 16)
                    sp.dma_start(x[:, 2:4, :], A["ctx"][0].rearrange("(t p) d -> p t d", p=P)).then_inc(dma_in.sem, 16)
                    sp.wait_ge(dma_in.sem, dma_in.at(len(small) + 2))
                dma_in.passed(8)

                @b.vector
                def _(dve):
                    dve.memset(ones[:, :], 1.0)
                    dve.memset(c.minus_half[:, :], -0.5)
            with block(c) as b:
                @b.tensor
                def _(pe):
                    pe.transpose(c.ps[:, 0, 0:16], cond[:, :], eye[0:16, 0:16])
            on_scalar(c, lambda act, link: act.activation(cond_t[:, 0, 0:16], c.ps[:, 0, 0:16], ACT.Silu))
            cv = cond_t[:, 0, 0:16].rearrange("p (v k) -> p k v", v=2)
            on_scalar(c, lambda act, link: act.activation(silu4[:, :, 0:2], cv, ACT.Copy))
            on_vector(c, lambda dve, link: dve.tensor_tensor(silu4[:, :, 2:4], cv, silu4[:, :, 0:2].bitcast(F32), ALU.subtract))

        def mod_cols(j, ntt):
            def cols(k):
                return [(v * TOK, (v + 1) * TOK, mod[:, (j + 1) * KT + k, v:v + 1], mod[:, j * KT + k, v:v + 1])
                        for v in range(ntt // 2)]
            return cols

        def modulated(st, j, ntt):
            pair = [c.sb(st, "xt_hi", [P, KT, ntt * P], F32R), c.sb(st, "xt_lo", [P, KT, ntt * P], F32R)]
            with ExitStack() as s2:
                xs = c.sb(s2, "xs", [P, ntt, D])
                rms_rows(c, x, ntt, xs)
                turn(c, lambda t, k: xs[:, t, k * P:(k + 1) * P], pair, KT, ntt, P, eye[:, :], cols=mod_cols(j, ntt))
            return pair

        def feed_forward(l, which, j, ntt):
            with ExitStack() as st:
                pair = modulated(st, j, ntt)
                y = c.sb(st, "y", [P, ntt, D])
                swiglu(c, A[f"ffn{which}_w1"][l], A[f"ffn{which}_w3"][l], A[f"ffn{which}_w2"][l], pair, ntt, y)
                residual(c, x, y, ntt, mod, j + 2, eye[:, :])

        for l in range(LAYERS):
            final = l == LAYERS - 1
            with ExitStack() as st:
                bm = c.sb(st, "b_mod", [9 * KT, P])
                bt = c.sb(st, "b_mod_t", [P, 1, P])
                load_all([(bm[:, :], A["b_mod"][l].rearrange("(f p) -> f p", p=P))])
                with block(c) as b:
                    @b.tensor
                    def _(pe):
                        pe.transpose(c.ps[:, 7, 0:9 * KT], bm[:, :], eye[0:9 * KT, 0:9 * KT])
                on_vector(c, lambda dve, link: dve.tensor_copy(bt[:, 0, 0:9 * KT], c.ps[:, 7, 0:9 * KT]))
                modulation(c, A["w_mod"][l], silu4, bt[:, 0, 0:9 * KT], mod, comb[:, :])
            if stop == f"mod{l}":
                return
            feed_forward(l, 1, 0, 4)
            if stop == f"ffn1_{l}":
                return
            nmix = 2 if final else 4
            with ExitStack() as st_mix:
                mix = c.sb(st_mix, "mix", [P, nmix, D])
                with ExitStack() as st:
                    h = c.sb(st, "h", [P, 4, D_IN])
                    with ExitStack() as s2:
                        pair = modulated(s2, 3, 4)
                        project(c, win[l], lhs_of(pair), 4, into(h, 256))
                    if stop == f"win{l}":
                        return
                    first_mixers(c, A, l, final, h, mix, eye, rope, ones, load_all)
                if stop == f"mix{l}":
                    return
                with ExitStack() as s2:
                    pair = [c.sb(s2, "mt_hi", [P, KT, nmix * P], F32R), c.sb(s2, "mt_lo", [P, KT, nmix * P], F32R)]
                    turn(c, lambda t, k: mix[:, t, k * P:(k + 1) * P], pair, KT, nmix, P, eye[:, :])
                    y = c.sb(s2, "y", [P, nmix, D])
                    project(c, wout[l], lhs_of(pair), nmix, into(y, 256))
                    residual(c, x, y, nmix, mod, 5, eye[:, :])
            feed_forward(l, 2, 6, nmix)
            if stop == f"first{l}":
                return

        rotary_tables(c, A, angles, load_all)
        for l in range(LAYERS):
            second_layer(c, A, l, x, angles, second[l], eye, load_all, stop)
            if stop in (f"branches{l}", f"attn2_{l}", f"second{l}"):
                return
        with block(c) as b:
            @b.sync
            def _(sp):
                sp.dma_start(out[0].rearrange("(t p) d -> p t d", p=P), x[:, 0:2, :]).then_inc(dma_in.sem, 16)
                sp.wait_ge(dma_in.sem, dma_in.at(1))


def first_mixers(c, A, l, final, h, mix, eye, rope, ones, load_all):
    O = OFF
    nmix = 2 if final else 4
    with ExitStack() as st:
        tok = c.sb(st, "dft_tok", [P, 2, 512])
        ch = c.sb(st, "dft_ch", [P, 2, P])
        load_all([(tok[:, :, :], A["k_dft_tok"]), (ch[:, :, :], A["k_dft_ch"])])
        for s in range(nmix // 2):
            t = slice(2 * s, 2 * s + 2)
            fourier(c, h[:, t, 0:256], mix[:, t, 0:256], tok, ch)
    with ExitStack() as st:
        dec = c.sb(st, "decay_tables", [P, 19, P])
        lev = c.sb(st, "level_masks", [P, 14, P], I32)
        gw = c.sb(st, "gate_w", [32, 256])
        gb = c.sb(st, "gate_b", [1, 256])
        gain = c.sb(st, "gla_gain", [P, 256])
        state = c.sb(st, "state", [P, 2, 256])
        a = c.sb(st, "log_decay", [P, 2, 256])
        qk = c.sb(st, "qk_t", [P, 2, TOK])
        on_vector(c, lambda dve, link: dve.memset(gw[:, :], 0.0))
        load_all([(dec[:, :, :], A["k_decay"]), (lev[:, :, :], A["k_levels"]),
                  (gw[0:16, 0:P], A["gla_w_gate_f"][l]), (gw[16:32, P:2 * P], A["gla_w_gate_b"][l]),
                  (gb[:, 0:P], A["gla_b_gate_f"][l:l + 1]), (gb[:, P:2 * P], A["gla_b_gate_b"][l:l + 1]),
                  (gain[:, :].rearrange("p (h d) -> p h d", d=HD), A["gla_norm"][l:l + 1].unsqueeze(1).to_broadcast([P, 4, HD]))])
        for s in (1, 0):
            t = slice(2 * s, 2 * s + 2)
            v = h[:, t, O["gla_v"]:O["gla_v"] + 256]
            gla_decay(c, h[:, t, O["gla_g"]:O["gla_g"] + 32], gw[:, :], gb[:, :], a, ones[:, :], eye[:, :])
            if s == 0 or not final:
                hs = h[:, t, O["gla_q"]:O["gla_q"] + 256]
                turn(c, lambda tt, k: hs[:, tt, k * P:(k + 1) * P], qk, 2, 2, P, eye[:, :], split=False)
                on_vector(c, lambda dve, link: dve.tensor_scalar(qk[:, 0, :], qk[:, 0, :], GLA_DK ** -0.5, None, ALU.mult))
                gla_output(c, qk, v, a, dec, lev, state if s == 0 else None, mix[:, t, 512:768])
            if s == 1:
                gla_state(c, h[:, t, O["gla_k"]:O["gla_k"] + P], v, a, dec, state)
        head_rms(c, mix[:, :, 512:768], nmix, 4, HD, gain[:, :], EPS)
        r = h[:, 0:nmix, O["gla_r"]:O["gla_r"] + 256]
        on_scalar(c, lambda act, link: act.activation(r, r, ACT.Silu))
        on_vector(c, lambda dve, link: dve.tensor_tensor(mix[:, :, 512:768], mix[:, :, 512:768], r, ALU.mult))
    with ExitStack() as st:
        g_na = c.sb(st, "na_gain", [P, 512])
        g_gqa = c.sb(st, "gqa_gain", [P, 384])
        mask = c.sb(st, "na_mask", [P, 512])
        flip = c.sb(st, "flip", [P, P])
        bias = c.sb(st, "na_bias", [P, 2, NA_HEADS, 4, GRID_W])
        rep = lambda g, n: g[l:l + 1].unsqueeze(1).to_broadcast([P, n, HD])
        hd = lambda v: v.rearrange("p (h d) -> p h d", d=HD)
        loads = [(hd(g_na[:, 0:256]), rep(A["na_q_norm"], 4)), (hd(g_na[:, 256:512]), rep(A["na_k_norm"], 4)),
                 (hd(g_gqa[:, 0:256]), rep(A["gqa_q_norm"], 4)), (hd(g_gqa[:, 256:384]), rep(A["gqa_k_norm"], 2)),
                 (mask[:, :], A["k_na_mask"]), (flip[:, :], A["k_flip"])]
        rpb = A["na_rpb"]
        for rq in range(4):
            for hh in range(NA_HEADS):
                at = ((l * NA_HEADS + hh) * RPB_ROWS + 7 - rq) * RPB_COLS + 15 - (GRID_W - 1)
                src = bass.AP(tensor=rpb.tensor, offset=rpb.offset + at, ap=[[1, GRID_W], [RPB_COLS, 4], [1, GRID_W]])
                loads.append((bias[64 * (rq % 2):64 * (rq % 2) + 64, rq // 2, hh, :, :], src))
        load_all(loads)
        head_rms(c, h[:, :, O["na_q"]:O["na_q"] + 512], 4, 8, HD, g_na[:, :], EPS)
        head_rms(c, h[:, :, O["gqa_q"]:O["gqa_q"] + 384], 4, 6, HD, g_gqa[:, :], EPS)
        groups = []
        for t in range(2):
            v = h[:, t, O["gqa_q"]:O["gqa_q"] + 384].rearrange("p (h d) -> p h d", d=HD)
            groups.append((v[:, :, 0:32], v[:, :, 32:64], rope[:, t, 0, :], rope[:, t, 1, :]))
        rotate(c, groups, 32)
        na_t = c.sb(st, "na_t", [P, 4, 512])
        turn(c, lambda t, k: h[:, t, O["na_q"] + k * P:O["na_q"] + (k + 1) * P], na_t, 4, 4, P, eye[:, :], split=False)
        units = []
        for hh in range(NA_HEADS):
            r = slice(64 * (hh % 2), 64 * (hh % 2) + 64)
            for qt in range(2):
                q = na_t[r, hh // 2, qt * P:(qt + 1) * P]
                vs = [h[:, kt, O["na_v"] + 64 * hh:O["na_v"] + 64 * hh + 64] for kt in range(4)]
                units.append(dict(q=[q, q], keys=[na_t[r, 2 + hh // 2, 0:256], na_t[r, 2 + hh // 2, 256:512]], v=vs,
                                  bias=(flip[:, :], bias[:, qt, hh, :, :].rearrange("p r c -> p (r c)")),
                                  out=mix[:, qt, 256 + 64 * hh:256 + 64 * hh + 64]))
        attention(c, units, HD ** -0.5, eye[:, :], mask=mask)
        if not final:
            units = []
            for hh in range(NA_HEADS):
                r = slice(64 * (hh % 2), 64 * (hh % 2) + 64)
                for qt in range(2, 4):
                    vs = [h[:, kt, O["na_v"] + 64 * hh:O["na_v"] + 64 * hh + 64] for kt in (2, 3)]
                    units.append(dict(q=[na_t[r, hh // 2, qt * P:(qt + 1) * P]], keys=[na_t[r, 2 + hh // 2, 256:512]], v=vs,
                                      out=mix[:, qt, 256 + 64 * hh:256 + 64 * hh + 64]))
            attention(c, units, HD ** -0.5, eye[:, :])
    with ExitStack() as st:
        g_t = c.sb(st, "gqa_t", [HD, 6, 512])
        turn(c, lambda t, k: h[:, t, O["gqa_q"] + k * HD:O["gqa_q"] + (k + 1) * HD], g_t, 6, 4, HD, eye[:, :], split=False)
        units = []
        for qt in range(nmix):
            for hh in range(4):
                kv = hh // 2
                lo = 0 if qt < 2 else 2
                vs = [h[:, kt, O["gqa_v"] + HD * kv:O["gqa_v"] + HD * kv + HD] for kt in range(lo, 4)]
                units.append(dict(q=[g_t[:, hh, qt * P:(qt + 1) * P]], keys=[g_t[:, 4 + kv, lo * P:512]], v=vs,
                                  out=mix[:, qt, 768 + HD * hh:768 + HD * hh + HD]))
        attention(c, units, HD ** -0.5, eye[:, :])


TWO_PI = 2 * math.pi
PI_A = 6.28125
PI_B = float(np.float32(TWO_PI - PI_A))
PI_C = float(TWO_PI - PI_A - PI_B)
PI_TOP = 3.1415925
ROUND = 12582912.0


def rotary_tables(c, A, angles, load_all):
    with ExitStack() as st:
        pos = c.sb(st, "pos", [P, 2], I32)
        posf = c.sb(st, "posf", [P, 2])
        inv = c.sb(st, "inv", [P, 24])
        ang = c.sb(st, "ang", [P, 2, 24])
        k = c.sb(st, "turns", [P, 2, 24])
        load_all([(pos[:, :], A["positions_2"].rearrange("o (t p) -> p (o t)", p=P)), (inv[:, :], A["k_inv"])])

        def steps(dve, link):
            link(dve.tensor_copy(posf[:, :], pos[:, :]))
            for t in range(2):
                link(dve.tensor_scalar(ang[:, t, :], inv[:, :], posf[:, t:t + 1], None, ALU.mult))
            link(dve.tensor_scalar(k[:, :, :], ang[:, :, :], 1.0 / TWO_PI, None, ALU.mult))
            link(dve.tensor_scalar(k[:, :, :], k[:, :, :], ROUND, None, ALU.add))
            link(dve.tensor_scalar(k[:, :, :], k[:, :, :], -ROUND, None, ALU.add))
            for part in (PI_A, PI_B, PI_C):
                link(dve.scalar_tensor_tensor(out=ang[:, :, :].rearrange("p t n -> p (t n)"),
                                              in0=k[:, :, :].rearrange("p t n -> p (t n)"), scalar=-part,
                                              in1=ang[:, :, :].rearrange("p t n -> p (t n)"), op0=ALU.mult, op1=ALU.add))
            link(dve.tensor_scalar(angles[:, :, 1, :], ang[:, :, :], PI_TOP, -PI_TOP, ALU.min, ALU.max))
            link(dve.tensor_scalar(ang[:, :, :], angles[:, :, 1, :], -1.0, None, ALU.mult))
            link(dve.tensor_tensor(ang[:, :, :], ang[:, :, :], angles[:, :, 1, :], ALU.max))
            link(dve.tensor_scalar(angles[:, :, 0, :], ang[:, :, :], -1.0, math.pi / 2, ALU.mult, ALU.add))
        on_vector(c, steps)
        on_scalar(c, lambda act, link: link(act.activation(angles[:, :, :, :].rearrange("p a b n -> p (a b n)"),
                                                           angles[:, :, :, :].rearrange("p a b n -> p (a b n)"), ACT.Sin)))


def layer_norm(c, x, y, g, b_):
    with ExitStack() as st:
        mean = c.sb(st, "mean", [P, 2])
        ss = c.sb(st, "ss", [P, 2])

        def center(dve, link):
            for t in range(2):
                link(dve.scalar_tensor_tensor(out=x[:, t, :], in0=x[:, t, :], scalar=ALPHA, in1=y[:, t, :],
                                              op0=ALU.mult, op1=ALU.add))
            link(dve.tensor_reduce(mean[:, :], x[:, 0:2, :], AX, ALU.add))
            link(dve.tensor_scalar(mean[:, :], mean[:, :], -1.0 / D, None, ALU.mult))
        on_vector(c, center)
        on_scalar(c, lambda act, link: [link(act.activation(y[:, t, :], x[:, t, :], ACT.Square, bias=mean[:, t:t + 1],
                                                            accum_out=ss[:, t:t + 1])) for t in range(2)])
        inverse_root(c, ss[:, :], 1.0 / D, LN_EPS)

        def scale(dve, link):
            for t in range(2):
                link(dve.tensor_scalar(x[:, t, :], x[:, t, :], mean[:, t:t + 1], ss[:, t:t + 1], ALU.add, ALU.mult))
            for t in range(2):
                link(dve.tensor_tensor(x[:, t, :], x[:, t, :], g, ALU.mult))
            for t in range(2):
                link(dve.tensor_tensor(x[:, t, :], x[:, t, :], b_, ALU.add))
        on_vector(c, scale)


def second_layer(c, A, l, x, angles, S, eye, load_all, stop):
    O = OFF2
    lam0 = 0.8 - 0.6 * math.exp(-0.3 * l)
    ident = eye[:, :]
    with ExitStack() as st_o:
        o = c.sb(st_o, "branches", [P, 2, 2048])
        with ExitStack() as st_g:
            xt = [c.sb(st_g, "x2_hi", [P, KT, TOK], F32R), c.sb(st_g, "x2_lo", [P, KT, TOK], F32R)]
            turn(c, lambda t, k: x[:, t, k * P:(k + 1) * P], xt, KT, 2, P, ident)
            with ExitStack() as st:
                h = c.sb(st, "h2", [P, 2, O["gate"]])
                project(c, S["main"], lhs_of(xt), 2, into(h, 256))
                with ExitStack() as sm:
                    q = c.sb(sm, "mla_q", [P, 2, MLA_HEADS * MLA_QK])
                    kv = c.sb(sm, "mla_kv", [P, 2, MLA_HEADS * 2 * MLA_NOPE])
                    with ExitStack() as sn:
                        gq = c.sb(sn, "gq", [P, 3])
                        gk = c.sb(sn, "gk", [P, 2])
                        load_all([(gq[:, :], A["mla_q_norm_2"][l].rearrange("(k p) -> p k", p=P)),
                                  (gk[:, :], A["mla_kv_norm_2"][l].rearrange("(k p) -> p k", p=P))])
                        head_rms(c, h[:, :, 0:Q_LORA], 2, 1, Q_LORA, None, EPS)
                        head_rms(c, h[:, :, O["ckv"]:O["ckv"] + KV_LORA], 2, 1, KV_LORA, None, EPS)
                        cq = [c.sb(sn, "cq_hi", [P, 3, TOK], F32R), c.sb(sn, "cq_lo", [P, 3, TOK], F32R)]
                        turn(c, lambda t, k: h[:, t, k * P:(k + 1) * P], cq, 3, 2, P, ident,
                             cols=lambda k: [(0, TOK, gq[:, k:k + 1], None)])
                        project(c, S["uq"], lhs_of(cq), 2, into(q, 512))
                        ck = [c.sb(sn, "ck_hi", [P, 2, TOK], F32R), c.sb(sn, "ck_lo", [P, 2, TOK], F32R)]
                        turn(c, lambda t, k: h[:, t, O["ckv"] + k * P:O["ckv"] + (k + 1) * P], ck, 2, 2, P, ident,
                             cols=lambda k: [(0, TOK, gk[:, k:k + 1], None)])
                        project(c, S["ukv"], lhs_of(ck), 2, into(kv, 512))
                    groups = []
                    for t in range(2):
                        co, si = angles[:, t, 0, 0:16], angles[:, t, 1, 0:16]
                        qv = q[:, t, :].rearrange("p (h d) -> p h d", d=MLA_QK)
                        groups.append((qv[:, :, 64:80], qv[:, :, 80:96], co, si))
                        kp = h[:, t, O["kpe"]:O["kpe"] + 32].unsqueeze(1)
                        groups.append((kp[:, :, 0:16], kp[:, :, 16:32], co, si))
                    rotate(c, groups, 16)
                    qt_ = c.sb(sm, "mla_qt", [MLA_QK, MLA_HEADS, TOK])
                    kt_ = c.sb(sm, "mla_kt", [MLA_QK, MLA_HEADS, TOK])
                    with ExitStack() as sn:
                        kk = c.sb(sn, "mla_k", [P, 2, MLA_HEADS, MLA_QK])

                        def assemble(dve, link):
                            for t in range(2):
                                src = kv[:, t, :].rearrange("p (h d) -> p h d", d=2 * MLA_NOPE)[:, :, 0:MLA_NOPE]
                                dve.tensor_copy(kk[:, t, :, 0:MLA_NOPE], src)
                                pe_ = h[:, t, O["kpe"]:O["kpe"] + 32].unsqueeze(1).to_broadcast([P, MLA_HEADS, MLA_ROPE])
                                dve.tensor_copy(kk[:, t, :, MLA_NOPE:MLA_QK], pe_)
                        on_vector(c, assemble)
                        turn(c, lambda t, k: q[:, t, k * MLA_QK:(k + 1) * MLA_QK], qt_, MLA_HEADS, 2, MLA_QK, ident, split=False)
                        turn(c, lambda t, k: kk[:, t, k, :], kt_, MLA_HEADS, 2, MLA_QK, ident, split=False)
                    units = []
                    for hh in range(MLA_HEADS):
                        for t in range(2):
                            units.append(dict(q=[qt_[:, hh, t * P:(t + 1) * P]], keys=[kt_[:, hh, :]],
                                              v=[kv[:, j, hh * 128 + 64:hh * 128 + 128] for j in range(2)],
                                              out=o[:, t, hh * 64:hh * 64 + 64]))
                    attention(c, units, MLA_QK ** -0.5, ident)
                with ExitStack() as sm:
                    groups = []
                    for t in range(2):
                        v = h[:, t, O["dq"]:O["dq"] + 2048].rearrange("p (h d) -> p h d", d=DIFF_D)
                        groups.append((v[:, :, 0:8], v[:, :, 8:16], angles[:, t, 0, 16:24], angles[:, t, 1, 16:24]))
                    rotate(c, groups, 8)
                    lam = c.sb(sm, "lam", [P, 4, DIFF_D])
                    ld = c.sb(sm, "lam_dot", [P, 2])
                    neg = c.sb(sm, "neg_lambda", [P, 1])
                    sub = c.sb(sm, "subln", [P, 8 * 128])
                    load_all([(lam[:, :, :], A["diff_lambda_2"][l:l + 1].to_broadcast([P, 4, DIFF_D])),
                              (sub[:, :].rearrange("p (h d) -> p h d", d=128),
                               A["diff_subln_2"][l:l + 1].unsqueeze(1).to_broadcast([P, 8, 128]))])

                    def dots(dve, link):
                        lv = lam[:, :, :].rearrange("p (a b) d -> p a b d", b=2)
                        link(dve.tensor_tensor(lv[:, :, 0, :], lv[:, :, 0, :], lv[:, :, 1, :], ALU.mult))
                        link(dve.tensor_reduce(ld[:, :], lv[:, :, 0, :], AX, ALU.add))
                    on_vector(c, dots)
                    on_scalar(c, lambda act, link: act.activation(ld[:, :], ld[:, :], ACT.Exp))

                    def lam_full(dve, link):
                        link(dve.tensor_tensor(neg[:, :], ld[:, 1:2], ld[:, 0:1], ALU.subtract))
                        link(dve.tensor_scalar(neg[:, :], neg[:, :], -lam0, None, ALU.add))
                    on_vector(c, lam_full)
                    dt_ = c.sb(sm, "diff_t", [P, 16, TOK])
                    turn(c, lambda t, k: h[:, t, O["dq"] + k * P:O["dq"] + (k + 1) * P], dt_, 16, 2, P, ident, split=False)
                    units = []
                    for hh in range(DIFF_HEADS):
                        for t in range(2):
                            units.append(dict(q=[dt_[64 * m:64 * m + 64, hh, t * P:(t + 1) * P] for m in range(2)],
                                              keys=[dt_[64 * m:64 * m + 64, 8 + hh, :] for m in range(2)],
                                              v=[h[:, j, O["dv"] + hh * 128:O["dv"] + (hh + 1) * 128] for j in range(2)],
                                              out=o[:, t, 512 + hh * 128:512 + (hh + 1) * 128]))
                    attention(c, units, DIFF_D ** -0.5, ident, pair=neg[:, :])
                with ExitStack() as sm:
                    sub = c.sb(sm, "subln", [P, 8 * 128])
                    load_all([(sub[:, :].rearrange("p (h d) -> p h d", d=128),
                               A["diff_subln_2"][l:l + 1].unsqueeze(1).to_broadcast([P, 8, 128]))])
                    head_rms(c, o[:, :, 512:1536], 2, 8, 128, sub[:, :], 1e-5, extra=1.0 - lam0)
                with ExitStack() as sm:
                    mkv = c.sb(sm, "mem_kv", [P, 2, 1024])
                    with ExitStack() as sn:
                        mem = c.sb(sn, "mem", [P, 2, D])
                        load_all([(mem[:, :, :], A["mem_2"][0].rearrange("(t p) d -> p t d", p=P))])
                        mt = [c.sb(sn, "mem_hi", [P, KT, TOK], F32R), c.sb(sn, "mem_lo", [P, KT, TOK], F32R)]
                        turn(c, lambda t, k: mem[:, t, k * P:(k + 1) * P], mt, KT, 2, P, ident)
                        project(c, S["memkv"], lhs_of(mt), 2, into(mkv, 256))
                    mq = c.sb(sm, "mem_qt", [P, 4, TOK])
                    mk = c.sb(sm, "mem_kt", [P, 4, TOK])
                    turn(c, lambda t, k: h[:, t, O["mq"] + k * P:O["mq"] + (k + 1) * P], mq, 4, 2, P, ident, split=False)
                    turn(c, lambda t, k: mkv[:, t, k * P:(k + 1) * P], mk, 4, 2, P, ident, split=False)
                    units = []
                    for hh in range(MEM_HEADS):
                        for t in range(2):
                            units.append(dict(q=[mq[:, hh, t * P:(t + 1) * P]], keys=[mk[:, hh, :]],
                                              v=[mkv[:, j, 512 + hh * 128:512 + (hh + 1) * 128] for j in range(2)],
                                              out=o[:, t, 1536 + hh * 128:1536 + (hh + 1) * 128]))
                    attention(c, units, MEM_HD ** -0.5, ident)
            if stop == f"branches{l}":
                return
            sg_stack = ExitStack()
            merged_in = c.sb(sg_stack, "gates", [P, 2, 3 * D])
            project(c, S["gate"], lhs_of(xt), 2, into(merged_in, 256))
            with ExitStack() as sn:
                bg = c.sb(sn, "b_gate", [P, 3 * D])
                load_all([(bg[:, :], A["b_gate_2"][l:l + 1].rearrange("o a d -> o (a d)").to_broadcast([P, 3 * D]))])
                on_vector(c, lambda dve, link: [dve.tensor_tensor(merged_in[:, t, :], merged_in[:, t, :], bg[:, :], ALU.add)
                                                for t in range(2)])
            on_scalar(c, lambda act, link: act.activation(merged_in[:, :, :], merged_in[:, :, :], ACT.Sigmoid))
            with ExitStack() as sn:
                ot = [c.sb(sn, "o_hi", [P, 16, TOK], F32R), c.sb(sn, "o_lo", [P, 16, TOK], F32R)]
                turn(c, lambda t, k: o[:, t, k * P:(k + 1) * P], ot, 16, 2, P, ident)
                for br, key in enumerate(("b0", "b1", "b2")):
                    k0 = BRANCH_ROWS[br] // P
                    cw = 512 if br != 1 else 256

                    def gated(dve, n, v, br=br, cw=cw):
                        m = merged_in[:, :, br * D + n * cw:br * D + (n + 1) * cw]
                        return dve.tensor_tensor(m, v, m, ALU.mult)
                    project(c, S[key], [lambda n, k, a=a, k0=k0: a[:, k0 + k, :] for a in ot], 2, gated, on_act=False)

            def add_up(dve, link):
                m = merged_in
                link(dve.tensor_tensor(m[:, :, 0:D], m[:, :, 0:D], m[:, :, D:2 * D], ALU.add))
                link(dve.tensor_tensor(m[:, :, 0:D], m[:, :, 0:D], m[:, :, 2 * D:3 * D], ALU.add))
            on_vector(c, add_up)
            with ExitStack() as sn:
                mt = [c.sb(sn, "m_hi", [P, KT, TOK], F32R), c.sb(sn, "m_lo", [P, KT, TOK], F32R)]
                y = c.sb(sn, "y2", [P, 2, D])
                turn(c, lambda t, k: merged_in[:, t, k * P:(k + 1) * P], mt, KT, 2, P, ident)
                project(c, S["out"], lhs_of(mt), 2, into(y, 256))
                gb = c.sb(sn, "ln", [P, 2, D])
                load_all([(gb[:, 0, :], A["ln1_g_2"][l:l + 1].to_broadcast([P, D])),
                          (gb[:, 1, :], A["ln1_b_2"][l:l + 1].to_broadcast([P, D]))])
                layer_norm(c, x, y, gb[:, 0, :], gb[:, 1, :])
            sg_stack.close()
    if stop == f"attn2_{l}":
        return
    with ExitStack() as sn:
        xt = [c.sb(sn, "x2_hi", [P, KT, TOK], F32R), c.sb(sn, "x2_lo", [P, KT, TOK], F32R)]
        y = c.sb(sn, "y2", [P, 2, D])
        turn(c, lambda t, k: x[:, t, k * P:(k + 1) * P], xt, KT, 2, P, ident)
        relu_squared_mlp(c, A["mlp_w1_2"][l], A["mlp_w2_2"][l], xt, y)
        gb = c.sb(sn, "ln", [P, 2, D])
        load_all([(gb[:, 0, :], A["ln2_g_2"][l:l + 1].to_broadcast([P, D])),
                  (gb[:, 1, :], A["ln2_b_2"][l:l + 1].to_broadcast([P, D]))])
        layer_norm(c, x, y, gb[:, 0, :], gb[:, 1, :])


_INS = ["x", "c", "ctx", "c_ctx", "w_mod", "b_mod", "ffn1_w1", "ffn1_w3", "ffn1_w2", "w_in", "na_q_norm", "na_k_norm",
        "na_rpb", "gla_w_gate_f", "gla_b_gate_f", "gla_w_gate_b", "gla_b_gate_b", "gla_norm", "gqa_q_norm", "gqa_k_norm",
        "w_out", "ffn2_w1", "ffn2_w3", "ffn2_w2", "mem_2", "positions_2", "w_in_2", "b_gate_2", "mla_q_norm_2",
        "mla_kv_norm_2", "mla_w_uq_2", "mla_w_ukv_2", "diff_lambda_2", "diff_subln_2", "mem_w_kv_2", "w_branch_2",
        "w_out_2", "ln1_g_2", "ln1_b_2", "mlp_w1_2", "mlp_w2_2", "ln2_g_2", "ln2_b_2"]


def kernel(**inputs):
    import concourse.bacc as _bacc
    from concourse.bass_utils import run_bass_kernel_spmd as _run

    nc = _bacc.Bacc("TRN2", target_bir_lowering=False, num_devices=1)
    arrays, A = {}, {}
    given = {name: np.ascontiguousarray(inputs[name]) for name in _INS}
    given.update(shape_constants())
    for name, a in given.items():
        arrays[f"in_{name}_dram"] = a
        A[name] = nc.dram_tensor(f"in_{name}_dram", a.shape, mybir.dt.from_np(a.dtype), kind="ExternalInput").ap()
    out = nc.dram_tensor("out_0_dram", (1, TOK, D), F32, kind="ExternalOutput").ap()
    encoder_program(nc, A, out)
    r = _run(nc, [arrays], core_ids=[0])
    return r.results[0]["out_0_dram"]
```

```python
import math
from contextlib import ExitStack

import numpy as np

import concourse.bass as bass
from concourse import mybir

F32 = mybir.dt.float32
F32R = mybir.dt.float32r
I32 = mybir.dt.int32
ACT = mybir.ActivationFunctionType
ALU = mybir.AluOpType
AX = mybir.AxisListType.X

P = 128
D = 1024
KT = D // P
LAYERS = 2
TOK = 256
CHUNK = 2048
SLOTS = 3

D_FF = 2816
HD = 64
NA_HEADS = 4
GLA_HEADS = 4
GLA_DK = 32
GLA_LEVELS = 7
POOL_EARLY = 3
OFF = dict(fourier=0, na_q=256, na_k=512, na_v=768, gla_q=1024, gla_k=1152, gla_v=1280, gla_r=1536,
           gla_g=1792, gqa_q=1824, gqa_k=2080, gqa_v=2208)
D_IN = 2336
GRID_W = 64
NA_COLS = 16
RPB_ROWS, RPB_COLS = 15, 31
EPS = 1e-6

MLA_HEADS, MLA_NOPE, MLA_ROPE, MLA_V = 8, 64, 32, 64
MLA_QK = MLA_NOPE + MLA_ROPE
Q_LORA, KV_LORA = 384, 256
DIFF_HEADS, DIFF_D, DIFF_ROT = 8, 64, 16
MEM_HEADS, MEM_HD = 4, 128
OFF2 = dict(cq=0, ckv=384, kpe=640, dq=672, dk=1696, dv=2720, mq=3744, gate=4256)
N_IN = 7328
D_FF_2 = 4096
ALPHA = (2 * LAYERS) ** 0.25
LN_EPS = 1e-5
BRANCH_ROWS = (0, 512, 1536, 2048)


def shape_constants():
    t = np.arange(TOK)
    ang = 2 * np.pi * np.outer(t, t) / TOK
    dft_tok = np.concatenate([np.cos(ang), np.sin(ang)], 1) / math.sqrt(TOK)
    e = np.arange(HD)
    a2 = 2 * np.pi * np.outer(e, e) / HD
    eye2 = np.eye(2)
    dft_ch = np.stack([np.kron(eye2, np.cos(a2)), -np.kron(eye2, np.sin(a2))], 1) / math.sqrt(HD)

    c = np.arange(GRID_W)
    start = np.clip(c - NA_COLS // 2, 0, GRID_W - NA_COLS)
    seen = (c[None, :] >= start[:, None]) & (c[None, :] < start[:, None] + NA_COLS)
    na_mask = np.zeros((P, 2 * TOK))
    na_mask[:, :TOK] = np.where(np.tile(seen, (2, 4)), 0.0, -1e30)
    flip = np.zeros((P, P))
    for r in range(2):
        for i in range(GRID_W):
            flip[r * GRID_W + GRID_W - 1 - i, r * GRID_W + i] = math.sqrt(HD)

    i = np.arange(P)
    T_, I_ = i[:, None], i[None, :]
    dec = []
    for back in (False, True):
        for lv in range(GLA_LEVELS):
            s = 2 ** lv
            lo = (I_ // s) * s
            end = lo + s - 1
            late = (I_ // s) % 2 == 1
            if not back:
                m = np.where(late, (T_ >= lo) & (T_ <= I_), (T_ > I_) & (T_ <= end))
            else:
                m = np.where(late, (T_ >= lo) & (T_ < I_), (T_ >= I_) & (T_ <= end))
            dec.append(m)
    dec += [T_ <= I_, T_ > I_, T_ < I_, T_ >= I_, np.ones((P, P), bool)]
    dec = np.stack(dec, 1).astype(np.float64) / 16.0
    J_ = T_
    masks = np.stack([(J_ >> lv) == ((I_ >> lv) ^ 1) for lv in range(GLA_LEVELS)], 1).astype(np.int32)

    row, col = (t // GRID_W).astype(np.float32), (t % GRID_W).astype(np.float32)
    inv = np.float32(10000.0) ** (-np.arange(16, dtype=np.float32) / np.float32(16))
    an = np.concatenate([row[:, None] * inv, col[:, None] * inv], -1)
    rope = np.stack([np.cos(an), np.sin(an)], 1).reshape(2, P, 2, 32).transpose(1, 0, 2, 3)
    inv_m = np.float32(500000.0) ** (-np.arange(0, MLA_ROPE, 2, dtype=np.float32) / np.float32(MLA_ROPE))
    inv_d = np.float32(500000.0) ** (-np.arange(0, DIFF_ROT, 2, dtype=np.float32) / np.float32(DIFF_ROT))
    inv2 = np.tile(np.concatenate([inv_m, inv_d])[None], (P, 1))
    f = lambda a: np.ascontiguousarray(a, dtype=np.float32)
    return dict(k_dft_tok=f(dft_tok.reshape(2, P, 2 * TOK).transpose(1, 0, 2)), k_dft_ch=f(dft_ch),
                k_na_mask=f(na_mask), k_flip=f(flip), k_decay=f(dec), k_levels=np.ascontiguousarray(masks),
                k_rope=f(rope), k_inv=f(inv2), k_eye=f(np.eye(P)))


ROOT_GUESS = float(0x5F3759DF)
TAB = dict(le=14, gt=15, lt=16, ge=17, ones=18)


class Signal:

    def __init__(self, sem, unit=1):
        self.sem, self.unit, self.base = sem, unit, 0

    def at(self, n):
        return (self.base + n) * self.unit

    def passed(self, n):
        self.base += n


def loop(eng, first, last, body):
    if last - first == 1:
        body(first)
    elif last > first:
        with eng.Fori(first, last) as i:
            body(i)


def split_product(pe, out, a, b, first, last):
    pe.matmul(out, a[0], b[0], start=first, stop=False)
    pe.matmul(out, a[0], b[1], start=False, stop=False)
    return pe.matmul(out, a[1], b[0], start=False, stop=last)


class Core:

    def __init__(self, nc, ctx):
        self.nc, self.ctx = nc, ctx
        self.serial = 0
        self.ps = ctx.enter_context(nc.psum_tensor("psum", [P, 8, 512], F32))
        self.raw = ctx.enter_context(nc.sbuf_tensor("w_raw", [P, SLOTS, CHUNK], F32))
        self.w_hi = ctx.enter_context(nc.sbuf_tensor("w_hi", [P, SLOTS, CHUNK], F32R))
        self.w_lo = ctx.enter_context(nc.sbuf_tensor("w_lo", [P, SLOTS, CHUNK], F32R))
        self.loaded = [self.counter(f"w_loaded{s}", 16) for s in range(SLOTS)]
        self.hi_done = [self.counter(f"w_hi_done{s}") for s in range(SLOTS)]
        self.split = [self.counter(f"w_split{s}") for s in range(SLOTS)]
        self.pre = set()
        self.heads = []
        self.next_heads = 0
        self.counters = {}

    def counter(self, name, unit=1):
        return Signal(self.ctx.enter_context(self.nc.semaphore(name)), unit)

    def sig(self, name, unit=1):
        if name not in self.counters:
            self.counters[name] = self.counter(name, unit)
        return self.counters[name]

    def sb(self, stack, name, shape, dt=F32):
        self.serial += 1
        return stack.enter_context(self.nc.sbuf_tensor(f"{name}_{self.serial}", shape, dt))

    def load(self, sp, slot, used, src):
        if not isinstance(used, int) or self.split[slot].base + used > 0:
            sp.wait_ge(self.split[slot].sem, self.split[slot].at(used))
        a, b = src.shape[1], src.shape[2]
        dst = self.raw[:, slot, 0:a * b].rearrange("p (a b) -> p a b", b=b)
        sp.dma_start(dst, src).then_inc(self.loaded[slot].sem, 16)

    def load_heads(self, sp, used):
        self.next_heads += 1
        if self.next_heads <= len(self.heads):
            for slot, src in self.heads[self.next_heads - 1]:
                self.load(sp, slot, used[slot], src)

    def hi(self, act, slot, u, n=CHUNK):
        if isinstance(u, int) and u == 0 and slot in self.pre:
            return
        act.wait_ge(self.loaded[slot].sem, self.loaded[slot].at(u + 1))
        act.activation(self.w_hi[:, slot, 0:n], self.raw[:, slot, 0:n], ACT.Copy).then_inc(self.hi_done[slot].sem, 1)

    def lo(self, dve, slot, u, n=CHUNK):
        if isinstance(u, int) and u == 0 and slot in self.pre:
            return
        dve.wait_ge(self.hi_done[slot].sem, self.hi_done[slot].at(u + 1))
        dve.tensor_tensor(self.w_lo[:, slot, 0:n], self.raw[:, slot, 0:n], self.w_hi[:, slot, 0:n].bitcast(F32),
                          ALU.subtract).then_inc(self.split[slot].sem, 1)

    def ready(self, pe, slot, u):
        pe.wait_ge(self.split[slot].sem, self.split[slot].at(u + 1))

    def w(self, slot, nk, cw):
        return [t[:, slot, 0:nk * cw].rearrange("p (k c) -> p k c", c=cw) for t in (self.w_hi, self.w_lo)]

    def weights_passed(self, used):
        for s in range(SLOTS):
            self.loaded[s].passed(used[s])
            self.hi_done[s].passed(used[s])
            self.split[s].passed(used[s])
        self.pre = set()

    def coming(self):
        return [(slot, src.shape[1] * src.shape[2]) for slot, src in self.heads[self.next_heads - 1]]


def block(c):
    return c.nc.Block(no_gpsimd_drain=True)


def chunk_of(w2d, r0, nk, c0, cw):
    cols = w2d[r0:r0 + nk * P, c0:c0 + cw] if isinstance(c0, int) else w2d[r0:r0 + nk * P, bass.ds(c0, cw)]
    return cols.rearrange("(k p) n -> p k n", p=P)


def rows_of(w2d, i, nk):
    rows = w2d[i * nk * P:(i + 1) * nk * P, :] if isinstance(i, int) else w2d[bass.ds(i * (nk * P), nk * P), :]
    return rows.rearrange("(k p) n -> p k n", p=P)


class Chain:

    def __init__(self, eng, count):
        self.eng, self.count, self.n = eng, count, 0

    def __call__(self, ins):
        ins.then_inc(self.count.sem, 1)
        self.n += 1
        self.eng.wait_ge(self.count.sem, self.count.at(self.n))

    def close(self):
        self.count.passed(self.n)


def on_vector(c, steps):
    with block(c) as b:
        @b.vector
        def _(dve):
            link = Chain(dve, c.sig("dve_step"))
            steps(dve, link)
            link.close()


def on_scalar(c, steps):
    with block(c) as b:
        @b.scalar
        def _(act):
            link = Chain(act, c.sig("act_step"))
            steps(act, link)
            link.close()


def inverse_root_steps(c, dve, link, ss, scale, eps, r, t):
    link(dve.tensor_scalar(ss, ss, scale, eps, ALU.mult, ALU.add))
    link(dve.tensor_scalar(t.bitcast(I32), ss.bitcast(I32), 1, None, ALU.arith_shift_right))
    link(dve.tensor_scalar(r.bitcast(I32), t.bitcast(I32), -1.0, ROOT_GUESS, ALU.mult, ALU.add))
    for _ in range(3):
        link(dve.tensor_tensor(t, r, r, ALU.mult))
        link(dve.scalar_tensor_tensor(out=t, in0=t, scalar=-0.5, in1=ss, op0=ALU.mult, op1=ALU.mult))
        link(dve.scalar_tensor_tensor(out=r, in0=t, scalar=1.5, in1=r, op0=ALU.add, op1=ALU.mult))


def turn(c, src, dst, nk, ntt, w, eye, split=True, cols=None, side=None, presplit=True):
    nt = ntt * P
    banks = 4
    turned, moved, highs = c.sig("turned"), c.sig("turn_moved"), c.sig("turn_hi")
    lows, moved_dve = c.sig("turn_lo"), c.sig("turn_moved_dve")
    early = c.coming() if split and presplit else []
    with ExitStack() as st:
        tmp = c.sb(st, "turn_tmp", [P, 2, nt]) if split else None
        with block(c) as b:
            @b.tensor
            def _(pe):
                for k in range(nk):
                    if k >= banks:
                        pe.wait_ge(moved.sem, moved.at(k - banks + 1))
                        if split:
                            pe.wait_ge(moved_dve.sem, moved_dve.at(k - banks + 1))
                    for t in range(ntt):
                        last = pe.transpose(c.ps[0:w, k % banks, t * P:(t + 1) * P], src(t, k), eye)
                    last.then_inc(turned.sem, 1)

            def evacuate(eng, on_act, k, part):
                t0, t1, sc, sh = part
                o, i_ = tmp[0:w, k % 2, t0:t1], c.ps[0:w, k % banks, t0:t1]
                if on_act:
                    if sc is None:
                        return eng.activation(o, i_, ACT.Copy)
                    return eng.activation(o, i_, ACT.Identity, scale=sc, bias=0.0 if sh is None else sh)
                if sc is None:
                    return eng.tensor_copy(o, i_)
                if sh is None:
                    return eng.tensor_scalar(o, i_, sc, None, ALU.mult)
                return eng.tensor_scalar(o, i_, sc, sh, ALU.mult, ALU.add)

            def halves(k):
                p_ = cols(k) if cols else [(0, nt, None, None)]
                if len(p_) == 1:
                    t0, t1, sc, sh = p_[0]
                    p_ = [(0, nt // 2, sc, sh), (nt // 2, nt, sc, sh)]
                return p_

            if not split:
                @b.scalar
                def _(act):
                    for k in range(nk):
                        act.wait_ge(turned.sem, turned.at(k + 1))
                        act.activation(dst[0:w, k, :], c.ps[0:w, k % banks, 0:nt], ACT.Copy,
                                       scale=side(k) if side else 1.0).then_inc(moved.sem, 1)
            else:
                @b.scalar
                def _(act):
                    for n, (slot, size) in enumerate(early[:1]):
                        c.hi(act, slot, 0, size)
                    for k in range(nk):
                        act.wait_ge(turned.sem, turned.at(k + 1))
                        if k >= 2:
                            act.wait_ge(lows.sem, lows.at(k - 1))
                        evacuate(act, True, k, halves(k)[0]).then_inc(moved.sem, 1)
                        act.wait_ge(moved_dve.sem, moved_dve.at(k + 1))
                        act.wait_ge(moved.sem, moved.at(k + 1))
                        act.activation(dst[0][0:w, k, :], tmp[0:w, k % 2, :], ACT.Copy).then_inc(highs.sem, 1)
                    for slot, size in early[1:]:
                        c.hi(act, slot, 0, size)

                @b.vector
                def _(dve):
                    def low(k):
                        dve.wait_ge(highs.sem, highs.at(k + 1))
                        dve.tensor_tensor(dst[1][0:w, k, :], tmp[0:w, k % 2, :], dst[0][0:w, k, :].bitcast(F32),
                                          ALU.subtract).then_inc(lows.sem, 1)

                    for k in range(nk):
                        dve.wait_ge(moved.sem, moved.at(k + 1))
                        if k >= 2:
                            dve.wait_ge(lows.sem, lows.at(k - 1))
                        evacuate(dve, False, k, halves(k)[1]).then_inc(moved_dve.sem, 1)
                        if k >= 1:
                            low(k - 1)
                    low(nk - 1)

                if early:
                    @b.gpsimd
                    def _(pool):
                        for slot, size in early[:POOL_EARLY]:
                            c.lo(pool, slot, 0, size)
                        pool.wait_ge(c.split[early[0][0]].sem, c.split[early[0][0]].at(1))
    turned.passed(nk)
    moved.passed(nk)
    if split:
        moved_dve.passed(nk)
        highs.passed(nk)
        lows.passed(nk)
        c.pre = {slot for slot, _ in early}


def rms_rows(c, x, ntt, xs):
    squares = c.sig("squares_ready")
    with ExitStack() as st:
        ss, r, tm = (c.sb(st, n, [P, ntt]) for n in ("ss", "root", "root_tmp"))
        with block(c) as b:
            @b.scalar
            def _(act):
                for t in range(0, ntt, 2):
                    act.activation(xs[:, t, :], x[:, t, :], ACT.Square, accum_out=ss[:, t:t + 1]).then_inc(squares.sem, 1)

            @b.vector
            def _(dve):
                link = Chain(dve, c.sig("dve_step"))
                for t in range(1, ntt, 2):
                    link(dve.tensor_tensor(xs[:, t, :], x[:, t, :], x[:, t, :], ALU.mult))
                    link(dve.tensor_reduce(ss[:, t:t + 1], xs[:, t, :], AX, ALU.add))
                dve.wait_ge(squares.sem, squares.at(ntt // 2))
                inverse_root_steps(c, dve, link, ss[:, :], 1.0 / D, EPS, r[:, :], tm[:, :])
                link.close()
        squares.passed(ntt // 2)
        with block(c) as b:
            @b.scalar
            def _(act):
                for t in range(0, ntt, 2):
                    act.activation(xs[:, t, :], x[:, t, :], ACT.Copy, scale=r[:, t:t + 1])

            @b.vector
            def _(dve):
                for t in range(1, ntt, 2):
                    dve.tensor_scalar(xs[:, t, :], x[:, t, :], r[:, t:t + 1], None, ALU.mult)


def chunks_of(w2d, r0, nk, col0, ncols):
    cw = min(CHUNK // nk, 512)
    out, at = [], 0
    while at < ncols:
        out.append((w2d, r0, nk, col0 + at, min(cw, ncols - at)))
        at += cw
    return out


def project_heads(chunks):
    return [(n, chunk_of(*chunks[n])) for n in range(min(SLOTS, len(chunks)))]


def project(c, chunks, lhs, ntt, evac, on_act=True):
    n_all = len(chunks)
    nk, cw = chunks[0][2], chunks[0][4]
    full = n_all if chunks[-1][4] == cw else n_all - 1
    per_bank = 512 // cw
    banks = (ntt + per_bank - 1) // per_bank
    out_ready, out_read = c.sig("proj_ready"), c.sig("proj_read")
    used = [len(range(s, n_all, SLOTS)) for s in range(SLOTS)]

    def view(slot, width):
        v = c.ps[:, 2 * slot:2 * slot + banks, :].rearrange("p b (t n) -> p (b t) n", n=cw)
        return v[:, 0:ntt, 0:width]

    def width(n):
        return chunks[n][4] if isinstance(n, int) else cw

    turns = max(0, (full - 1) // SLOTS) if full == n_all else max(0, (full - 1) // SLOTS)

    with block(c) as b:
        @b.sync
        def _(sp):
            whole = max(0, full // SLOTS)

            def three(i):
                for j in range(SLOTS):
                    w2d, r0, k_, c0, _ = chunks[0]
                    c.load(sp, j, i, chunk_of(w2d, r0, k_, c0 + (i * SLOTS + j) * cw, cw))

            regular = all(ch[:3] == chunks[0][:3] for ch in chunks) if n_all > 2 * SLOTS else False
            if regular:
                loop(sp, 1, whole, three)
                rest = range(max(1, whole) * SLOTS, n_all)
            else:
                rest = range(SLOTS, n_all)
            for n in rest:
                c.load(sp, n % SLOTS, n // SLOTS, chunk_of(*chunks[n]))
            c.load_heads(sp, used)

        @b.scalar
        def _(act):
            def high(n, i, j, wd):
                if not isinstance(n, int) or n >= SLOTS:
                    act.wait_ge(out_ready.sem, out_ready.at(n - SLOTS + 1))
                c.hi(act, j, i, nk * wd)

            def one(n, i, j, ahead):
                if ahead:
                    jn = (j + 1) % SLOTS
                    high(n + 1, i + (j + 1) // SLOTS, jn, width(n + 1))
                if on_act:
                    act.wait_ge(out_ready.sem, out_ready.at(n + 1))
                    evac(act, n, view(j, width(n))).then_inc(out_read.sem, 1)

            high(0, 0, 0, width(0))
            for n in range(min(SLOTS, n_all)):
                one(n, 0, n, n + 1 < n_all)
            loop(act, 1, turns, lambda i: [one(i * SLOTS + j, i, j, True) for j in range(SLOTS)])
            for n in range(max(1, turns) * SLOTS, n_all):
                one(n, n // SLOTS, n % SLOTS, n + 1 < n_all)

        @b.vector
        def _(dve):
            def one(n, i, j, ahead):
                if ahead:
                    c.lo(dve, (j + 1) % SLOTS, i + (j + 1) // SLOTS, nk * width(n + 1))
                if not on_act:
                    dve.wait_ge(out_ready.sem, out_ready.at(n + 1))
                    evac(dve, n, view(j, width(n))).then_inc(out_read.sem, 1)

            c.lo(dve, 0, 0, nk * width(0))
            for n in range(min(SLOTS, n_all)):
                one(n, 0, n, n + 1 < n_all)
            loop(dve, 1, turns, lambda i: [one(i * SLOTS + j, i, j, True) for j in range(SLOTS)])
            for n in range(max(1, turns) * SLOTS, n_all):
                one(n, n // SLOTS, n % SLOTS, n + 1 < n_all)

        @b.tensor
        def _(pe):
            def one(n, i, j):
                wd = width(n)
                c.ready(pe, j, i)
                if not isinstance(n, int) or n >= SLOTS:
                    pe.wait_ge(out_read.sem, out_read.at(n - SLOTS + 1))
                w = c.w(j, nk, wd)
                v = view(j, wd)
                for t in range(ntt):
                    for k in range(nk):
                        last = split_product(pe, v[:, t, :], [a(n, k)[:, t * P:(t + 1) * P] for a in lhs],
                                             [x[:, k, :] for x in w], k == 0, k == nk - 1)
                last.then_inc(out_ready.sem, 1)

            for n in range(min(SLOTS, n_all)):
                one(n, 0, n)
            loop(pe, 1, turns, lambda i: [one(i * SLOTS + j, i, j) for j in range(SLOTS)])
            for n in range(max(1, turns) * SLOTS, n_all):
                one(n, n // SLOTS, n % SLOTS)
    out_ready.passed(n_all)
    out_read.passed(n_all)
    c.weights_passed(used)


def lhs_of(pair):
    return [lambda n, k, a=a: a[:, k, :] for a in pair]


def into(dst, cw):
    def evac(eng, n, v):
        wd = v.shape[2]
        cols = slice(n * cw, n * cw + wd) if isinstance(n, int) else bass.ds(n * cw, cw)
        return eng.activation(dst[:, :, cols], v, ACT.Copy)
    return evac


def ffn_heads(w1, w3, w2):
    return [(0, chunk_of(w1, 0, KT, 0, 2 * P)), (2, chunk_of(w3, 0, KT, 0, 2 * P)), (1, rows_of(w2, 0, 2))]


def swiglu(c, w1, w3, w2, xt, ntt, y):
    nt = ntt * P
    n = D_FF // (2 * P)
    h1_ready, h3_ready, silu_ready = c.sig("h1_ready"), c.sig("h3_ready"), c.sig("silu_ready")
    g_ready, ghi_ready, glo_ready = c.sig("g_ready"), c.sig("ghi_ready"), c.sig("glo_ready")
    y_ready, y_added, y_clear = c.sig("y_ready"), c.sig("y_added"), c.sig("y_clear")
    ny = 2 * ntt
    with ExitStack() as st:
        s1 = c.sb(st, "silu", [P, 2, nt])
        g = c.sb(st, "gated", [P, 2, nt])
        gh = c.sb(st, "gated_hi", [P, 2, nt], F32R)
        gl = c.sb(st, "gated_lo", [P, 2, nt], F32R)
        with block(c) as b:
            @b.gpsimd
            def _(pool):
                pool.memset(y[:, 0:ntt, :], 0.0).then_inc(y_clear.sem, 1)

            @b.sync
            def _(sp):
                up = lambda w, i: chunk_of(w, 0, KT, i * (2 * P), 2 * P)
                c.load(sp, 0, 1, up(w1, 1))
                c.load(sp, 2, 1, up(w3, 1))
                c.load(sp, 0, 2, up(w1, 2))

                def body(i):
                    c.load(sp, 1, i, rows_of(w2, i, 2))
                    c.load(sp, 2, i + 1, up(w3, i + 1))
                    c.load(sp, 0, i + 2, up(w1, i + 2))
                loop(sp, 1, n - 2, body)
                c.load(sp, 1, n - 2, rows_of(w2, n - 2, 2))
                c.load(sp, 2, n - 1, up(w3, n - 1))
                c.load(sp, 1, n - 1, rows_of(w2, n - 1, 2))
                c.load_heads(sp, [n, n, n])

            @b.tensor
            def _(pe):
                def up(i, slot, bank, ready, held, per):
                    c.ready(pe, slot, i)
                    w = c.w(slot, KT, 2 * P)
                    for f in range(2):
                        if not isinstance(i, int) or i > 0:
                            pe.wait_ge(held.sem, held.at((i - 1) * 2 + f + 1))
                        for k in range(KT):
                            last = split_product(pe, c.ps[:, bank + f, 0:nt], [x[:, k, f * P:(f + 1) * P] for x in w],
                                                 [x[:, k, :] for x in xt], k == 0, k == KT - 1)
                        last.then_inc(ready.sem, 1)

                def down(i):
                    c.ready(pe, 1, i)
                    w = c.w(1, 2, D)
                    pe.wait_ge(glo_ready.sem, glo_ready.at((i + 1) * 2))
                    for m in range(ny):
                        t, half = m // 2, m % 2
                        if not (isinstance(i, int) and i * ny + m < 4):
                            pe.wait_ge(y_added.sem, y_added.at(i * ny + (m - 3)))
                        for f in range(2):
                            last = split_product(pe, c.ps[:, 4 + m % 4, :], [x[:, f, t * P:(t + 1) * P] for x in (gh, gl)],
                                                 [x[:, f, half * 512:(half + 1) * 512] for x in w], f == 0, f == 1)
                        last.then_inc(y_ready.sem, 1)

                def body(i):
                    up(i, 0, 0, h1_ready, silu_ready, 2)
                    down(i - 1)
                    up(i, 2, 2, h3_ready, g_ready, 2)
                up(0, 0, 0, h1_ready, silu_ready, 2)
                up(0, 2, 2, h3_ready, g_ready, 2)
                body(1)
                loop(pe, 2, n, body)
                down(n - 1)

            @b.scalar
            def _(act):
                def gate_hi(i):
                    if not isinstance(i, int) or i > 0:
                        act.wait_ge(y_ready.sem, y_ready.at(i * ny))
                    for f in range(2):
                        act.wait_ge(g_ready.sem, g_ready.at(i * 2 + f + 1))
                        act.activation(gh[:, f, :], g[:, f, :], ACT.Copy).then_inc(ghi_ready.sem, 1)

                def silu(i):
                    for f in range(2):
                        act.wait_ge(h1_ready.sem, h1_ready.at(i * 2 + f + 1))
                        if not isinstance(i, int) or i > 0:
                            act.wait_ge(g_ready.sem, g_ready.at((i - 1) * 2 + f + 1))
                        act.activation(s1[:, f, :], c.ps[:, f, 0:nt], ACT.Silu).then_inc(silu_ready.sem, 1)

                def w3_hi(i):
                    if not isinstance(i, int) or i > 0:
                        act.wait_ge(h3_ready.sem, h3_ready.at(i * 2))
                    c.hi(act, 2, i)

                def w1_hi(i):
                    if not isinstance(i, int) or i > 0:
                        act.wait_ge(h1_ready.sem, h1_ready.at(i * 2))
                    c.hi(act, 0, i)

                def w2_hi(i):
                    c.hi(act, 1, i)

                def body(i):
                    gate_hi(i - 1)
                    w2_hi(i - 1)
                    w3_hi(i)
                    silu(i)
                    w1_hi(i + 1)
                w1_hi(0)
                w3_hi(0)
                silu(0)
                w1_hi(1)
                body(1)
                loop(act, 2, n - 1, body)
                gate_hi(n - 2)
                w2_hi(n - 2)
                w3_hi(n - 1)
                silu(n - 1)
                gate_hi(n - 1)
                w2_hi(n - 1)

            @b.vector
            def _(dve):
                def gate(i):
                    for f in range(2):
                        dve.wait_ge(h3_ready.sem, h3_ready.at(i * 2 + f + 1))
                        dve.wait_ge(silu_ready.sem, silu_ready.at(i * 2 + f + 1))
                        if not isinstance(i, int) or i > 0:
                            dve.wait_ge(glo_ready.sem, glo_ready.at((i - 1) * 2 + f + 1))
                        dve.tensor_tensor(g[:, f, :], s1[:, f, :], c.ps[:, 2 + f, 0:nt], ALU.mult).then_inc(g_ready.sem, 1)
                    for f in range(2):
                        dve.wait_ge(ghi_ready.sem, ghi_ready.at(i * 2 + f + 1))
                        dve.tensor_tensor(gl[:, f, :], g[:, f, :], gh[:, f, :].bitcast(F32),
                                          ALU.subtract).then_inc(glo_ready.sem, 1)

                def add(i):
                    for m in range(ny):
                        t, half = m // 2, m % 2
                        dve.wait_ge(y_ready.sem, y_ready.at(i * ny + m + 1))
                        if not isinstance(i, int) or i > 0:
                            dve.wait_ge(y_added.sem, y_added.at((i - 1) * ny + m + 1))
                        yv = y[:, t, half * 512:(half + 1) * 512]
                        dve.tensor_tensor(yv, c.ps[:, 4 + m % 4, :], yv, ALU.add).then_inc(y_added.sem, 1)

                def body(i):
                    gate(i - 1)
                    c.lo(dve, 1, i - 1)
                    c.lo(dve, 2, i)
                    c.lo(dve, 0, i + 1)
                    add(i - 1)
                c.lo(dve, 0, 0)
                c.lo(dve, 2, 0)
                c.lo(dve, 0, 1)
                dve.wait_ge(y_clear.sem, y_clear.at(1))
                gate(0)
                c.lo(dve, 1, 0)
                c.lo(dve, 2, 1)
                c.lo(dve, 0, 2)
                add(0)
                loop(dve, 2, n - 1, body)
                gate(n - 2)
                c.lo(dve, 1, n - 2)
                c.lo(dve, 2, n - 1)
                add(n - 2)
                gate(n - 1)
                c.lo(dve, 1, n - 1)
                add(n - 1)
    for s in (h1_ready, h3_ready, silu_ready, g_ready, ghi_ready, glo_ready):
        s.passed(2 * n)
    y_ready.passed(ny * n)
    y_added.passed(ny * n)
    y_clear.passed(1)
    c.weights_passed([n, n, n])


def mlp_heads(w1, w2):
    return [(0, chunk_of(w1, 0, KT, 0, 2 * P)), (2, chunk_of(w1, 0, KT, 2 * P, 2 * P)), (1, rows_of(w2, 0, 2))]


def relu_squared_mlp(c, w1, w2, xt, y):
    ntt, nt = 2, 2 * P
    n = D_FF_2 // (2 * P)
    h_ready, relu_ready, g_ready = c.sig("h1_ready"), c.sig("silu_ready"), c.sig("g_ready")
    ghi_ready, glo_ready = c.sig("ghi_ready"), c.sig("glo_ready")
    y_ready, y_added, y_clear = c.sig("y_ready"), c.sig("y_added"), c.sig("y_clear")
    ny = 2 * ntt
    turns = n // 2
    with ExitStack() as st:
        s1 = c.sb(st, "relu", [P, 2, 2, nt])
        g = c.sb(st, "squared", [P, 2, 2, nt])
        gh = c.sb(st, "squared_hi", [P, 2, 2, nt], F32R)
        gl = c.sb(st, "squared_lo", [P, 2, 2, nt], F32R)
        slot_of = (0, 2)
        later = lambda q, m: not isinstance(q, int) or q >= m
        with block(c) as b:
            @b.gpsimd
            def _(pool):
                pool.memset(y[:, 0:ntt, :], 0.0).then_inc(y_clear.sem, 1)

            @b.sync
            def _(sp):
                up = lambda i, a: chunk_of(w1, 0, KT, i * (4 * P) + a * 2 * P, 2 * P)

                def body(i):
                    c.load(sp, 1, 2 * i - 1, rows_of(w2, 2 * i - 1, 2))
                    c.load(sp, 0, i + 1, up(i + 1, 0))
                    c.load(sp, 1, 2 * i, rows_of(w2, 2 * i, 2))
                    c.load(sp, 2, i + 1, up(i + 1, 1))
                c.load(sp, 0, 1, up(1, 0))
                c.load(sp, 2, 1, up(1, 1))
                loop(sp, 1, turns - 1, body)
                for q in range(n - 3, n):
                    c.load(sp, 1, q, rows_of(w2, q, 2))
                c.load_heads(sp, [turns, n, turns])

            @b.tensor
            def _(pe):
                def up(h, i, a):
                    c.ready(pe, slot_of[a], i)
                    w = c.w(slot_of[a], KT, 2 * P)
                    if later(h, 2):
                        pe.wait_ge(relu_ready.sem, relu_ready.at(h - 1))
                    for f in range(2):
                        for k in range(KT):
                            last = split_product(pe, c.ps[:, a, f * nt:(f + 1) * nt], [x[:, k, f * P:(f + 1) * P] for x in w],
                                                 [x[:, k, :] for x in xt], k == 0, k == KT - 1)
                    last.then_inc(h_ready.sem, 1)

                def down(q, a):
                    c.ready(pe, 1, q)
                    pe.wait_ge(glo_ready.sem, glo_ready.at(q + 1))
                    w = c.w(1, 2, D)
                    for m in range(ny):
                        t, half = m // 2, m % 2
                        if later(q, 1):
                            pe.wait_ge(y_added.sem, y_added.at((q - 1) * ny + m + 1))
                        for f in range(2):
                            last = split_product(pe, c.ps[:, 4 + m, :], [x[:, a, f, t * P:(t + 1) * P] for x in (gh, gl)],
                                                 [x[:, f, half * 512:(half + 1) * 512] for x in w], f == 0, f == 1)
                        last.then_inc(y_ready.sem, 1)

                def body(i):
                    for a in range(2):
                        up(2 * i + a, i, a)
                        if later(2 * i + a, 1):
                            down(2 * i + (a - 1), 1 - a)
                body(0)
                body(1)
                loop(pe, 2, turns, body)
                down(n - 1, 1)

            @b.scalar
            def _(act):
                def w1_hi(h, i, a):
                    if later(h, 2):
                        act.wait_ge(h_ready.sem, h_ready.at(h - 1))
                    c.hi(act, slot_of[a], i)

                def w2_hi(q):
                    if later(q, 1):
                        act.wait_ge(y_ready.sem, y_ready.at(q * ny))
                    c.hi(act, 1, q)

                def relu(h, a):
                    act.wait_ge(h_ready.sem, h_ready.at(h + 1))
                    if later(h, 2):
                        act.wait_ge(g_ready.sem, g_ready.at(h - 1))
                    act.activation(s1[:, a, :, :].rearrange("p f n -> p (f n)"), c.ps[:, a, :], ACT.Relu).then_inc(relu_ready.sem, 1)

                def g_hi(h, a):
                    act.wait_ge(g_ready.sem, g_ready.at(h + 1))
                    if later(h, 2):
                        act.wait_ge(y_ready.sem, y_ready.at((h - 1) * ny))
                    act.activation(gh[:, a, :, :], g[:, a, :, :], ACT.Copy).then_inc(ghi_ready.sem, 1)

                def body(i, last=False):
                    for a in range(2):
                        h = 2 * i + a
                        if later(h, 1):
                            w2_hi(2 * i + (a - 1))
                        if not (last and a == 1):
                            w1_hi(2 * i + (a + 1), i + a, 1 - a)
                        relu(h, a)
                        g_hi(h, a)
                w1_hi(0, 0, 0)
                body(0)
                body(1)
                loop(act, 2, turns - 1, body)
                body(turns - 1, True)
                w2_hi(n - 1)

            @b.vector
            def _(dve):
                def gate(h, a):
                    dve.wait_ge(relu_ready.sem, relu_ready.at(h + 1))
                    if later(h, 2):
                        dve.wait_ge(glo_ready.sem, glo_ready.at(h - 1))
                    dve.tensor_tensor(g[:, a, :, :], s1[:, a, :, :], s1[:, a, :, :], ALU.mult).then_inc(g_ready.sem, 1)
                    dve.wait_ge(ghi_ready.sem, ghi_ready.at(h + 1))
                    dve.tensor_tensor(gl[:, a, :, :], g[:, a, :, :], gh[:, a, :, :].bitcast(F32),
                                      ALU.subtract).then_inc(glo_ready.sem, 1)

                def add(q):
                    for m in range(ny):
                        t, half = m // 2, m % 2
                        dve.wait_ge(y_ready.sem, y_ready.at(q * ny + m + 1))
                        if later(q, 1):
                            dve.wait_ge(y_added.sem, y_added.at((q - 1) * ny + m + 1))
                        yv = y[:, t, half * 512:(half + 1) * 512]
                        dve.tensor_tensor(yv, c.ps[:, 4 + m, :], yv, ALU.add).then_inc(y_added.sem, 1)

                def body(i, last=False):
                    for a in range(2):
                        h = 2 * i + a
                        if later(h, 1):
                            c.lo(dve, 1, 2 * i + (a - 1))
                        if not (last and a == 1):
                            c.lo(dve, slot_of[1 - a], i + a)
                        gate(h, a)
                        if later(h, 1):
                            add(2 * i + (a - 1))
                c.lo(dve, 0, 0)
                dve.wait_ge(y_clear.sem, y_clear.at(1))
                body(0)
                body(1)
                loop(dve, 2, turns - 1, body)
                body(turns - 1, True)
                c.lo(dve, 1, n - 1)
                add(n - 1)
    for s in (h_ready, relu_ready, g_ready, ghi_ready, glo_ready):
        s.passed(n)
    y_ready.passed(ny * n)
    y_added.passed(ny * n)
    y_clear.passed(1)
    c.weights_passed([turns, n, turns])


def modulation_heads(w):
    return [(j, chunk_of(w, 0, KT, j * 2 * P, 2 * P)) for j in range(SLOTS)]


def modulation(c, w, silu4, bias_t, mod, comb):
    n = w.shape[1] // (2 * P)
    turns = n // SLOTS
    row_ready, row_moved = c.sig("mod_row_ready"), c.sig("mod_row_moved")
    col_ready, col_moved = c.sig("mod_col_ready"), c.sig("mod_col_moved")
    with ExitStack() as st:
        rows = c.sb(st, "mod_rows", [4, SLOTS, 2 * P])
        with block(c) as b:
            @b.sync
            def _(sp):
                loop(sp, 1, turns, lambda i: [c.load(sp, j, i, chunk_of(w, 0, KT, i * (SLOTS * 2 * P) + j * 2 * P, 2 * P))
                                              for j in range(SLOTS)])
                c.load_heads(sp, [turns] * SLOTS)

            @b.scalar
            def _(act):
                def body(i, last=False):
                    for j in range(SLOTS):
                        q = i * SLOTS + j
                        if not (last and j == SLOTS - 1):
                            if not isinstance(i, int) or q >= 2:
                                act.wait_ge(row_ready.sem, row_ready.at(q - 1))
                            c.hi(act, (j + 1) % SLOTS, i + (j + 1) // SLOTS)
                        act.wait_ge(row_ready.sem, row_ready.at(q + 1))
                        if not isinstance(i, int) or q >= SLOTS:
                            act.wait_ge(col_ready.sem, col_ready.at(q - SLOTS + 1))
                        act.activation(rows[:, j, :], c.ps[0:4, j, 0:2 * P], ACT.Copy).then_inc(row_moved.sem, 1)
                c.hi(act, 0, 0)
                body(0)
                loop(act, 1, turns - 1, body)
                body(turns - 1, True)

            @b.vector
            def _(dve):
                def add(q, i, jb):
                    dve.wait_ge(col_ready.sem, col_ready.at(q + 1))
                    o = mod[:, 2 * q:2 * q + 2, :] if isinstance(i, int) else mod[:, bass.ds(q * 2, 2), :]
                    bt = bias_t[:, 2 * q:2 * q + 2] if isinstance(i, int) else bias_t[:, bass.ds(q * 2, 2)]
                    dve.tensor_tensor(o, c.ps[:, 3 + jb, 0:4].rearrange("p (f v) -> p f v", v=2),
                                      bt.unsqueeze(2).to_broadcast([P, 2, 2]), ALU.add).then_inc(col_moved.sem, 1)

                def body(i, last=False):
                    for j in range(SLOTS):
                        q = i * SLOTS + j
                        if not (last and j == SLOTS - 1):
                            c.lo(dve, (j + 1) % SLOTS, i + (j + 1) // SLOTS)
                        if not isinstance(i, int) or q >= 1:
                            add(q - 1, i, (j - 1) % SLOTS)
                c.lo(dve, 0, 0)
                body(0)
                loop(dve, 1, turns - 1, body)
                body(turns - 1, True)
                add(n - 1, 0, SLOTS - 1)

            @b.tensor
            def _(pe):
                def cols(q, i, jb):
                    pe.wait_ge(row_moved.sem, row_moved.at(q + 1))
                    if not isinstance(i, int) or q >= SLOTS:
                        pe.wait_ge(col_moved.sem, col_moved.at(q - SLOTS + 1))
                    for f in range(2):
                        last = pe.matmul(c.ps[:, 3 + jb, 2 * f:2 * f + 2], rows[:, jb, f * P:(f + 1) * P], comb,
                                         start=True, stop=True)
                    last.then_inc(col_ready.sem, 1)

                def body(i):
                    for j in range(SLOTS):
                        q = i * SLOTS + j
                        c.ready(pe, j, i)
                        if not isinstance(i, int) or q >= SLOTS:
                            pe.wait_ge(row_moved.sem, row_moved.at(q - SLOTS + 1))
                        wv = c.w(j, KT, 2 * P)
                        for h in range(2):
                            for k in range(KT):
                                last = pe.matmul(c.ps[0:4, j, 0:2 * P], silu4[:, k, :], wv[h][:, k, :],
                                                 start=(h + k == 0), stop=(h == 1 and k == KT - 1))
                        last.then_inc(row_ready.sem, 1)
                        if not isinstance(i, int) or q >= 1:
                            cols(q - 1, i if not isinstance(i, int) else 0, (j - 1) % SLOTS)
                body(0)
                body(1)
                loop(pe, 2, turns, body)
                cols(n - 1, 0, SLOTS - 1)
    for s in (row_ready, row_moved, col_ready, col_moved):
        s.passed(n)
    c.weights_passed([turns] * SLOTS)
    m = mod[:, :, :].rearrange("p (j k) v -> p j (k v)", k=KT)

    def finish(dve, link):
        for j in (1, 4, 7):
            link(dve.tensor_scalar(m[:, j, :], m[:, j, :], 1.0, None, ALU.add))
        for j in (2, 8):
            link(dve.tensor_scalar(m[:, j, :], m[:, j, :], 0.5, None, ALU.mult))
    on_vector(c, finish)


def residual(c, x, y, ntt, mod, j, eye):
    spread, scaled = c.sig("gate_spread"), c.sig("gated_rows")
    nv = ntt // 2
    with block(c) as b:
        @b.tensor
        def _(pe):
            for v in range(nv):
                for k in range(KT):
                    col = mod[:, j * KT + k, v:v + 1].to_broadcast([P, P])
                    last = pe.matmul(c.ps[:, 2 * v + k // 4, (k % 4) * P:(k % 4 + 1) * P], col, eye, start=True, stop=True)
                last.then_inc(spread.sem, 1)

        @b.vector
        def _(dve):
            for t in range(ntt):
                dve.wait_ge(spread.sem, spread.at(t // 2 + 1))
                g = c.ps[:, 2 * (t // 2):2 * (t // 2) + 2, :].rearrange("p b n -> p (b n)")
                dve.tensor_tensor(y[:, t, :], y[:, t, :], g, ALU.mult).then_inc(scaled.sem, 1)
            for t in range(ntt):
                dve.wait_ge(scaled.sem, scaled.at(t + 1))
                dve.tensor_tensor(x[:, t, :], x[:, t, :], y[:, t, :], ALU.add)
    spread.passed(nv)
    scaled.passed(ntt)


def attention(c, units, scale, eye, mask=None, pair=None):
    s_ready, neg_ready, p_ready = c.sig("s_ready"), c.sig("negmax_ready"), c.sig("p_ready")
    w_ready, pt_ready, pt_moved = c.sig("w_ready"), c.sig("pt_ready"), c.sig("pt_moved")
    o_ready, o_moved, step = c.sig("o_ready"), c.sig("o_moved"), c.sig("dve_step")
    n = len(units)
    nk = [sum(k.shape[-1] for k in u["keys"]) for u in units]
    top = max(nk)
    maps = 2 if pair is not None else 1
    with ExitStack() as st:
        sm = c.sb(st, "scores", [P, 2, top]) if mask is not None else None
        p = c.sb(st, "probs", [P, 2, top])
        w = c.sb(st, "mixed", [P, 2, top // 2]) if maps == 2 else None
        pt = c.sb(st, "probs_t", [P, 2, 512])
        neg = c.sb(st, "negmax", [P, 2, 2])
        sums = c.sb(st, "sums", [P, 2, 2])
        inv = c.sb(st, "inv", [P, 2, 2])
        with block(c) as b:
            @b.tensor
            def _(pe):
                def score(u):
                    if u >= 2:
                        pe.wait_ge(p_ready.sem, p_ready.at(u - 1))
                    at, un, bank = 0, units[u], 2 * (u % 2)
                    for i, (q, k) in enumerate(zip(un["q"], un["keys"])):
                        m = k.shape[-1]
                        biased = un.get("bias") is not None and i == 0
                        last = pe.matmul(c.ps[:, bank, at:at + m], q, k, start=True, stop=not biased)
                        if biased:
                            last = pe.matmul(c.ps[:, bank, at:at + m], un["bias"][0], un["bias"][1], start=False, stop=True)
                        if maps == 2:
                            bank += 1
                        else:
                            at += m
                    last.then_inc(s_ready.sem, 1)

                def turns(u):
                    if maps == 2:
                        pe.wait_ge(w_ready.sem, w_ready.at(u + 1))
                    else:
                        pe.wait_ge(p_ready.sem, p_ready.at(u + 1))
                    if u >= 2:
                        pe.wait_ge(pt_moved.sem, pt_moved.at(u - 1))
                    src = w if maps == 2 else p
                    for i in range(nk[u] // maps // P):
                        last = pe.transpose(c.ps[:, 4 + u % 2, i * P:(i + 1) * P], src[:, u % 2, i * P:(i + 1) * P], eye)
                    last.then_inc(pt_ready.sem, 1)

                def values(u):
                    pe.wait_ge(pt_moved.sem, pt_moved.at(u + 1))
                    if u >= 2:
                        pe.wait_ge(o_moved.sem, o_moved.at(u - 1))
                    nv = nk[u] // maps // P
                    dv = units[u]["out"].shape[-1]
                    for i in range(nv):
                        last = pe.matmul(c.ps[:, 6 + u % 2, 0:dv], pt[:, u % 2, i * P:(i + 1) * P], units[u]["v"][i],
                                         start=(i == 0), stop=(i == nv - 1))
                    last.then_inc(o_ready.sem, 1)

                for u in range(n + 3):
                    if u < n:
                        score(u)
                    if 0 <= u - 2 < n:
                        turns(u - 2)
                    if 0 <= u - 3 < n:
                        values(u - 3)

            @b.scalar
            def _(act):
                def exps(u):
                    act.wait_ge(neg_ready.sem, neg_ready.at(u + 1))
                    if u >= 2:
                        if maps == 2:
                            act.wait_ge(w_ready.sem, w_ready.at(u - 1))
                        else:
                            act.wait_ge(pt_ready.sem, pt_ready.at(u - 1))
                    m = nk[u] // maps
                    for i in range(maps):
                        src = c.ps[:, 2 * (u % 2) + i, 0:m] if mask is None else sm[:, u % 2, 0:m]
                        last = act.activation(p[:, u % 2, i * m:(i + 1) * m], src, ACT.Exp, bias=neg[:, u % 2, i:i + 1],
                                              scale=scale if mask is None else 1.0, accum_out=sums[:, u % 2, i:i + 1])
                    last.then_inc(p_ready.sem, 1)

                def move(u):
                    act.wait_ge(pt_ready.sem, pt_ready.at(u + 1))
                    if u >= 2:
                        act.wait_ge(o_ready.sem, o_ready.at(u - 1))
                    m = nk[u] // maps
                    act.activation(pt[:, u % 2, 0:m], c.ps[:, 4 + u % 2, 0:m], ACT.Copy).then_inc(pt_moved.sem, 1)

                for u in range(n + 2):
                    if u < n:
                        exps(u)
                    if u >= 2:
                        move(u - 2)

            @b.vector
            def _(dve):
                link = Chain(dve, step)

                def top_of(u):
                    dve.wait_ge(s_ready.sem, s_ready.at(u + 1))
                    if u >= 2:
                        dve.wait_ge(p_ready.sem, p_ready.at(u - 1))
                    m = nk[u] // maps
                    src = c.ps[:, 2 * (u % 2):2 * (u % 2) + maps, 0:m]
                    if mask is not None:
                        link(dve.scalar_tensor_tensor(out=sm[:, u % 2, 0:m], in0=src[:, 0, :], scalar=scale, in1=mask[:, 0:m],
                                                      op0=ALU.mult, op1=ALU.add))
                        src = sm[:, u % 2:u % 2 + 1, 0:m]
                    link(dve.tensor_reduce(neg[:, u % 2, 0:maps], src, AX, ALU.max))
                    dve.tensor_scalar(neg[:, u % 2, 0:maps], neg[:, u % 2, 0:maps], -1.0 if mask is not None else -scale, None,
                                      ALU.mult).then_inc(neg_ready.sem, 1)

                def mix(u):
                    dve.wait_ge(p_ready.sem, p_ready.at(u + 1))
                    if u >= 2:
                        dve.wait_ge(pt_ready.sem, pt_ready.at(u - 1))
                    m = nk[u] // 2
                    link(dve.reciprocal(inv[:, u % 2, :], sums[:, u % 2, :]))
                    link(dve.tensor_scalar(inv[:, u % 2, 1:2], inv[:, u % 2, 1:2], pair, None, ALU.mult))
                    link(dve.tensor_scalar(w[:, u % 2, :], p[:, u % 2, 0:m], inv[:, u % 2, 0:1], None, ALU.mult))
                    dve.scalar_tensor_tensor(out=w[:, u % 2, :], in0=p[:, u % 2, m:2 * m], scalar=inv[:, u % 2, 1:2],
                                             in1=w[:, u % 2, :], op0=ALU.mult, op1=ALU.add).then_inc(w_ready.sem, 1)

                def recip(u):
                    dve.wait_ge(p_ready.sem, p_ready.at(u + 1))
                    link(dve.reciprocal(inv[:, u % 2, 0:1], sums[:, u % 2, 0:1]))

                def out(u):
                    dve.wait_ge(o_ready.sem, o_ready.at(u + 1))
                    dv = units[u]["out"].shape[-1]
                    src = c.ps[:, 6 + u % 2, 0:dv]
                    if maps == 2:
                        dve.tensor_copy(units[u]["out"], src).then_inc(o_moved.sem, 1)
                    else:
                        dve.tensor_scalar(units[u]["out"], src, inv[:, u % 2, 0:1], None, ALU.mult).then_inc(o_moved.sem, 1)

                for u in range(n + 3):
                    if u < n:
                        top_of(u)
                    if maps == 2 and 0 <= u - 1 < n:
                        mix(u - 1)
                    if 0 <= u - 3 < n:
                        out(u - 3)
                    if maps == 1 and 0 <= u - 1 < n:
                        if u >= 3:
                            dve.wait_ge(o_moved.sem, o_moved.at(u - 2))
                        recip(u - 1)
                link.close()
    for s in (s_ready, neg_ready, p_ready, pt_ready, pt_moved, o_ready, o_moved):
        s.passed(n)
    if maps == 2:
        w_ready.passed(n)


def head_rms(c, v, ntt, h, d, gain, eps, extra=1.0):
    squares = c.sig("squares_ready")
    with ExitStack() as st:
        sq = c.sb(st, "sq", [P, ntt, h * d])
        ss, r, tm = (c.sb(st, n, [P, ntt, h]) for n in ("ss", "root", "root_tmp"))
        flat = lambda a: a[:, :, :].rearrange("p t h -> p (t h)")
        with block(c) as b:
            @b.scalar
            def _(act):
                for t in range(ntt):
                    act.activation(sq[:, t, :], v[:, t, :], ACT.Square).then_inc(squares.sem, 1)

            @b.vector
            def _(dve):
                link = Chain(dve, c.sig("dve_step"))
                for t in range(ntt):
                    dve.wait_ge(squares.sem, squares.at(t + 1))
                    link(dve.tensor_reduce(ss[:, t, :], sq[:, t, :].rearrange("p (h d) -> p h d", d=d), AX, ALU.add))
                inverse_root_steps(c, dve, link, flat(ss), 1.0 / d, eps, flat(r), flat(tm))
                if gain is None:
                    for t in range(ntt):
                        dve.tensor_scalar(v[:, t, :], v[:, t, :], r[:, t, 0:1], None, ALU.mult)
                else:
                    for t in range(ntt):
                        a = v[:, t, :].rearrange("p (h d) -> p h d", d=d)
                        link(dve.tensor_tensor(a, a, r[:, t, :].unsqueeze(2).to_broadcast([P, h, d]), ALU.mult))
                    for t in range(ntt):
                        a = v[:, t, :]
                        if extra == 1.0:
                            dve.tensor_tensor(a, a, gain, ALU.mult)
                        else:
                            dve.scalar_tensor_tensor(out=a, in0=a, scalar=extra, in1=gain, op0=ALU.mult, op1=ALU.mult)
                link.close()
        squares.passed(ntt)


def rotate(c, groups, half):
    hmax = max(g[0].shape[1] for g in groups)
    with ExitStack() as st:
        t = c.sb(st, "rot", [P, len(groups), 4, hmax, half])

        def products(dve, link):
            for i, (x1, x2, co, si) in enumerate(groups):
                h = x1.shape[1]
                cb, sb_ = (a.unsqueeze(1).to_broadcast([P, h, half]) for a in (co, si))
                for m, (a, bb) in enumerate(((x1, cb), (x2, sb_), (x1, sb_), (x2, cb))):
                    dve.tensor_tensor(t[:, i, m, 0:h, :], a, bb, ALU.mult)

        def sums(dve, link):
            for i, (x1, x2, co, si) in enumerate(groups):
                h = x1.shape[1]
                dve.tensor_tensor(x1, t[:, i, 0, 0:h, :], t[:, i, 1, 0:h, :], ALU.subtract)
                dve.tensor_tensor(x2, t[:, i, 2, 0:h, :], t[:, i, 3, 0:h, :], ALU.add)
        on_vector(c, products)
        on_vector(c, sums)


def fourier(c, u, out, tok, ch):
    with ExitStack() as st:
        a = c.sb(st, "dft", [P, 2, 512])
        with block(c) as b:
            @b.tensor
            def _(pe):
                for fg in range(2):
                    for l in range(2):
                        pe.matmul(c.ps[:, fg, :], u[:, l, fg * P:(fg + 1) * P], tok[:, l, :], start=(l == 0), stop=(l == 1))
        with block(c) as b:
            @b.scalar
            def _(act):
                act.activation(a[:, 0, :], c.ps[:, 0, :], ACT.Copy)

            @b.vector
            def _(dve):
                dve.tensor_copy(a[:, 1, :], c.ps[:, 1, :])
        with block(c) as b:
            @b.tensor
            def _(pe):
                for t in range(2):
                    for fg in range(2):
                        for part in range(2):
                            pe.matmul(c.ps[:, 2, t * 256 + fg * P:t * 256 + (fg + 1) * P],
                                      a[:, fg, part * 256 + t * P:part * 256 + (t + 1) * P], ch[:, part, :],
                                      start=(part == 0), stop=(part == 1))
        with block(c) as b:
            @b.vector
            def _(dve):
                dve.tensor_copy(out, c.ps[:, 2, :].rearrange("p (t n) -> p t n", t=2))


def gla_decay(c, g, gate_w, gate_b, a, ones, eye):
    with ExitStack() as st:
        gt = c.sb(st, "gate_t", [32, 1, 4 * P])
        turn(c, lambda t, k: g[:, t, :], gt, 1, 4, 32, eye, split=False)
        pre = c.sb(st, "pre", [P, 4 * 256])
        e = c.sb(st, "gate_e", [P, 4 * 256])
        with block(c) as b:
            @b.tensor
            def _(pe):
                for t in range(4):
                    o = c.ps[:, t // 2, (t % 2) * 256:(t % 2 + 1) * 256]
                    pe.matmul(o, gt[:, 0, t * P:(t + 1) * P], gate_w, start=True, stop=False)
                    pe.matmul(o, ones, gate_b, start=False, stop=True)
        on_vector(c, lambda dve, link: dve.tensor_copy(pre[:, :], c.ps[:, 0:2, :].rearrange("p b n -> p (b n)")))

        def steps(act, link):
            link(act.activation(e[:, :], pre[:, :], ACT.Abs))
            link(act.activation(e[:, :], e[:, :], ACT.Exp, scale=-1.0))
            link(act.activation(e[:, :], e[:, :], ACT.Ln, bias=1.0))
        on_scalar(c, steps)
        on_vector(c, lambda dve, link: dve.scalar_tensor_tensor(
            out=a[:, :, :].rearrange("p t n -> p (t n)"), in0=pre[:, :], scalar=0.0, in1=e[:, :], op0=ALU.min, op1=ALU.subtract))


def decay_sums(pe, ps, a, dec, parts):
    for n, (t, d, tab) in enumerate(parts):
        last = pe.matmul(ps, a[:, t, d * P:(d + 1) * P], dec[:, tab, :], start=(n == 0), stop=(n == len(parts) - 1))
    return last


def gla_state(c, k, v, a, dec, state):
    f = TAB
    with ExitStack() as st:
        e = c.sb(st, "end_decay", [P, 2, 2, P])
        kd = c.sb(st, "k_decayed", [P, 2, 2, P])
        parts = [[[(0, f["gt"]), (1, f["ones"])], [(1, f["gt"])]], [[(0, f["lt"])], [(1, f["lt"]), (0, f["ones"])]]]
        with block(c) as b:
            @b.tensor
            def _(pe):
                for d in range(2):
                    for t in range(2):
                        pp = parts[d][t]
                        for n, (src, tab) in enumerate(pp):
                            pe.matmul(c.ps[:, d, t * P:(t + 1) * P], dec[:, tab, :], a[:, src, d * P:(d + 1) * P],
                                      start=(n == 0), stop=(n == len(pp) - 1))

            @b.vector
            def _(dve):
                dve.memset(state[:, :, :], 0.0)
        on_scalar(c, lambda act, link: [act.activation(e[:, d, :, :].rearrange("p t n -> p (t n)"), c.ps[:, d, 0:256], ACT.Exp)
                                        for d in range(2)])
        on_vector(c, lambda dve, link: [dve.tensor_tensor(kd[:, d, :, :], e[:, d, :, :], k, ALU.mult) for d in range(2)])
        with block(c) as b:
            @b.tensor
            def _(pe):
                for d in range(2):
                    for t in range(2):
                        pe.matmul(c.ps[:, d, 0:256], kd[:, d, t, :], v[:, t, :], start=(t == 0), stop=(t == 1))
        on_vector(c, lambda dve, link: [dve.tensor_copy(state[32 * h:32 * h + 32, d, 64 * h:64 * h + 64],
                                                        c.ps[32 * h:32 * h + 32, d, 64 * h:64 * h + 64])
                                        for d in range(2) for h in range(GLA_HEADS)])


def halves_of(t, at, s, first, second):
    one = t[:, 0:1]
    return bass.AP(tensor=one.tensor, offset=one.offset + at + first,
                   ap=[list(one.ap[0]), [2 * s, 256 // (2 * s)], [s + second - first, 2], [1, s]])


def gla_output(c, qk, at, v, a, dec, levels, state, out):
    f = TAB
    span = qk.shape[1] // 2
    e_ready, e_exp, qk_ready = c.sig("decay_ready"), c.sig("decay_exp"), c.sig("qk_ready")
    sc_ready, sc_taken = c.sig("level_ready"), c.sig("level_taken")
    across = GLA_LEVELS
    n = GLA_LEVELS + 1
    with ExitStack() as st:
        near = c.sb(st, "scores_near", [P, GLA_HEADS, 2, P])
        far = c.sb(st, "scores_far", [P, GLA_HEADS, 2, P])
        ex = c.sb(st, "decays", [P, 2, n, 256])
        exi = c.sb(st, "start_decays", [P, 2, 256])
        dq = c.sb(st, "decayed", [P, 2, 512])
        dqi = c.sb(st, "q_since_start", [P, 2, 256])
        with block(c) as b:
            @b.tensor
            def _(pe):
                for d in range(2):
                    for t in range(2):
                        bank = 4 * d + 2 * t
                        l0 = d * GLA_LEVELS
                        at_ = a[:, t, d * P:(d + 1) * P]
                        pe.matmul(c.ps[:, bank, :], at_, dec[:, l0:l0 + 4, :], start=True, stop=True).then_inc(e_ready.sem, 1)
                        pe.matmul(c.ps[:, bank + 1, 0:3 * P], at_, dec[:, l0 + 4:l0 + 7, :], start=True, stop=True)
                        tab = ((f["gt"], f["le"]), (f["ge"], f["lt"]))[d][t]
                        pe.matmul(c.ps[:, bank + 1, 3 * P:4 * P], at_, dec[:, tab, :], start=True, stop=True).then_inc(e_ready.sem, 1)
                if state is not None:
                    pe.wait_ge(e_exp.sem, e_exp.at(1))
                    decay_sums(pe, c.ps[:, 0, 0:P], a, dec, [(0, 0, f["le"])])
                    decay_sums(pe, c.ps[:, 0, P:2 * P], a, dec, [(1, 0, f["le"]), (0, 0, f["ones"])])
                    decay_sums(pe, c.ps[:, 0, 2 * P:3 * P], a, dec, [(0, 1, f["ge"]), (1, 1, f["ones"])])
                    decay_sums(pe, c.ps[:, 0, 3 * P:4 * P], a, dec, [(1, 1, f["ge"])]).then_inc(e_ready.sem, 1)

            @b.scalar
            def _(act):
                for m in range(8):
                    d, t, part = m // 4, m // 2 % 2, m % 2
                    act.wait_ge(e_ready.sem, e_ready.at(m + 1))
                    act.activation(ex[:, d, 4 * part:4 * part + 4, t * P:(t + 1) * P],
                                   c.ps[:, m, :].rearrange("p (l n) -> p l n", l=4), ACT.Exp).then_inc(e_exp.sem, 1)
                if state is not None:
                    act.wait_ge(e_ready.sem, e_ready.at(9))
                    act.activation(exi[:, :, :].rearrange("p d n -> p (d n)"), c.ps[:, 0, :], ACT.Exp)
        e_ready.passed(9 if state is not None else 8)
        e_exp.passed(8)
        units = [(m, pair) for m in range(-1, n) for pair in range(2)]
        with block(c) as b:
            @b.tensor
            def _(pe):
                for u, (m, pair) in enumerate(units):
                    if m >= 0:
                        pe.wait_ge(qk_ready.sem, qk_ready.at(m + 1))
                    if u >= 4:
                        pe.wait_ge(sc_taken.sem, sc_taken.at(u - 3))
                    for t in range(2):
                        jt, it = (t, 1 - t) if m == across else (t, t)
                        for i in range(2):
                            r = slice(32 * (2 * pair + i), 32 * (2 * pair + i) + 32)
                            if m >= 0:
                                k_, q_ = dq[r, m % 2, 256 + jt * P:256 + (jt + 1) * P], dq[r, m % 2, it * P:(it + 1) * P]
                            else:
                                k_, q_ = qk[r, span + at + jt * P:span + at + (jt + 1) * P], qk[r, at + it * P:at + (it + 1) * P]
                            last = pe.matmul(c.ps[:, 2 * (u % 4) + i, t * P:(t + 1) * P], k_, q_, start=True, stop=True)
                    last.then_inc(sc_ready.sem, 1)

            @b.vector
            def _(dve):
                def decayed(m):
                    if m >= 2:
                        dve.wait_ge(sc_ready.sem, sc_ready.at(2 * m))
                    s = 2 ** m
                    buf = dq[:, m % 2, :]
                    for d in range(2):
                        first, second = (1, 0) if d == 0 else (0, 1)
                        last = dve.tensor_tensor(halves_of(buf, 0, s, first * 256, second * 256),
                                                 halves_of(qk, at, s, first * span, second * span),
                                                 halves_of(ex[:, d, m, :], 0, s, 0, 0), ALU.mult)
                    last.then_inc(qk_ready.sem, 1)

                def take(u):
                    m, pair = units[u]
                    dve.wait_ge(sc_ready.sem, sc_ready.at(u + 1))
                    if u >= 2:
                        dve.wait_ge(sc_taken.sem, sc_taken.at(u - 1))
                    b0 = 2 * (u % 4)
                    src = c.ps[:, b0:b0 + 2, 0:2 * P]
                    hs = slice(2 * pair, 2 * pair + 2)
                    if m == -1:
                        last = dve.tensor_scalar(near[:, hs, :, :].rearrange("p h t n -> p h (t n)"), src, 2.0, None, ALU.mult)
                    elif m == across:
                        last = dve.tensor_copy(far[:, hs, :, :].rearrange("p h t n -> p h (t n)"), src)
                    else:
                        last = dve.copy_predicated(near[:, hs, :, :].rearrange("p h t n -> p (h t) n"),
                                                   levels[:, m, :].unsqueeze(1).to_broadcast([P, 4, P]),
                                                   src.rearrange("p h (t n) -> p h t n", t=2))
                    last.then_inc(sc_taken.sem, 1)
                decayed(0)
                for m in range(-1, n):
                    if 0 < m + 1 < n:
                        decayed(m + 1)
                    take(2 * (m + 1))
                    take(2 * (m + 1) + 1)
                if state is not None:
                    for d in range(2):
                        dve.tensor_tensor(dqi[:, d, :], qk[:, at:at + 256], exi[:, d, :], ALU.mult)
        qk_ready.passed(n)
        sc_ready.passed(len(units))
        sc_taken.passed(len(units))
        with block(c) as b:
            @b.tensor
            def _(pe):
                for it in range(2):
                    for h in range(GLA_HEADS):
                        o = c.ps[:, 6 + it, 64 * h:64 * h + 64]
                        if state is not None:
                            for d in range(2):
                                pe.matmul(o, dqi[:, d, it * P:(it + 1) * P], state[:, d, 64 * h:64 * h + 64],
                                          start=(d == 0), stop=False)
                        for jt in range(2):
                            s_t = near[:, h, it, :] if it == jt else far[:, h, jt, :]
                            last = pe.matmul(o, s_t, v[:, jt, 64 * h:64 * h + 64], start=(state is None and jt == 0), stop=(jt == 1))
                    last.then_inc(sc_ready.sem, 1)

            @b.vector
            def _(dve):
                for it in range(2):
                    dve.wait_ge(sc_ready.sem, sc_ready.at(it + 1))
                    dve.tensor_copy(out[:, it, :], c.ps[:, 6 + it, 0:256])
        sc_ready.passed(2)


def encoder_program(nc, A, out, stop=None):
    with ExitStack() as ctx:
        c = Core(nc, ctx)
        sb = lambda name, shape, dt=F32: ctx.enter_context(nc.sbuf_tensor(name, shape, dt))
        dma_in = c.sig("dma_in", 16)

        x = sb("x", [P, 4, D])
        eye = sb("eye", [P, P])
        rope = sb("rope", [P, 2, 2, 32])
        mod = sb("mod", [P, 9 * KT, 2])
        silu4 = sb("silu4", [P, KT, 4], F32R)
        comb = sb("comb", [4, 2])
        ones = sb("ones", [1, P])
        angles = sb("angles", [P, 2, 2, 24])

        win = [chunks_of(A["w_in"][l], 0, KT, 0, D_IN) for l in range(LAYERS)]
        wout = [chunks_of(A["w_out"][l], 0, KT, 0, D) for l in range(LAYERS)]
        for l in range(LAYERS):
            c.heads.append(modulation_heads(A["w_mod"][l]))
            c.heads.append(ffn_heads(A["ffn1_w1"][l], A["ffn1_w3"][l], A["ffn1_w2"][l]))
            c.heads.append(project_heads(win[l]))
            c.heads.append(project_heads(wout[l]))
            c.heads.append(ffn_heads(A["ffn2_w1"][l], A["ffn2_w3"][l], A["ffn2_w2"][l]))
        second = []
        for l in range(LAYERS):
            s = dict(
                main=chunks_of(A["w_in_2"][l], 0, KT, 0, OFF2["gate"]),
                uq=chunks_of(A["mla_w_uq_2"][l], 0, 3, 0, MLA_HEADS * MLA_QK),
                ukv=chunks_of(A["mla_w_ukv_2"][l], 0, 2, 0, MLA_HEADS * 2 * MLA_NOPE),
                memkv=chunks_of(A["mem_w_kv_2"][l], 0, KT, 0, 2 * MEM_HEADS * MEM_HD),
                gate=chunks_of(A["w_in_2"][l], 0, KT, OFF2["gate"], 3 * D),
                b0=chunks_of(A["w_branch_2"][l], 0, 4, 0, D),
                b1=chunks_of(A["w_branch_2"][l], 512, 8, 0, D),
                b2=chunks_of(A["w_branch_2"][l], 1536, 4, 0, D),
                out=chunks_of(A["w_out_2"][l], 0, KT, 0, D))
            second.append(s)
            c.heads += [project_heads(s[k]) for k in ("main", "uq", "ukv", "memkv", "gate", "b0", "b1", "b2", "out")]
            c.heads.append(mlp_heads(A["mlp_w1_2"][l], A["mlp_w2_2"][l]))

        def load_all(pairs):
            with block(c) as b:
                @b.sync
                def _(sp):
                    with nc.allow_non_contiguous_dma(reason="small vectors"):
                        for dst, src in pairs:
                            sp.dma_start(dst, src).then_inc(dma_in.sem, 16)
                    sp.wait_ge(dma_in.sem, dma_in.at(len(pairs)))
            dma_in.passed(len(pairs))

        with ExitStack() as st:
            cond = c.sb(st, "cond", [16, P])
            cond_t = c.sb(st, "cond_t", [P, 1, P])
            with block(c) as b:
                @b.sync
                def _(sp):
                    small = [(cond[0:8, :], A["c"].rearrange("o (k p) -> (o k) p", p=P)),
                             (cond[8:16, :], A["c_ctx"].rearrange("(k p) -> k p", p=P)),
                             (eye[:, :], A["k_eye"]), (rope[:, :, :, :], A["k_rope"]),
                             (comb[0:2, :], A["k_eye"][0:2, 0:2]), (comb[2:4, :], A["k_eye"][0:2, 0:2])]
                    for dst, src in small:
                        with nc.allow_non_contiguous_dma(reason="small vectors"):
                            sp.dma_start(dst, src).then_inc(dma_in.sem, 16)
                    c.load_heads(sp, [0] * SLOTS)
                    sp.dma_start(x[:, 0:2, :], A["x"][0].rearrange("(t p) d -> p t d", p=P)).then_inc(dma_in.sem, 16)
                    sp.dma_start(x[:, 2:4, :], A["ctx"][0].rearrange("(t p) d -> p t d", p=P)).then_inc(dma_in.sem, 16)
                    sp.wait_ge(dma_in.sem, dma_in.at(len(small) + 2))
                dma_in.passed(8)

                @b.vector
                def _(dve):
                    dve.memset(ones[:, :], 1.0)
            with block(c) as b:
                @b.tensor
                def _(pe):
                    pe.transpose(c.ps[:, 0, 0:16], cond[:, :], eye[0:16, 0:16])
            on_scalar(c, lambda act, link: act.activation(cond_t[:, 0, 0:16], c.ps[:, 0, 0:16], ACT.Silu))
            cv = cond_t[:, 0, 0:16].rearrange("p (v k) -> p k v", v=2)
            on_scalar(c, lambda act, link: act.activation(silu4[:, :, 0:2], cv, ACT.Copy))
            on_vector(c, lambda dve, link: dve.tensor_tensor(silu4[:, :, 2:4], cv, silu4[:, :, 0:2].bitcast(F32), ALU.subtract))

        def mod_cols(j, ntt):
            def cols(k):
                return [(v * TOK, (v + 1) * TOK, mod[:, (j + 1) * KT + k, v:v + 1], mod[:, j * KT + k, v:v + 1])
                        for v in range(ntt // 2)]
            return cols

        def modulated(st, j, ntt):
            pair = [c.sb(st, "xt_hi", [P, KT, ntt * P], F32R), c.sb(st, "xt_lo", [P, KT, ntt * P], F32R)]
            with ExitStack() as s2:
                xs = c.sb(s2, "xs", [P, ntt, D])
                rms_rows(c, x, ntt, xs)
                turn(c, lambda t, k: xs[:, t, k * P:(k + 1) * P], pair, KT, ntt, P, eye[:, :], cols=mod_cols(j, ntt))
            return pair

        def feed_forward(l, which, j, ntt):
            with ExitStack() as st:
                pair = modulated(st, j, ntt)
                y = c.sb(st, "y", [P, ntt, D])
                swiglu(c, A[f"ffn{which}_w1"][l], A[f"ffn{which}_w3"][l], A[f"ffn{which}_w2"][l], pair, ntt, y)
                residual(c, x, y, ntt, mod, j + 2, eye[:, :])

        for l in range(LAYERS):
            final = l == LAYERS - 1
            with ExitStack() as st:
                bm = c.sb(st, "b_mod", [9 * KT, P])
                bt = c.sb(st, "b_mod_t", [P, 1, P])
                load_all([(bm[:, :], A["b_mod"][l].rearrange("(f p) -> f p", p=P))])
                with block(c) as b:
                    @b.tensor
                    def _(pe):
                        pe.transpose(c.ps[:, 7, 0:9 * KT], bm[:, :], eye[0:9 * KT, 0:9 * KT])
                on_vector(c, lambda dve, link: dve.tensor_copy(bt[:, 0, 0:9 * KT], c.ps[:, 7, 0:9 * KT]))
                modulation(c, A["w_mod"][l], silu4, bt[:, 0, 0:9 * KT], mod, comb[:, :])
            if stop == f"mod{l}":
                return
            feed_forward(l, 1, 0, 4)
            if stop == f"ffn1_{l}":
                return
            nmix = 2 if final else 4
            with ExitStack() as st_mix:
                mix = c.sb(st_mix, "mix", [P, nmix, D])
                with ExitStack() as st:
                    h = c.sb(st, "h", [P, 4, D_IN])
                    with ExitStack() as s2:
                        pair = modulated(s2, 3, 4)
                        project(c, win[l], lhs_of(pair), 4, into(h, 256))
                    if stop == f"win{l}":
                        return
                    first_mixers(c, A, l, final, h, mix, eye, rope, ones, load_all)
                if stop == f"mix{l}":
                    return
                with ExitStack() as s2:
                    pair = [c.sb(s2, "mt_hi", [P, KT, nmix * P], F32R), c.sb(s2, "mt_lo", [P, KT, nmix * P], F32R)]
                    turn(c, lambda t, k: mix[:, t, k * P:(k + 1) * P], pair, KT, nmix, P, eye[:, :])
                    y = c.sb(s2, "y", [P, nmix, D])
                    project(c, wout[l], lhs_of(pair), nmix, into(y, 256))
                    residual(c, x, y, nmix, mod, 5, eye[:, :])
            feed_forward(l, 2, 6, nmix)
            if stop == f"first{l}":
                return

        rotary_tables(c, A, angles, load_all)
        for l in range(LAYERS):
            second_layer(c, A, l, x, angles, second[l], eye, load_all, stop)
            if stop in (f"branches{l}", f"attn2_{l}", f"second{l}"):
                return
        with block(c) as b:
            @b.sync
            def _(sp):
                sp.dma_start(out[0].rearrange("(t p) d -> p t d", p=P), x[:, 0:2, :]).then_inc(dma_in.sem, 16)
                sp.wait_ge(dma_in.sem, dma_in.at(1))


def first_mixers(c, A, l, final, h, mix, eye, rope, ones, load_all):
    O = OFF
    nmix = 2 if final else 4
    with ExitStack() as st:
        tok = c.sb(st, "dft_tok", [P, 2, 512])
        ch = c.sb(st, "dft_ch", [P, 2, P])
        load_all([(tok[:, :, :], A["k_dft_tok"]), (ch[:, :, :], A["k_dft_ch"])])
        for s in range(nmix // 2):
            t = slice(2 * s, 2 * s + 2)
            fourier(c, h[:, t, 0:256], mix[:, t, 0:256], tok, ch)
    with ExitStack() as st:
        dec = c.sb(st, "decay_tables", [P, 19, P])
        lev = c.sb(st, "level_masks", [P, GLA_LEVELS, P], I32)
        gw = c.sb(st, "gate_w", [32, 256])
        gb = c.sb(st, "gate_b", [1, 256])
        gain = c.sb(st, "gla_gain", [P, 256])
        state = c.sb(st, "state", [P, 2, 256])
        a = c.sb(st, "log_decay", [P, 4, 256])
        qk = c.sb(st, "qk_t", [P, 2 * nmix * P])
        on_vector(c, lambda dve, link: dve.memset(gw[:, :], 0.0))
        load_all([(dec[:, :, :], A["k_decay"]), (lev[:, :, :], A["k_levels"]),
                  (gw[0:16, 0:P], A["gla_w_gate_f"][l]), (gw[16:32, P:2 * P], A["gla_w_gate_b"][l]),
                  (gb[:, 0:P], A["gla_b_gate_f"][l:l + 1]), (gb[:, P:2 * P], A["gla_b_gate_b"][l:l + 1]),
                  (gain[:, :].rearrange("p (h d) -> p h d", d=HD), A["gla_norm"][l:l + 1].unsqueeze(1).to_broadcast([P, 4, HD]))])
        gla_decay(c, h[:, :, O["gla_g"]:O["gla_g"] + 32], gw[:, :], gb[:, :], a, ones[:, :], eye[:, :])
        turn(c, lambda tt, k: h[:, tt, O["gla_q"] + k * P:O["gla_q"] + (k + 1) * P], qk[:, :].rearrange("p (k n) -> p k n", k=2),
             2, nmix, P, eye[:, :], split=False, side=lambda k: GLA_DK ** -0.5 if k == 0 else 1.0)
        for s in (1, 0):
            t = slice(2 * s, 2 * s + 2)
            v = h[:, t, O["gla_v"]:O["gla_v"] + 256]
            a_s = a[:, t, :]
            if s == 0 or not final:
                gla_output(c, qk, s * TOK, v, a_s, dec, lev, state if s == 0 else None, mix[:, t, 512:768])
            if s == 1:
                gla_state(c, h[:, t, O["gla_k"]:O["gla_k"] + P], v, a_s, dec, state)
        head_rms(c, mix[:, :, 512:768], nmix, 4, HD, gain[:, :], EPS)
        r = h[:, 0:nmix, O["gla_r"]:O["gla_r"] + 256]
        on_scalar(c, lambda act, link: act.activation(r, r, ACT.Silu))
        on_vector(c, lambda dve, link: dve.tensor_tensor(mix[:, :, 512:768], mix[:, :, 512:768], r, ALU.mult))
    with ExitStack() as st:
        g_na = c.sb(st, "na_gain", [P, 512])
        g_gqa = c.sb(st, "gqa_gain", [P, 384])
        mask = c.sb(st, "na_mask", [P, 512])
        flip = c.sb(st, "flip", [P, P])
        bias = c.sb(st, "na_bias", [P, 2, NA_HEADS, 4, GRID_W])
        rep = lambda g, n: g[l:l + 1].unsqueeze(1).to_broadcast([P, n, HD])
        hd = lambda v: v.rearrange("p (h d) -> p h d", d=HD)
        loads = [(hd(g_na[:, 0:256]), rep(A["na_q_norm"], 4)), (hd(g_na[:, 256:512]), rep(A["na_k_norm"], 4)),
                 (hd(g_gqa[:, 0:256]), rep(A["gqa_q_norm"], 4)), (hd(g_gqa[:, 256:384]), rep(A["gqa_k_norm"], 2)),
                 (mask[:, :], A["k_na_mask"]), (flip[:, :], A["k_flip"])]
        rpb = A["na_rpb"]
        for rq in range(4):
            for hh in range(NA_HEADS):
                at = ((l * NA_HEADS + hh) * RPB_ROWS + 7 - rq) * RPB_COLS + 15 - (GRID_W - 1)
                src = bass.AP(tensor=rpb.tensor, offset=rpb.offset + at, ap=[[1, GRID_W], [RPB_COLS, 4], [1, GRID_W]])
                loads.append((bias[64 * (rq % 2):64 * (rq % 2) + 64, rq // 2, hh, :, :], src))
        load_all(loads)
        head_rms(c, h[:, :, O["na_q"]:O["na_q"] + 512], 4, 8, HD, g_na[:, :], EPS)
        head_rms(c, h[:, :, O["gqa_q"]:O["gqa_q"] + 384], 4, 6, HD, g_gqa[:, :], EPS)
        groups = []
        for t in range(2):
            v = h[:, t, O["gqa_q"]:O["gqa_q"] + 384].rearrange("p (h d) -> p h d", d=HD)
            groups.append((v[:, :, 0:32], v[:, :, 32:64], rope[:, t, 0, :], rope[:, t, 1, :]))
        rotate(c, groups, 32)
        na_t = c.sb(st, "na_t", [P, 4, 512])
        turn(c, lambda t, k: h[:, t, O["na_q"] + k * P:O["na_q"] + (k + 1) * P], na_t, 4, 4, P, eye[:, :], split=False)
        units = []
        for hh in range(NA_HEADS):
            r = slice(64 * (hh % 2), 64 * (hh % 2) + 64)
            for qt in range(2):
                q = na_t[r, hh // 2, qt * P:(qt + 1) * P]
                vs = [h[:, kt, O["na_v"] + 64 * hh:O["na_v"] + 64 * hh + 64] for kt in range(4)]
                units.append(dict(q=[q, q], keys=[na_t[r, 2 + hh // 2, 0:256], na_t[r, 2 + hh // 2, 256:512]], v=vs,
                                  bias=(flip[:, :], bias[:, qt, hh, :, :].rearrange("p r c -> p (r c)")),
                                  out=mix[:, qt, 256 + 64 * hh:256 + 64 * hh + 64]))
        attention(c, units, HD ** -0.5, eye[:, :], mask=mask)
        if not final:
            units = []
            for hh in range(NA_HEADS):
                r = slice(64 * (hh % 2), 64 * (hh % 2) + 64)
                for qt in range(2, 4):
                    vs = [h[:, kt, O["na_v"] + 64 * hh:O["na_v"] + 64 * hh + 64] for kt in (2, 3)]
                    units.append(dict(q=[na_t[r, hh // 2, qt * P:(qt + 1) * P]], keys=[na_t[r, 2 + hh // 2, 256:512]], v=vs,
                                      out=mix[:, qt, 256 + 64 * hh:256 + 64 * hh + 64]))
            attention(c, units, HD ** -0.5, eye[:, :])
    with ExitStack() as st:
        g_t = c.sb(st, "gqa_t", [HD, 6, 512])
        turn(c, lambda t, k: h[:, t, O["gqa_q"] + k * HD:O["gqa_q"] + (k + 1) * HD], g_t, 6, 4, HD, eye[:, :], split=False)
        units = []
        for qt in range(nmix):
            for hh in range(4):
                kv = hh // 2
                lo = 0 if qt < 2 else 2
                vs = [h[:, kt, O["gqa_v"] + HD * kv:O["gqa_v"] + HD * kv + HD] for kt in range(lo, 4)]
                units.append(dict(q=[g_t[:, hh, qt * P:(qt + 1) * P]], keys=[g_t[:, 4 + kv, lo * P:512]], v=vs,
                                  out=mix[:, qt, 768 + HD * hh:768 + HD * hh + HD]))
        attention(c, units, HD ** -0.5, eye[:, :])


TWO_PI = 2 * math.pi
PI_A = 6.28125
PI_B = float(np.float32(TWO_PI - PI_A))
PI_C = float(TWO_PI - PI_A - PI_B)
PI_TOP = 3.1415925
ROUND = 12582912.0


def rotary_tables(c, A, angles, load_all):
    with ExitStack() as st:
        pos = c.sb(st, "pos", [P, 2], I32)
        posf = c.sb(st, "posf", [P, 2])
        inv = c.sb(st, "inv", [P, 24])
        ang = c.sb(st, "ang", [P, 2, 24])
        k = c.sb(st, "turns", [P, 2, 24])
        load_all([(pos[:, :], A["positions_2"].rearrange("o (t p) -> p (o t)", p=P)), (inv[:, :], A["k_inv"])])

        def steps(dve, link):
            link(dve.tensor_copy(posf[:, :], pos[:, :]))
            for t in range(2):
                link(dve.tensor_scalar(ang[:, t, :], inv[:, :], posf[:, t:t + 1], None, ALU.mult))
            link(dve.tensor_scalar(k[:, :, :], ang[:, :, :], 1.0 / TWO_PI, None, ALU.mult))
            link(dve.tensor_scalar(k[:, :, :], k[:, :, :], ROUND, None, ALU.add))
            link(dve.tensor_scalar(k[:, :, :], k[:, :, :], -ROUND, None, ALU.add))
            for part in (PI_A, PI_B, PI_C):
                link(dve.scalar_tensor_tensor(out=ang[:, :, :].rearrange("p t n -> p (t n)"),
                                              in0=k[:, :, :].rearrange("p t n -> p (t n)"), scalar=-part,
                                              in1=ang[:, :, :].rearrange("p t n -> p (t n)"), op0=ALU.mult, op1=ALU.add))
            link(dve.tensor_scalar(angles[:, :, 1, :], ang[:, :, :], PI_TOP, -PI_TOP, ALU.min, ALU.max))
            link(dve.tensor_scalar(ang[:, :, :], angles[:, :, 1, :], -1.0, None, ALU.mult))
            link(dve.tensor_tensor(ang[:, :, :], ang[:, :, :], angles[:, :, 1, :], ALU.max))
            link(dve.tensor_scalar(angles[:, :, 0, :], ang[:, :, :], -1.0, math.pi / 2, ALU.mult, ALU.add))
        on_vector(c, steps)
        on_scalar(c, lambda act, link: link(act.activation(angles[:, :, :, :].rearrange("p a b n -> p (a b n)"),
                                                           angles[:, :, :, :].rearrange("p a b n -> p (a b n)"), ACT.Sin)))


def layer_norm(c, x, y, g, b_):
    centered, squared, rooted = c.sig("mean_ready"), c.sig("squares_ready"), c.sig("root_ready")
    normed = c.sig("normed")
    with ExitStack() as st:
        sums, mean, ss, r, tm, shift = (c.sb(st, n, [P, 2]) for n in ("sum", "mean", "ss", "root", "root_tmp", "shift"))
        with block(c) as b:
            @b.vector
            def _(dve):
                link = Chain(dve, c.sig("dve_step"))
                for t in range(2):
                    link(dve.scalar_tensor_tensor(out=x[:, t, :], in0=x[:, t, :], scalar=ALPHA, in1=y[:, t, :],
                                                  op0=ALU.mult, op1=ALU.add, accum_out=sums[:, t:t + 1]))
                    dve.tensor_scalar(mean[:, t:t + 1], sums[:, t:t + 1], -1.0 / D, None, ALU.mult).then_inc(centered.sem, 1)
                dve.wait_ge(squared.sem, squared.at(2))
                inverse_root_steps(c, dve, link, ss[:, :], 1.0 / D, LN_EPS, r[:, :], tm[:, :])
                dve.tensor_tensor(shift[:, :], mean[:, :], r[:, :], ALU.mult).then_inc(rooted.sem, 1)
                dve.wait_ge(normed.sem, normed.at(1))
                link(dve.tensor_tensor(x[:, 0, :], x[:, 0, :], g, ALU.mult))
                link(dve.tensor_tensor(x[:, 0, :], x[:, 0, :], b_, ALU.add))
                dve.wait_ge(normed.sem, normed.at(2))
                link(dve.tensor_tensor(x[:, 1, :], x[:, 1, :], g, ALU.mult))
                link(dve.tensor_tensor(x[:, 1, :], x[:, 1, :], b_, ALU.add))
                link.close()

            @b.scalar
            def _(act):
                for t in range(2):
                    act.wait_ge(centered.sem, centered.at(t + 1))
                    act.activation(y[:, t, :], x[:, t, :], ACT.Square, bias=mean[:, t:t + 1],
                                   accum_out=ss[:, t:t + 1]).then_inc(squared.sem, 1)
                act.wait_ge(rooted.sem, rooted.at(1))
                for t in range(2):
                    act.activation(x[:, t, :], x[:, t, :], ACT.Identity, scale=r[:, t:t + 1],
                                   bias=shift[:, t:t + 1]).then_inc(normed.sem, 1)
        for s_, k in ((centered, 2), (squared, 2), (rooted, 1), (normed, 2)):
            s_.passed(k)


def second_layer(c, A, l, x, angles, S, eye, load_all, stop):
    O = OFF2
    lam0 = 0.8 - 0.6 * math.exp(-0.3 * l)
    ident = eye[:, :]
    with ExitStack() as st_o:
        o = c.sb(st_o, "branches", [P, 2, 2048])
        with ExitStack() as st_g:
            xt = [c.sb(st_g, "x2_hi", [P, KT, TOK], F32R), c.sb(st_g, "x2_lo", [P, KT, TOK], F32R)]
            turn(c, lambda t, k: x[:, t, k * P:(k + 1) * P], xt, KT, 2, P, ident)
            with ExitStack() as st:
                h = c.sb(st, "h2", [P, 2, O["gate"]])
                project(c, S["main"], lhs_of(xt), 2, into(h, 256))
                with ExitStack() as sm:
                    q = c.sb(sm, "mla_q", [P, 2, MLA_HEADS * MLA_QK])
                    kv = c.sb(sm, "mla_kv", [P, 2, MLA_HEADS * 2 * MLA_NOPE])
                    with ExitStack() as sn:
                        gq = c.sb(sn, "gq", [P, 3])
                        gk = c.sb(sn, "gk", [P, 2])
                        load_all([(gq[:, :], A["mla_q_norm_2"][l].rearrange("(k p) -> p k", p=P)),
                                  (gk[:, :], A["mla_kv_norm_2"][l].rearrange("(k p) -> p k", p=P))])
                        head_rms(c, h[:, :, 0:Q_LORA], 2, 1, Q_LORA, None, EPS)
                        head_rms(c, h[:, :, O["ckv"]:O["ckv"] + KV_LORA], 2, 1, KV_LORA, None, EPS)
                        cq = [c.sb(sn, "cq_hi", [P, 3, TOK], F32R), c.sb(sn, "cq_lo", [P, 3, TOK], F32R)]
                        turn(c, lambda t, k: h[:, t, k * P:(k + 1) * P], cq, 3, 2, P, ident,
                             cols=lambda k: [(0, TOK, gq[:, k:k + 1], None)])
                        project(c, S["uq"], lhs_of(cq), 2, into(q, 512))
                        ck = [c.sb(sn, "ck_hi", [P, 2, TOK], F32R), c.sb(sn, "ck_lo", [P, 2, TOK], F32R)]
                        turn(c, lambda t, k: h[:, t, O["ckv"] + k * P:O["ckv"] + (k + 1) * P], ck, 2, 2, P, ident,
                             cols=lambda k: [(0, TOK, gk[:, k:k + 1], None)])
                        project(c, S["ukv"], lhs_of(ck), 2, into(kv, 512))
                    groups = []
                    for t in range(2):
                        co, si = angles[:, t, 0, 0:16], angles[:, t, 1, 0:16]
                        qv = q[:, t, :].rearrange("p (h d) -> p h d", d=MLA_QK)
                        groups.append((qv[:, :, 64:80], qv[:, :, 80:96], co, si))
                        kp = h[:, t, O["kpe"]:O["kpe"] + 32].unsqueeze(1)
                        groups.append((kp[:, :, 0:16], kp[:, :, 16:32], co, si))
                    rotate(c, groups, 16)
                    qt_ = c.sb(sm, "mla_qt", [MLA_QK, MLA_HEADS, TOK])
                    kt_ = c.sb(sm, "mla_kt", [MLA_QK, MLA_HEADS, TOK])
                    with ExitStack() as sn:
                        kk = c.sb(sn, "mla_k", [P, 2, MLA_HEADS, MLA_QK])

                        def assemble(dve, link):
                            for t in range(2):
                                src = kv[:, t, :].rearrange("p (h d) -> p h d", d=2 * MLA_NOPE)[:, :, 0:MLA_NOPE]
                                dve.tensor_copy(kk[:, t, :, 0:MLA_NOPE], src)
                                pe_ = h[:, t, O["kpe"]:O["kpe"] + 32].unsqueeze(1).to_broadcast([P, MLA_HEADS, MLA_ROPE])
                                dve.tensor_copy(kk[:, t, :, MLA_NOPE:MLA_QK], pe_)
                        on_vector(c, assemble)
                        turn(c, lambda t, k: q[:, t, k * MLA_QK:(k + 1) * MLA_QK], qt_, MLA_HEADS, 2, MLA_QK, ident, split=False)
                        turn(c, lambda t, k: kk[:, t, k, :], kt_, MLA_HEADS, 2, MLA_QK, ident, split=False)
                    units = []
                    for hh in range(MLA_HEADS):
                        for t in range(2):
                            units.append(dict(q=[qt_[:, hh, t * P:(t + 1) * P]], keys=[kt_[:, hh, :]],
                                              v=[kv[:, j, hh * 128 + 64:hh * 128 + 128] for j in range(2)],
                                              out=o[:, t, hh * 64:hh * 64 + 64]))
                    attention(c, units, MLA_QK ** -0.5, ident)
                with ExitStack() as sm:
                    groups = []
                    for t in range(2):
                        v = h[:, t, O["dq"]:O["dq"] + 2048].rearrange("p (h d) -> p h d", d=DIFF_D)
                        groups.append((v[:, :, 0:8], v[:, :, 8:16], angles[:, t, 0, 16:24], angles[:, t, 1, 16:24]))
                    rotate(c, groups, 8)
                    lam = c.sb(sm, "lam", [P, 4, DIFF_D])
                    ld = c.sb(sm, "lam_dot", [P, 2])
                    neg = c.sb(sm, "neg_lambda", [P, 1])
                    sub = c.sb(sm, "subln", [P, 8 * 128])
                    load_all([(lam[:, :, :], A["diff_lambda_2"][l:l + 1].to_broadcast([P, 4, DIFF_D])),
                              (sub[:, :].rearrange("p (h d) -> p h d", d=128),
                               A["diff_subln_2"][l:l + 1].unsqueeze(1).to_broadcast([P, 8, 128]))])

                    def dots(dve, link):
                        lv = lam[:, :, :].rearrange("p (a b) d -> p a b d", b=2)
                        link(dve.tensor_tensor(lv[:, :, 0, :], lv[:, :, 0, :], lv[:, :, 1, :], ALU.mult))
                        link(dve.tensor_reduce(ld[:, :], lv[:, :, 0, :], AX, ALU.add))
                    on_vector(c, dots)
                    on_scalar(c, lambda act, link: act.activation(ld[:, :], ld[:, :], ACT.Exp))

                    def lam_full(dve, link):
                        link(dve.tensor_tensor(neg[:, :], ld[:, 1:2], ld[:, 0:1], ALU.subtract))
                        link(dve.tensor_scalar(neg[:, :], neg[:, :], -lam0, None, ALU.add))
                    on_vector(c, lam_full)
                    dt_ = c.sb(sm, "diff_t", [P, 16, TOK])
                    turn(c, lambda t, k: h[:, t, O["dq"] + k * P:O["dq"] + (k + 1) * P], dt_, 16, 2, P, ident, split=False)
                    units = []
                    for hh in range(DIFF_HEADS):
                        for t in range(2):
                            units.append(dict(q=[dt_[64 * m:64 * m + 64, hh, t * P:(t + 1) * P] for m in range(2)],
                                              keys=[dt_[64 * m:64 * m + 64, 8 + hh, :] for m in range(2)],
                                              v=[h[:, j, O["dv"] + hh * 128:O["dv"] + (hh + 1) * 128] for j in range(2)],
                                              out=o[:, t, 512 + hh * 128:512 + (hh + 1) * 128]))
                    attention(c, units, DIFF_D ** -0.5, ident, pair=neg[:, :])
                with ExitStack() as sm:
                    sub = c.sb(sm, "subln", [P, 8 * 128])
                    load_all([(sub[:, :].rearrange("p (h d) -> p h d", d=128),
                               A["diff_subln_2"][l:l + 1].unsqueeze(1).to_broadcast([P, 8, 128]))])
                    head_rms(c, o[:, :, 512:1536], 2, 8, 128, sub[:, :], 1e-5, extra=1.0 - lam0)
                with ExitStack() as sm:
                    mkv = c.sb(sm, "mem_kv", [P, 2, 1024])
                    with ExitStack() as sn:
                        mem = c.sb(sn, "mem", [P, 2, D])
                        load_all([(mem[:, :, :], A["mem_2"][0].rearrange("(t p) d -> p t d", p=P))])
                        mt = [c.sb(sn, "mem_hi", [P, KT, TOK], F32R), c.sb(sn, "mem_lo", [P, KT, TOK], F32R)]
                        turn(c, lambda t, k: mem[:, t, k * P:(k + 1) * P], mt, KT, 2, P, ident)
                        project(c, S["memkv"], lhs_of(mt), 2, into(mkv, 256))
                    mq = c.sb(sm, "mem_qt", [P, 4, TOK])
                    mk = c.sb(sm, "mem_kt", [P, 4, TOK])
                    turn(c, lambda t, k: h[:, t, O["mq"] + k * P:O["mq"] + (k + 1) * P], mq, 4, 2, P, ident, split=False)
                    turn(c, lambda t, k: mkv[:, t, k * P:(k + 1) * P], mk, 4, 2, P, ident, split=False)
                    units = []
                    for hh in range(MEM_HEADS):
                        for t in range(2):
                            units.append(dict(q=[mq[:, hh, t * P:(t + 1) * P]], keys=[mk[:, hh, :]],
                                              v=[mkv[:, j, 512 + hh * 128:512 + (hh + 1) * 128] for j in range(2)],
                                              out=o[:, t, 1536 + hh * 128:1536 + (hh + 1) * 128]))
                    attention(c, units, MEM_HD ** -0.5, ident)
            if stop == f"branches{l}":
                return
            sg_stack = ExitStack()
            merged_in = c.sb(sg_stack, "gates", [P, 2, 3 * D])
            project(c, S["gate"], lhs_of(xt), 2, into(merged_in, 256))
            with ExitStack() as sn:
                bg = c.sb(sn, "b_gate", [P, 3 * D])
                load_all([(bg[:, :], A["b_gate_2"][l:l + 1].rearrange("o a d -> o (a d)").to_broadcast([P, 3 * D]))])
                on_vector(c, lambda dve, link: [dve.tensor_tensor(merged_in[:, t, :], merged_in[:, t, :], bg[:, :], ALU.add)
                                                for t in range(2)])
            on_scalar(c, lambda act, link: act.activation(merged_in[:, :, :], merged_in[:, :, :], ACT.Sigmoid))
            with ExitStack() as sn:
                ot = [c.sb(sn, "o_hi", [P, 16, TOK], F32R), c.sb(sn, "o_lo", [P, 16, TOK], F32R)]
                turn(c, lambda t, k: o[:, t, k * P:(k + 1) * P], ot, 16, 2, P, ident)
                for br, key in enumerate(("b0", "b1", "b2")):
                    k0 = BRANCH_ROWS[br] // P
                    cw = 512 if br != 1 else 256

                    def gated(dve, n, v, br=br, cw=cw):
                        m = merged_in[:, :, br * D + n * cw:br * D + (n + 1) * cw]
                        return dve.tensor_tensor(m, v, m, ALU.mult)
                    project(c, S[key], [lambda n, k, a=a, k0=k0: a[:, k0 + k, :] for a in ot], 2, gated, on_act=False)

            def add_up(dve, link):
                m = merged_in
                link(dve.tensor_tensor(m[:, :, 0:D], m[:, :, 0:D], m[:, :, D:2 * D], ALU.add))
                link(dve.tensor_tensor(m[:, :, 0:D], m[:, :, 0:D], m[:, :, 2 * D:3 * D], ALU.add))
            on_vector(c, add_up)
            with ExitStack() as sn:
                mt = [c.sb(sn, "m_hi", [P, KT, TOK], F32R), c.sb(sn, "m_lo", [P, KT, TOK], F32R)]
                y = c.sb(sn, "y2", [P, 2, D])
                turn(c, lambda t, k: merged_in[:, t, k * P:(k + 1) * P], mt, KT, 2, P, ident)
                project(c, S["out"], lhs_of(mt), 2, into(y, 256))
                gb = c.sb(sn, "ln", [P, 2, D])
                load_all([(gb[:, 0, :], A["ln1_g_2"][l:l + 1].to_broadcast([P, D])),
                          (gb[:, 1, :], A["ln1_b_2"][l:l + 1].to_broadcast([P, D]))])
                layer_norm(c, x, y, gb[:, 0, :], gb[:, 1, :])
            sg_stack.close()
    if stop == f"attn2_{l}":
        return
    with ExitStack() as sn:
        xt = [c.sb(sn, "x2_hi", [P, KT, TOK], F32R), c.sb(sn, "x2_lo", [P, KT, TOK], F32R)]
        y = c.sb(sn, "y2", [P, 2, D])
        turn(c, lambda t, k: x[:, t, k * P:(k + 1) * P], xt, KT, 2, P, ident)
        relu_squared_mlp(c, A["mlp_w1_2"][l], A["mlp_w2_2"][l], xt, y)
        gb = c.sb(sn, "ln", [P, 2, D])
        load_all([(gb[:, 0, :], A["ln2_g_2"][l:l + 1].to_broadcast([P, D])),
                  (gb[:, 1, :], A["ln2_b_2"][l:l + 1].to_broadcast([P, D]))])
        layer_norm(c, x, y, gb[:, 0, :], gb[:, 1, :])


_INS = ["x", "c", "ctx", "c_ctx", "w_mod", "b_mod", "ffn1_w1", "ffn1_w3", "ffn1_w2", "w_in", "na_q_norm", "na_k_norm",
        "na_rpb", "gla_w_gate_f", "gla_b_gate_f", "gla_w_gate_b", "gla_b_gate_b", "gla_norm", "gqa_q_norm", "gqa_k_norm",
        "w_out", "ffn2_w1", "ffn2_w3", "ffn2_w2", "mem_2", "positions_2", "w_in_2", "b_gate_2", "mla_q_norm_2",
        "mla_kv_norm_2", "mla_w_uq_2", "mla_w_ukv_2", "diff_lambda_2", "diff_subln_2", "mem_w_kv_2", "w_branch_2",
        "w_out_2", "ln1_g_2", "ln1_b_2", "mlp_w1_2", "mlp_w2_2", "ln2_g_2", "ln2_b_2"]


def kernel(**inputs):
    import concourse.bacc as _bacc
    from concourse.bass_utils import run_bass_kernel_spmd as _run

    nc = _bacc.Bacc("TRN2", target_bir_lowering=False, num_devices=1)
    arrays, A = {}, {}
    given = {name: np.ascontiguousarray(inputs[name]) for name in _INS}
    given.update(shape_constants())
    for name, a in given.items():
        arrays[f"in_{name}_dram"] = a
        A[name] = nc.dram_tensor(f"in_{name}_dram", a.shape, mybir.dt.from_np(a.dtype), kind="ExternalInput").ap()
    out = nc.dram_tensor("out_0_dram", (1, TOK, D), F32, kind="ExternalOutput").ap()
    encoder_program(nc, A, out)
    r = _run(nc, [arrays], core_ids=[0])
    return r.results[0]["out_0_dram"]
```

```python
import math
from contextlib import ExitStack

import numpy as np

import concourse.bass as bass
from concourse import mybir

F32 = mybir.dt.float32
F32R = mybir.dt.float32r
I32 = mybir.dt.int32
ACT = mybir.ActivationFunctionType
ALU = mybir.AluOpType
AX = mybir.AxisListType.X

P = 128
D = 1024
KT = D // P
LAYERS = 2
TOK = 256
CHUNK = 2048
SLOTS = 3

D_FF = 2816
HD = 64
NA_HEADS = 4
GLA_HEADS = 4
GLA_DK = 32
GLA_LEVELS = 7
OFF = dict(fourier=0, na_q=256, na_k=512, na_v=768, gla_q=1024, gla_k=1152, gla_v=1280, gla_r=1536,
           gla_g=1792, gqa_q=1824, gqa_k=2080, gqa_v=2208)
D_IN = 2336
GRID_W = 64
NA_COLS = 16
RPB_ROWS, RPB_COLS = 15, 31
EPS = 1e-6

MLA_HEADS, MLA_NOPE, MLA_ROPE, MLA_V = 8, 64, 32, 64
MLA_QK = MLA_NOPE + MLA_ROPE
Q_LORA, KV_LORA = 384, 256
DIFF_HEADS, DIFF_D, DIFF_ROT = 8, 64, 16
MEM_HEADS, MEM_HD = 4, 128
OFF2 = dict(cq=0, ckv=384, kpe=640, dq=672, dk=1696, dv=2720, mq=3744, gate=4256)
N_IN = 7328
D_FF_2 = 4096
ALPHA = (2 * LAYERS) ** 0.25
LN_EPS = 1e-5
BRANCH_ROWS = (0, 512, 1536, 2048)


def shape_constants():
    t = np.arange(TOK)
    ang = 2 * np.pi * np.outer(t, t) / TOK
    dft_tok = np.concatenate([np.cos(ang), np.sin(ang)], 1) / math.sqrt(TOK)
    e = np.arange(HD)
    a2 = 2 * np.pi * np.outer(e, e) / HD
    eye2 = np.eye(2)
    dft_ch = np.stack([np.kron(eye2, np.cos(a2)), -np.kron(eye2, np.sin(a2))], 1) / math.sqrt(HD)

    c = np.arange(GRID_W)
    start = np.clip(c - NA_COLS // 2, 0, GRID_W - NA_COLS)
    seen = (c[None, :] >= start[:, None]) & (c[None, :] < start[:, None] + NA_COLS)
    na_mask = np.zeros((P, 2 * TOK))
    na_mask[:, :TOK] = np.where(np.tile(seen, (2, 4)), 0.0, -1e30)
    flip = np.zeros((P, P))
    for r in range(2):
        for i in range(GRID_W):
            flip[r * GRID_W + GRID_W - 1 - i, r * GRID_W + i] = math.sqrt(HD)

    i = np.arange(P)
    T_, I_ = i[:, None], i[None, :]
    dec = []
    for back in (False, True):
        for lv in range(GLA_LEVELS):
            s = 2 ** lv
            lo = (I_ // s) * s
            end = lo + s - 1
            late = (I_ // s) % 2 == 1
            if not back:
                m = np.where(late, (T_ >= lo) & (T_ <= I_), (T_ > I_) & (T_ <= end))
            else:
                m = np.where(late, (T_ >= lo) & (T_ < I_), (T_ >= I_) & (T_ <= end))
            dec.append(m)
    dec += [T_ <= I_, T_ > I_, T_ < I_, T_ >= I_, np.ones((P, P), bool)]
    dec = np.stack(dec, 1).astype(np.float64) / 16.0
    J_ = T_
    masks = np.stack([(J_ >> lv) == ((I_ >> lv) ^ 1) for lv in range(GLA_LEVELS)], 1).astype(np.int32)

    row, col = (t // GRID_W).astype(np.float32), (t % GRID_W).astype(np.float32)
    inv = np.float32(10000.0) ** (-np.arange(16, dtype=np.float32) / np.float32(16))
    an = np.concatenate([row[:, None] * inv, col[:, None] * inv], -1)
    rope = np.stack([np.cos(an), np.sin(an)], 1).reshape(2, P, 2, 32).transpose(1, 0, 2, 3)
    inv_m = np.float32(500000.0) ** (-np.arange(0, MLA_ROPE, 2, dtype=np.float32) / np.float32(MLA_ROPE))
    inv_d = np.float32(500000.0) ** (-np.arange(0, DIFF_ROT, 2, dtype=np.float32) / np.float32(DIFF_ROT))
    inv2 = np.tile(np.concatenate([inv_m, inv_d])[None], (P, 1))
    f = lambda a: np.ascontiguousarray(a, dtype=np.float32)
    return dict(k_dft_tok=f(dft_tok.reshape(2, P, 2 * TOK).transpose(1, 0, 2)), k_dft_ch=f(dft_ch),
                k_na_mask=f(na_mask), k_flip=f(flip), k_decay=f(dec), k_levels=np.ascontiguousarray(masks),
                k_rope=f(rope), k_inv=f(inv2), k_eye=f(np.eye(P)))


ROOT_GUESS = float(0x5F3759DF)
TAB = dict(le=14, gt=15, lt=16, ge=17, ones=18)


class Signal:

    def __init__(self, sem, unit=1):
        self.sem, self.unit, self.base = sem, unit, 0

    def at(self, n):
        return (self.base + n) * self.unit

    def passed(self, n):
        self.base += n


def loop(eng, first, last, body):
    if last - first == 1:
        body(first)
    elif last > first:
        with eng.Fori(first, last) as i:
            body(i)


def split_product(pe, out, a, b, first, last):
    pe.matmul(out, a[0], b[0], start=first, stop=False)
    pe.matmul(out, a[0], b[1], start=False, stop=False)
    return pe.matmul(out, a[1], b[0], start=False, stop=last)


class Core:

    def __init__(self, nc, ctx):
        self.nc, self.ctx = nc, ctx
        self.serial = 0
        self.ps = ctx.enter_context(nc.psum_tensor("psum", [P, 8, 512], F32))
        self.raw = ctx.enter_context(nc.sbuf_tensor("w_raw", [P, SLOTS, CHUNK], F32))
        self.w_hi = ctx.enter_context(nc.sbuf_tensor("w_hi", [P, SLOTS, CHUNK], F32R))
        self.w_lo = ctx.enter_context(nc.sbuf_tensor("w_lo", [P, SLOTS, CHUNK], F32R))
        self.loaded = [self.counter(f"w_loaded{s}", 16) for s in range(SLOTS)]
        self.hi_done = [self.counter(f"w_hi_done{s}") for s in range(SLOTS)]
        self.split = [self.counter(f"w_split{s}") for s in range(SLOTS)]
        self.pre = set()
        self.heads = []
        self.next_heads = 0
        self.counters = {}

    def counter(self, name, unit=1):
        return Signal(self.ctx.enter_context(self.nc.semaphore(name)), unit)

    def sig(self, name, unit=1):
        if name not in self.counters:
            self.counters[name] = self.counter(name, unit)
        return self.counters[name]

    def sb(self, stack, name, shape, dt=F32):
        self.serial += 1
        return stack.enter_context(self.nc.sbuf_tensor(f"{name}_{self.serial}", shape, dt))

    def ask(self, b, pairs):
        dma_in = self.sig("dma_in", 16)

        @b.sync
        def _(sp):
            with self.nc.allow_non_contiguous_dma(reason="small vectors"):
                for dst, src in pairs:
                    sp.dma_start(dst, src).then_inc(dma_in.sem, 16)
        dma_in.passed(len(pairs))

    def arrived(self):
        dma_in = self.sig("dma_in", 16)
        with block(self) as b:
            @b.sync
            def _(sp):
                sp.wait_ge(dma_in.sem, dma_in.at(0))

    def load(self, sp, slot, used, src):
        if not isinstance(used, int) or self.split[slot].base + used > 0:
            sp.wait_ge(self.split[slot].sem, self.split[slot].at(used))
        a, b = src.shape[1], src.shape[2]
        dst = self.raw[:, slot, 0:a * b].rearrange("p (a b) -> p a b", b=b)
        sp.dma_start(dst, src).then_inc(self.loaded[slot].sem, 16)

    def load_heads(self, sp, used):
        self.next_heads += 1
        if self.next_heads <= len(self.heads):
            for slot, src in self.heads[self.next_heads - 1]:
                self.load(sp, slot, used[slot], src)

    def hi(self, act, slot, u, n=CHUNK):
        if isinstance(u, int) and u == 0 and slot in self.pre:
            return
        act.wait_ge(self.loaded[slot].sem, self.loaded[slot].at(u + 1))
        act.activation(self.w_hi[:, slot, 0:n], self.raw[:, slot, 0:n], ACT.Copy).then_inc(self.hi_done[slot].sem, 1)

    def lo(self, dve, slot, u, n=CHUNK):
        if isinstance(u, int) and u == 0 and slot in self.pre:
            return
        dve.wait_ge(self.hi_done[slot].sem, self.hi_done[slot].at(u + 1))
        dve.tensor_tensor(self.w_lo[:, slot, 0:n], self.raw[:, slot, 0:n], self.w_hi[:, slot, 0:n].bitcast(F32),
                          ALU.subtract).then_inc(self.split[slot].sem, 1)

    def ready(self, pe, slot, u):
        pe.wait_ge(self.split[slot].sem, self.split[slot].at(u + 1))

    def w(self, slot, nk, cw):
        return [t[:, slot, 0:nk * cw].rearrange("p (k c) -> p k c", c=cw) for t in (self.w_hi, self.w_lo)]

    def weights_passed(self, used):
        for s in range(SLOTS):
            self.loaded[s].passed(used[s])
            self.hi_done[s].passed(used[s])
            self.split[s].passed(used[s])
        self.pre = set()

    def coming(self):
        if self.next_heads > len(self.heads):
            return []
        return [(slot, src.shape[1] * src.shape[2]) for slot, src in self.heads[self.next_heads - 1]]


def block(c):
    return c.nc.Block(no_gpsimd_drain=True)


def chunk_of(w2d, r0, nk, c0, cw):
    cols = w2d[r0:r0 + nk * P, c0:c0 + cw] if isinstance(c0, int) else w2d[r0:r0 + nk * P, bass.ds(c0, cw)]
    return cols.rearrange("(k p) n -> p k n", p=P)


def rows_of(w2d, i, nk):
    rows = w2d[i * nk * P:(i + 1) * nk * P, :] if isinstance(i, int) else w2d[bass.ds(i * (nk * P), nk * P), :]
    return rows.rearrange("(k p) n -> p k n", p=P)


class Chain:

    def __init__(self, eng, count):
        self.eng, self.count, self.n = eng, count, 0

    def __call__(self, ins):
        ins.then_inc(self.count.sem, 1)
        self.n += 1
        self.eng.wait_ge(self.count.sem, self.count.at(self.n))

    def close(self):
        self.count.passed(self.n)


def on_vector(c, steps):
    with block(c) as b:
        @b.vector
        def _(dve):
            link = Chain(dve, c.sig("dve_step"))
            steps(dve, link)
            link.close()


def on_scalar(c, steps):
    with block(c) as b:
        @b.scalar
        def _(act):
            link = Chain(act, c.sig("act_step"))
            steps(act, link)
            link.close()


def inverse_root_steps(c, dve, link, ss, scale, eps, r, t):
    link(dve.tensor_scalar(ss, ss, scale, eps, ALU.mult, ALU.add))
    link(dve.tensor_scalar(t.bitcast(I32), ss.bitcast(I32), 1, None, ALU.arith_shift_right))
    link(dve.tensor_scalar(r.bitcast(I32), t.bitcast(I32), -1.0, ROOT_GUESS, ALU.mult, ALU.add))
    for _ in range(3):
        link(dve.tensor_tensor(t, r, r, ALU.mult))
        link(dve.scalar_tensor_tensor(out=t, in0=t, scalar=-0.5, in1=ss, op0=ALU.mult, op1=ALU.mult))
        link(dve.scalar_tensor_tensor(out=r, in0=t, scalar=1.5, in1=r, op0=ALU.add, op1=ALU.mult))


def turn(c, src, dst, nk, ntt, w, eye, split=True, cols=None, side=None, norm=None, loads=()):
    nt = ntt * P
    banks = 4
    turned, moved, highs = c.sig("turned"), c.sig("turn_moved"), c.sig("turn_hi")
    lows, moved_dve = c.sig("turn_lo"), c.sig("turn_moved_dve")
    early = c.coming()[:1] if split and not c.pre else []
    with ExitStack() as st:
        tmp = c.sb(st, "turn_tmp", [P, 3, nt]) if split else None
        if norm is not None:
            scale_ready = c.sig("scale_ready")
            diag = c.sb(st, "diag", [P, ntt, P])
            r, tm = c.sb(st, "root", [P, ntt]), c.sb(st, "root_tmp", [P, ntt])
        with block(c) as b:
            c.ask(b, loads)

            @b.tensor
            def _(pe):
                if norm is not None:
                    pe.wait_ge(scale_ready.sem, scale_ready.at(ntt))
                for k in range(nk):
                    if k >= banks:
                        pe.wait_ge(moved.sem, moved.at(k - banks + 1))
                        if split:
                            pe.wait_ge(moved_dve.sem, moved_dve.at(k - banks + 1))
                    for t in range(ntt):
                        o = c.ps[0:w, k % banks, t * P:(t + 1) * P]
                        if norm is None:
                            last = pe.transpose(o, src(t, k), eye)
                        else:
                            last = pe.matmul(o, src(t, k), diag[:, t, :], start=True, stop=True)
                    last.then_inc(turned.sem, 1)

            def evacuate(eng, on_act, k, part):
                t0, t1, sc, sh = part
                o, i_ = tmp[0:w, k % 3, t0:t1], c.ps[0:w, k % banks, t0:t1]
                if on_act:
                    if sc is None:
                        return eng.activation(o, i_, ACT.Copy)
                    return eng.activation(o, i_, ACT.Identity, scale=sc, bias=0.0 if sh is None else sh)
                if sc is None:
                    return eng.tensor_copy(o, i_)
                if sh is None:
                    return eng.tensor_scalar(o, i_, sc, None, ALU.mult)
                return eng.tensor_scalar(o, i_, sc, sh, ALU.mult, ALU.add)

            def halves(k):
                p_ = cols(k) if cols else [(0, nt, None, None)]
                if len(p_) == 1:
                    t0, t1, sc, sh = p_[0]
                    p_ = [(0, nt // 2, sc, sh), (nt // 2, nt, sc, sh)]
                return p_

            if not split:
                @b.scalar
                def _(act):
                    for k in range(nk):
                        act.wait_ge(turned.sem, turned.at(k + 1))
                        act.activation(dst[0:w, k, :], c.ps[0:w, k % banks, 0:nt], ACT.Copy,
                                       scale=side(k) if side else 1.0).then_inc(moved.sem, 1)
            else:
                @b.scalar
                def _(act):
                    def move(k):
                        act.wait_ge(turned.sem, turned.at(k + 1))
                        if k >= 3:
                            act.wait_ge(lows.sem, lows.at(k - 2))
                        evacuate(act, True, k, halves(k)[0]).then_inc(moved.sem, 1)

                    for slot, size in early:
                        c.hi(act, slot, 0, size)
                    move(0)
                    for k in range(nk):
                        if k + 1 < nk:
                            move(k + 1)
                        act.wait_ge(moved_dve.sem, moved_dve.at(k + 1))
                        act.wait_ge(moved.sem, moved.at(k + 1))
                        act.activation(dst[0][0:w, k, :], tmp[0:w, k % 3, :], ACT.Copy).then_inc(highs.sem, 1)

                @b.vector
                def _(dve):
                    def move(k):
                        dve.wait_ge(moved.sem, moved.at(k + 1))
                        if k >= 3:
                            dve.wait_ge(lows.sem, lows.at(k - 2))
                        evacuate(dve, False, k, halves(k)[1]).then_inc(moved_dve.sem, 1)

                    if norm is not None:
                        link = Chain(dve, c.sig("dve_step"))
                        inverse_root_steps(c, dve, link, norm[:, 0:ntt], 1.0 / D, EPS, r[:, :], tm[:, :])
                        for t in range(ntt):
                            dve.tensor_scalar(diag[:, t, :], eye, r[:, t:t + 1], None, ALU.mult).then_inc(scale_ready.sem, 1)
                        link.close()
                    move(0)
                    for k in range(nk):
                        if k + 1 < nk:
                            move(k + 1)
                        dve.wait_ge(highs.sem, highs.at(k + 1))
                        dve.tensor_tensor(dst[1][0:w, k, :], tmp[0:w, k % 3, :], dst[0][0:w, k, :].bitcast(F32),
                                          ALU.subtract).then_inc(lows.sem, 1)

                if early:
                    @b.gpsimd
                    def _(pool):
                        for slot, size in early:
                            c.lo(pool, slot, 0, size)
                            pool.wait_ge(c.split[slot].sem, c.split[slot].at(1))
    turned.passed(nk)
    moved.passed(nk)
    if norm is not None:
        scale_ready.passed(ntt)
    if split:
        moved_dve.passed(nk)
        highs.passed(nk)
        lows.passed(nk)
        c.pre |= {slot for slot, _ in early}


def chunks_of(w2d, r0, nk, col0, ncols):
    cw = min(CHUNK // nk, 512)
    out, at = [], 0
    while at < ncols:
        out.append((w2d, r0, nk, col0 + at, min(cw, ncols - at)))
        at += cw
    return out


def project_heads(chunks):
    return [(n, chunk_of(*chunks[n])) for n in range(min(SLOTS, len(chunks)))]


def project(c, chunks, lhs, ntt, evac, on_act=True, act_then=None, pool_then=None):
    n_all = len(chunks)
    nk, cw = chunks[0][2], chunks[0][4]
    full = n_all if chunks[-1][4] == cw else n_all - 1
    per_bank = 512 // cw
    banks = (ntt + per_bank - 1) // per_bank
    out_ready, out_read, pool_done = c.sig("proj_ready"), c.sig("proj_read"), c.sig("pool_done")
    used = [len(range(s, n_all, SLOTS)) for s in range(SLOTS)]
    n0 = (used[0] - 1) * SLOTS
    early_at = None if n0 == n_all - 1 else n0 if n0 == n_all - 2 else n0 + 1

    def view(slot, width):
        v = c.ps[:, 2 * slot:2 * slot + banks, :].rearrange("p b (t n) -> p (b t) n", n=cw)
        return v[:, 0:ntt, 0:width]

    def width(n):
        return chunks[n][4] if isinstance(n, int) else cw

    turns = max(0, (full - 1) // SLOTS) if full == n_all else max(0, (full - 1) // SLOTS)

    with block(c) as b:
        @b.sync
        def _(sp):
            whole = max(0, full // SLOTS)

            def three(i):
                for j in range(SLOTS):
                    w2d, r0, k_, c0, _ = chunks[0]
                    c.load(sp, j, i, chunk_of(w2d, r0, k_, c0 + (i * SLOTS + j) * cw, cw))

            regular = all(ch[:3] == chunks[0][:3] for ch in chunks) if n_all > 2 * SLOTS else False
            if regular:
                loop(sp, 1, whole, three)
                rest = range(max(1, whole) * SLOTS, n_all)
            else:
                rest = range(SLOTS, n_all)
            for n in rest:
                c.load(sp, n % SLOTS, n // SLOTS, chunk_of(*chunks[n]))
            c.load_heads(sp, used)

        @b.scalar
        def _(act):
            def high(n, i, j, wd):
                if not isinstance(n, int) or n >= SLOTS:
                    act.wait_ge(out_ready.sem, out_ready.at(n - SLOTS + 1))
                c.hi(act, j, i, nk * wd)

            def one(n, i, j, ahead):
                if ahead:
                    jn = (j + 1) % SLOTS
                    high(n + 1, i + (j + 1) // SLOTS, jn, width(n + 1))
                if on_act:
                    act.wait_ge(out_ready.sem, out_ready.at(n + 1))
                    evac(act, n, view(j, width(n))).then_inc(out_read.sem, 1)
                if act_then:
                    act.wait_ge(out_read.sem, out_read.at(n + 1))
                    act_then(act, n)
                if isinstance(n, int) and n == early_at:
                    for slot, size in c.coming()[:1]:
                        act.wait_ge(out_ready.sem, out_ready.at(n0 + 1))
                        c.hi(act, slot, used[0], size)

            high(0, 0, 0, width(0))
            for n in range(min(SLOTS, n_all)):
                one(n, 0, n, n + 1 < n_all)
            loop(act, 1, turns, lambda i: [one(i * SLOTS + j, i, j, True) for j in range(SLOTS)])
            for n in range(max(1, turns) * SLOTS, n_all):
                one(n, n // SLOTS, n % SLOTS, n + 1 < n_all)

        if pool_then:
            @b.gpsimd
            def _(pool):
                for n in range(n_all):
                    pool.wait_ge(out_read.sem, out_read.at(n + 1))
                    pool_then(pool, n).then_inc(pool_done.sem, 1)
                pool.wait_ge(pool_done.sem, pool_done.at(n_all))

        @b.vector
        def _(dve):
            def one(n, i, j, ahead):
                if ahead:
                    c.lo(dve, (j + 1) % SLOTS, i + (j + 1) // SLOTS, nk * width(n + 1))
                if not on_act:
                    dve.wait_ge(out_ready.sem, out_ready.at(n + 1))
                    evac(dve, n, view(j, width(n))).then_inc(out_read.sem, 1)
                if isinstance(n, int) and n == early_at:
                    for slot, size in c.coming()[:1]:
                        c.lo(dve, slot, used[0], size)

            c.lo(dve, 0, 0, nk * width(0))
            for n in range(min(SLOTS, n_all)):
                one(n, 0, n, n + 1 < n_all)
            loop(dve, 1, turns, lambda i: [one(i * SLOTS + j, i, j, True) for j in range(SLOTS)])
            for n in range(max(1, turns) * SLOTS, n_all):
                one(n, n // SLOTS, n % SLOTS, n + 1 < n_all)

        @b.tensor
        def _(pe):
            def one(n, i, j):
                wd = width(n)
                c.ready(pe, j, i)
                if not isinstance(n, int) or n >= SLOTS:
                    pe.wait_ge(out_read.sem, out_read.at(n - SLOTS + 1))
                w = c.w(j, nk, wd)
                v = view(j, wd)
                for t in range(ntt):
                    for k in range(nk):
                        last = split_product(pe, v[:, t, :], [a(n, k)[:, t * P:(t + 1) * P] for a in lhs],
                                             [x[:, k, :] for x in w], k == 0, k == nk - 1)
                last.then_inc(out_ready.sem, 1)

            for n in range(min(SLOTS, n_all)):
                one(n, 0, n)
            loop(pe, 1, turns, lambda i: [one(i * SLOTS + j, i, j) for j in range(SLOTS)])
            for n in range(max(1, turns) * SLOTS, n_all):
                one(n, n // SLOTS, n % SLOTS)
    out_ready.passed(n_all)
    out_read.passed(n_all)
    if pool_then:
        pool_done.passed(n_all)
    c.weights_passed(used)
    if early_at is not None:
        c.pre = {slot for slot, _ in c.coming()[:1]}


def lhs_of(pair):
    return [lambda n, k, a=a: a[:, k, :] for a in pair]


def into(dst, cw):
    def evac(eng, n, v):
        wd = v.shape[2]
        cols = slice(n * cw, n * cw + wd) if isinstance(n, int) else bass.ds(n * cw, cw)
        return eng.activation(dst[:, :, cols], v, ACT.Copy)
    return evac


def ffn_heads(w1, w3, w2):
    return [(0, chunk_of(w1, 0, KT, 0, 2 * P)), (2, chunk_of(w3, 0, KT, 0, 2 * P)), (1, rows_of(w2, 0, 2))]


def swiglu(c, w1, w3, w2, xt, ntt, y, x, mod, j, eye, ss):
    spread, rows_moved = c.sig("gate_spread"), c.sig("gate_rows_moved")
    scaled, last_scaled, added = c.sig("gated_rows"), c.sig("last_gated"), c.sig("rows_added")
    nv, last_t = ntt // 2, ntt - 1
    nt = ntt * P
    n = D_FF // (2 * P)
    h1_ready, h3_ready, silu_ready = c.sig("h1_ready"), c.sig("h3_ready"), c.sig("silu_ready")
    g_ready, ghi_ready, glo_ready = c.sig("g_ready"), c.sig("ghi_ready"), c.sig("glo_ready")
    y_ready, y_added, y_clear = c.sig("y_ready"), c.sig("y_added"), c.sig("y_clear")
    ny = 2 * ntt
    with ExitStack() as st:
        s1 = c.sb(st, "silu", [P, 2, nt])
        g = c.sb(st, "gated", [P, 2, nt])
        gh = c.sb(st, "gated_hi", [P, 2, nt], F32R)
        gl = c.sb(st, "gated_lo", [P, 2, nt], F32R)
        gate_rows = c.sb(st, "gate_rows", [P, nv, D])
        with block(c) as b:
            @b.gpsimd
            def _(pool):
                pool.memset(y[:, 0:ntt, :], 0.0).then_inc(y_clear.sem, 1)
                pool.wait_ge(rows_moved.sem, rows_moved.at(nv))
                for t in range(last_t):
                    pool.wait_ge(y_added.sem, y_added.at((n - 1) * ny + 2 * t + 2))
                    pool.tensor_tensor(y[:, t, :], y[:, t, :], gate_rows[:, t // 2, :], ALU.mult).then_inc(scaled.sem, 1)

            @b.sync
            def _(sp):
                up = lambda w, i: chunk_of(w, 0, KT, i * (2 * P), 2 * P)
                c.load(sp, 0, 1, up(w1, 1))
                c.load(sp, 2, 1, up(w3, 1))
                c.load(sp, 0, 2, up(w1, 2))

                def body(i):
                    c.load(sp, 1, i, rows_of(w2, i, 2))
                    c.load(sp, 2, i + 1, up(w3, i + 1))
                    c.load(sp, 0, i + 2, up(w1, i + 2))
                loop(sp, 1, n - 2, body)
                c.load(sp, 1, n - 2, rows_of(w2, n - 2, 2))
                c.load(sp, 2, n - 1, up(w3, n - 1))
                c.load(sp, 1, n - 1, rows_of(w2, n - 1, 2))
                c.load_heads(sp, [n, n, n])

            @b.tensor
            def _(pe):
                def up(i, slot, bank, ready, held, per):
                    c.ready(pe, slot, i)
                    w = c.w(slot, KT, 2 * P)
                    for f in range(2):
                        if not isinstance(i, int) or i > 0:
                            pe.wait_ge(held.sem, held.at((i - 1) * 2 + f + 1))
                        for k in range(KT):
                            last = split_product(pe, c.ps[:, bank + f, 0:nt], [x[:, k, f * P:(f + 1) * P] for x in w],
                                                 [x[:, k, :] for x in xt], k == 0, k == KT - 1)
                        last.then_inc(ready.sem, 1)

                def down(i):
                    c.ready(pe, 1, i)
                    w = c.w(1, 2, D)
                    pe.wait_ge(glo_ready.sem, glo_ready.at((i + 1) * 2))
                    for m in range(ny):
                        t, half = m // 2, m % 2
                        if not (isinstance(i, int) and i * ny + m < 4):
                            pe.wait_ge(y_added.sem, y_added.at(i * ny + (m - 3)))
                        for f in range(2):
                            last = split_product(pe, c.ps[:, 4 + m % 4, :], [x[:, f, t * P:(t + 1) * P] for x in (gh, gl)],
                                                 [x[:, f, half * 512:(half + 1) * 512] for x in w], f == 0, f == 1)
                        last.then_inc(y_ready.sem, 1)

                def body(i):
                    up(i, 0, 0, h1_ready, silu_ready, 2)
                    down(i - 1)
                    up(i, 2, 2, h3_ready, g_ready, 2)
                up(0, 0, 0, h1_ready, silu_ready, 2)
                up(0, 2, 2, h3_ready, g_ready, 2)
                body(1)
                loop(pe, 2, n, body)
                pe.wait_ge(g_ready.sem, g_ready.at(2 * n))
                for v in range(nv):
                    for k in range(KT):
                        col = mod[:, j * KT + k, v:v + 1].to_broadcast([P, P])
                        last = pe.matmul(c.ps[:, 2 * v + k // 4, (k % 4) * P:(k % 4 + 1) * P], col, eye, start=True, stop=True)
                    last.then_inc(spread.sem, 1)
                down(n - 1)

            @b.scalar
            def _(act):
                def gate_hi(i):
                    if not isinstance(i, int) or i > 0:
                        act.wait_ge(y_ready.sem, y_ready.at(i * ny))
                    for f in range(2):
                        act.wait_ge(g_ready.sem, g_ready.at(i * 2 + f + 1))
                        act.activation(gh[:, f, :], g[:, f, :], ACT.Copy).then_inc(ghi_ready.sem, 1)

                def silu(i):
                    for f in range(2):
                        act.wait_ge(h1_ready.sem, h1_ready.at(i * 2 + f + 1))
                        if not isinstance(i, int) or i > 0:
                            act.wait_ge(g_ready.sem, g_ready.at((i - 1) * 2 + f + 1))
                        act.activation(s1[:, f, :], c.ps[:, f, 0:nt], ACT.Silu).then_inc(silu_ready.sem, 1)

                def w3_hi(i):
                    if not isinstance(i, int) or i > 0:
                        act.wait_ge(h3_ready.sem, h3_ready.at(i * 2))
                    c.hi(act, 2, i)

                def w1_hi(i):
                    if not isinstance(i, int) or i > 0:
                        act.wait_ge(h1_ready.sem, h1_ready.at(i * 2))
                    c.hi(act, 0, i)

                def w2_hi(i):
                    c.hi(act, 1, i)

                def body(i):
                    gate_hi(i - 1)
                    w2_hi(i - 1)
                    w3_hi(i)
                    silu(i)
                    w1_hi(i + 1)
                w1_hi(0)
                w3_hi(0)
                silu(0)
                w1_hi(1)
                body(1)
                loop(act, 2, n - 1, body)
                gate_hi(n - 2)
                w2_hi(n - 2)
                w3_hi(n - 1)
                silu(n - 1)
                act.wait_ge(y_ready.sem, y_ready.at((n - 1) * ny))
                w2_hi(n - 1)
                gate_hi(n - 1)
                for v in range(nv):
                    act.wait_ge(spread.sem, spread.at(v + 1))
                    act.activation(gate_rows[:, v, :], c.ps[:, 2 * v:2 * v + 2, :].rearrange("p b n -> p (b n)"),
                                   ACT.Copy).then_inc(rows_moved.sem, 1)
                for t in range(ntt):
                    act.wait_ge(added.sem, added.at(t + 1))
                    act.activation(y[:, t, :], x[:, t, :], ACT.Square, accum_out=ss[:, t:t + 1])

            @b.vector
            def _(dve):
                def gate(i):
                    for f in range(2):
                        dve.wait_ge(h3_ready.sem, h3_ready.at(i * 2 + f + 1))
                        dve.wait_ge(silu_ready.sem, silu_ready.at(i * 2 + f + 1))
                        if not isinstance(i, int) or i > 0:
                            dve.wait_ge(glo_ready.sem, glo_ready.at((i - 1) * 2 + f + 1))
                        dve.tensor_tensor(g[:, f, :], s1[:, f, :], c.ps[:, 2 + f, 0:nt], ALU.mult).then_inc(g_ready.sem, 1)
                    for f in range(2):
                        dve.wait_ge(ghi_ready.sem, ghi_ready.at(i * 2 + f + 1))
                        dve.tensor_tensor(gl[:, f, :], g[:, f, :], gh[:, f, :].bitcast(F32),
                                          ALU.subtract).then_inc(glo_ready.sem, 1)

                def join(t):
                    dve.tensor_tensor(x[:, t, :], x[:, t, :], y[:, t, :], ALU.add).then_inc(added.sem, 1)

                def add(i, last=False):
                    for m in range(ny):
                        t, half = m // 2, m % 2
                        dve.wait_ge(y_ready.sem, y_ready.at(i * ny + m + 1))
                        if not isinstance(i, int) or i > 0:
                            dve.wait_ge(y_added.sem, y_added.at((i - 1) * ny + m + 1))
                        yv = y[:, t, half * 512:(half + 1) * 512]
                        dve.tensor_tensor(yv, c.ps[:, 4 + m % 4, :], yv, ALU.add).then_inc(y_added.sem, 1)
                        if last and half == 1 and t >= 1:
                            dve.wait_ge(scaled.sem, scaled.at(t))
                            join(t - 1)

                def body(i):
                    gate(i - 1)
                    c.lo(dve, 1, i - 1)
                    c.lo(dve, 2, i)
                    c.lo(dve, 0, i + 1)
                    add(i - 1)
                c.lo(dve, 0, 0)
                c.lo(dve, 2, 0)
                c.lo(dve, 0, 1)
                dve.wait_ge(y_clear.sem, y_clear.at(1))
                gate(0)
                c.lo(dve, 1, 0)
                c.lo(dve, 2, 1)
                c.lo(dve, 0, 2)
                add(0)
                loop(dve, 2, n - 1, body)
                gate(n - 2)
                c.lo(dve, 1, n - 2)
                c.lo(dve, 2, n - 1)
                add(n - 2)
                c.lo(dve, 1, n - 1)
                gate(n - 1)
                add(n - 1, last=True)
                dve.wait_ge(rows_moved.sem, rows_moved.at(nv))
                dve.wait_ge(y_added.sem, y_added.at(n * ny))
                dve.tensor_tensor(y[:, last_t, :], y[:, last_t, :], gate_rows[:, nv - 1, :], ALU.mult).then_inc(last_scaled.sem, 1)
                dve.wait_ge(last_scaled.sem, last_scaled.at(1))
                join(last_t)
    for s in (h1_ready, h3_ready, silu_ready, g_ready, ghi_ready, glo_ready):
        s.passed(2 * n)
    y_ready.passed(ny * n)
    y_added.passed(ny * n)
    for s, m in ((spread, nv), (rows_moved, nv), (scaled, last_t), (last_scaled, 1), (added, ntt)):
        s.passed(m)
    y_clear.passed(1)
    c.weights_passed([n, n, n])


def mlp_heads(w1, w2):
    return [(0, chunk_of(w1, 0, KT, 0, 2 * P)), (2, chunk_of(w1, 0, KT, 2 * P, 2 * P)), (1, rows_of(w2, 0, 2))]


def relu_squared_mlp(c, w1, w2, xt, y):
    ntt, nt = 2, 2 * P
    n = D_FF_2 // (2 * P)
    h_ready, relu_ready, g_ready = c.sig("h1_ready"), c.sig("silu_ready"), c.sig("g_ready")
    ghi_ready, glo_ready = c.sig("ghi_ready"), c.sig("glo_ready")
    y_ready, y_added, y_clear = c.sig("y_ready"), c.sig("y_added"), c.sig("y_clear")
    ny = 2 * ntt
    turns = n // 2
    with ExitStack() as st:
        s1 = c.sb(st, "relu", [P, 2, 2, nt])
        g = c.sb(st, "squared", [P, 2, 2, nt])
        gh = c.sb(st, "squared_hi", [P, 2, 2, nt], F32R)
        gl = c.sb(st, "squared_lo", [P, 2, 2, nt], F32R)
        slot_of = (0, 2)
        used = [turns + 1, n - 1, turns]
        later = lambda q, m: not isinstance(q, int) or q >= m
        with block(c) as b:
            @b.gpsimd
            def _(pool):
                pool.memset(y[:, 0:ntt, :], 0.0).then_inc(y_clear.sem, 1)

            @b.sync
            def _(sp):
                up = lambda i, a: chunk_of(w1, 0, KT, i * (4 * P) + a * 2 * P, 2 * P)

                def body(i):
                    c.load(sp, 1, 2 * i - 1, rows_of(w2, 2 * i - 1, 2))
                    c.load(sp, 0, i + 1, up(i + 1, 0))
                    c.load(sp, 1, 2 * i, rows_of(w2, 2 * i, 2))
                    c.load(sp, 2, i + 1, up(i + 1, 1))
                c.load(sp, 0, 1, up(1, 0))
                c.load(sp, 2, 1, up(1, 1))
                loop(sp, 1, turns - 1, body)
                for q in range(n - 3, n - 1):
                    c.load(sp, 1, q, rows_of(w2, q, 2))
                c.load(sp, 0, turns, rows_of(w2, n - 1, 2))
                c.load_heads(sp, used)

            @b.tensor
            def _(pe):
                def up(h, i, a):
                    c.ready(pe, slot_of[a], i)
                    w = c.w(slot_of[a], KT, 2 * P)
                    if later(h, 2):
                        pe.wait_ge(relu_ready.sem, relu_ready.at(h - 1))
                    for f in range(2):
                        for k in range(KT):
                            last = split_product(pe, c.ps[:, a, f * nt:(f + 1) * nt], [x[:, k, f * P:(f + 1) * P] for x in w],
                                                 [x[:, k, :] for x in xt], k == 0, k == KT - 1)
                    last.then_inc(h_ready.sem, 1)

                def down(q, a, slot=1, u=None):
                    c.ready(pe, slot, q if u is None else u)
                    pe.wait_ge(glo_ready.sem, glo_ready.at(q + 1))
                    w = c.w(slot, 2, D)
                    for m in range(ny):
                        t, half = m // 2, m % 2
                        if later(q, 1):
                            pe.wait_ge(y_added.sem, y_added.at((q - 1) * ny + m + 1))
                        for f in range(2):
                            last = split_product(pe, c.ps[:, 4 + m, :], [x[:, a, f, t * P:(t + 1) * P] for x in (gh, gl)],
                                                 [x[:, f, half * 512:(half + 1) * 512] for x in w], f == 0, f == 1)
                        last.then_inc(y_ready.sem, 1)

                def body(i):
                    for a in range(2):
                        up(2 * i + a, i, a)
                        if later(2 * i + a, 1):
                            down(2 * i + (a - 1), 1 - a)
                body(0)
                body(1)
                loop(pe, 2, turns, body)
                down(n - 1, 1, 0, turns)

            @b.scalar
            def _(act):
                def w1_hi(h, i, a):
                    if later(h, 2):
                        act.wait_ge(h_ready.sem, h_ready.at(h - 1))
                    c.hi(act, slot_of[a], i)

                def w2_hi(q):
                    if later(q, 1):
                        act.wait_ge(y_ready.sem, y_ready.at(q * ny))
                    c.hi(act, 1, q)

                def relu(h, a):
                    act.wait_ge(h_ready.sem, h_ready.at(h + 1))
                    if later(h, 2):
                        act.wait_ge(g_ready.sem, g_ready.at(h - 1))
                    act.activation(s1[:, a, :, :].rearrange("p f n -> p (f n)"), c.ps[:, a, :], ACT.Relu).then_inc(relu_ready.sem, 1)

                def g_hi(h, a):
                    act.wait_ge(g_ready.sem, g_ready.at(h + 1))
                    if later(h, 2):
                        act.wait_ge(y_ready.sem, y_ready.at((h - 1) * ny))
                    act.activation(gh[:, a, :, :], g[:, a, :, :], ACT.Copy).then_inc(ghi_ready.sem, 1)

                def body(i, last=False):
                    for a in range(2):
                        h = 2 * i + a
                        if later(h, 1):
                            w2_hi(2 * i + (a - 1))
                        if not (last and a == 1):
                            w1_hi(2 * i + (a + 1), i + a, 1 - a)
                        else:
                            act.wait_ge(h_ready.sem, h_ready.at(n - 1))
                            c.hi(act, 0, turns)
                        relu(h, a)
                        g_hi(h, a)
                w1_hi(0, 0, 0)
                body(0)
                body(1)
                loop(act, 2, turns - 1, body)
                body(turns - 1, True)

            @b.vector
            def _(dve):
                def gate(h, a):
                    dve.wait_ge(relu_ready.sem, relu_ready.at(h + 1))
                    if later(h, 2):
                        dve.wait_ge(glo_ready.sem, glo_ready.at(h - 1))
                    dve.tensor_tensor(g[:, a, :, :], s1[:, a, :, :], s1[:, a, :, :], ALU.mult).then_inc(g_ready.sem, 1)
                    dve.wait_ge(ghi_ready.sem, ghi_ready.at(h + 1))
                    dve.tensor_tensor(gl[:, a, :, :], g[:, a, :, :], gh[:, a, :, :].bitcast(F32),
                                      ALU.subtract).then_inc(glo_ready.sem, 1)

                def add(q):
                    for m in range(ny):
                        t, half = m // 2, m % 2
                        dve.wait_ge(y_ready.sem, y_ready.at(q * ny + m + 1))
                        if later(q, 1):
                            dve.wait_ge(y_added.sem, y_added.at((q - 1) * ny + m + 1))
                        yv = y[:, t, half * 512:(half + 1) * 512]
                        dve.tensor_tensor(yv, c.ps[:, 4 + m, :], yv, ALU.add).then_inc(y_added.sem, 1)

                def body(i, last=False):
                    for a in range(2):
                        h = 2 * i + a
                        if later(h, 1):
                            c.lo(dve, 1, 2 * i + (a - 1))
                        if not (last and a == 1):
                            c.lo(dve, slot_of[1 - a], i + a)
                        else:
                            c.lo(dve, 0, turns)
                        gate(h, a)
                        if later(h, 1):
                            add(2 * i + (a - 1))
                c.lo(dve, 0, 0)
                dve.wait_ge(y_clear.sem, y_clear.at(1))
                body(0)
                body(1)
                loop(dve, 2, turns - 1, body)
                body(turns - 1, True)
                add(n - 1)
    for s in (h_ready, relu_ready, g_ready, ghi_ready, glo_ready):
        s.passed(n)
    y_ready.passed(ny * n)
    y_added.passed(ny * n)
    y_clear.passed(1)
    c.weights_passed(used)


def modulation_heads(w):
    return [(j, chunk_of(w, 0, KT, j * 2 * P, 2 * P)) for j in range(SLOTS)]


def modulation(c, w, silu4, bias_t, mod, comb, rows_in=None):
    n = w.shape[1] // (2 * P)
    turns = n // SLOTS
    row_ready, row_moved = c.sig("mod_row_ready"), c.sig("mod_row_moved")
    col_ready, col_moved = c.sig("mod_col_ready"), c.sig("mod_col_moved")
    with ExitStack() as st:
        rows = c.sb(st, "mod_rows", [4, SLOTS, 2 * P])
        squares = c.sb(st, "squares", [P, 4, D]) if rows_in else None
        with block(c) as b:
            @b.sync
            def _(sp):
                loop(sp, 1, turns, lambda i: [c.load(sp, j, i, chunk_of(w, 0, KT, i * (SLOTS * 2 * P) + j * 2 * P, 2 * P))
                                              for j in range(SLOTS)])
                c.load_heads(sp, [turns] * SLOTS)

            @b.scalar
            def _(act):
                def body(i, last=False):
                    for j in range(SLOTS):
                        q = i * SLOTS + j
                        if not (last and j == SLOTS - 1):
                            if not isinstance(i, int) or q >= 2:
                                act.wait_ge(row_ready.sem, row_ready.at(q - 1))
                            c.hi(act, (j + 1) % SLOTS, i + (j + 1) // SLOTS)
                        act.wait_ge(row_ready.sem, row_ready.at(q + 1))
                        if not isinstance(i, int) or q >= SLOTS:
                            act.wait_ge(col_ready.sem, col_ready.at(q - SLOTS + 1))
                        act.activation(rows[:, j, :], c.ps[0:4, j, 0:2 * P], ACT.Copy).then_inc(row_moved.sem, 1)
                c.hi(act, 0, 0)
                body(0)
                if rows_in:
                    x, ss, dma_in = rows_in
                    act.wait_ge(dma_in.sem, dma_in.at(0))
                    for t in range(4):
                        act.activation(squares[:, t, :], x[:, t, :], ACT.Square, accum_out=ss[:, t:t + 1])
                loop(act, 1, turns - 1, body)
                body(turns - 1, True)

            @b.vector
            def _(dve):
                def add(q, i, jb):
                    dve.wait_ge(col_ready.sem, col_ready.at(q + 1))
                    o = mod[:, 2 * q:2 * q + 2, :] if isinstance(i, int) else mod[:, bass.ds(q * 2, 2), :]
                    bt = bias_t[:, 2 * q:2 * q + 2] if isinstance(i, int) else bias_t[:, bass.ds(q * 2, 2)]
                    dve.tensor_tensor(o, c.ps[:, 3 + jb, 0:4].rearrange("p (f v) -> p f v", v=2),
                                      bt.unsqueeze(2).to_broadcast([P, 2, 2]), ALU.add).then_inc(col_moved.sem, 1)

                def body(i, last=False):
                    for j in range(SLOTS):
                        q = i * SLOTS + j
                        if not (last and j == SLOTS - 1):
                            c.lo(dve, (j + 1) % SLOTS, i + (j + 1) // SLOTS)
                        if not isinstance(i, int) or q >= 1:
                            add(q - 1, i, (j - 1) % SLOTS)
                c.lo(dve, 0, 0)
                body(0)
                loop(dve, 1, turns - 1, body)
                body(turns - 1, True)
                add(n - 1, 0, SLOTS - 1)

            @b.tensor
            def _(pe):
                def cols(q, i, jb):
                    pe.wait_ge(row_moved.sem, row_moved.at(q + 1))
                    if not isinstance(i, int) or q >= SLOTS:
                        pe.wait_ge(col_moved.sem, col_moved.at(q - SLOTS + 1))
                    for f in range(2):
                        last = pe.matmul(c.ps[:, 3 + jb, 2 * f:2 * f + 2], rows[:, jb, f * P:(f + 1) * P], comb,
                                         start=True, stop=True)
                    last.then_inc(col_ready.sem, 1)

                def body(i):
                    for j in range(SLOTS):
                        q = i * SLOTS + j
                        c.ready(pe, j, i)
                        if not isinstance(i, int) or q >= SLOTS:
                            pe.wait_ge(row_moved.sem, row_moved.at(q - SLOTS + 1))
                        wv = c.w(j, KT, 2 * P)
                        for h in range(2):
                            for k in range(KT):
                                last = pe.matmul(c.ps[0:4, j, 0:2 * P], silu4[:, k, :], wv[h][:, k, :],
                                                 start=(h + k == 0), stop=(h == 1 and k == KT - 1))
                        last.then_inc(row_ready.sem, 1)
                        if not isinstance(i, int) or q >= 1:
                            cols(q - 1, i if not isinstance(i, int) else 0, (j - 1) % SLOTS)
                body(0)
                body(1)
                loop(pe, 2, turns, body)
                cols(n - 1, 0, SLOTS - 1)
    for s in (row_ready, row_moved, col_ready, col_moved):
        s.passed(n)
    c.weights_passed([turns] * SLOTS)
    m = mod[:, :, :].rearrange("p (j k) v -> p j (k v)", k=KT)

    def finish(dve, link):
        for j in (1, 4, 7):
            link(dve.tensor_scalar(m[:, j, :], m[:, j, :], 1.0, None, ALU.add))
        for j in (2, 8):
            link(dve.tensor_scalar(m[:, j, :], m[:, j, :], 0.5, None, ALU.mult))
    on_vector(c, finish)


def residual(c, x, y, ntt, mod, j, eye, ss):
    spread, scaled, added = c.sig("gate_spread"), c.sig("gated_rows"), c.sig("rows_added")
    nv = ntt // 2
    with block(c) as b:
        @b.tensor
        def _(pe):
            for v in range(nv):
                for k in range(KT):
                    col = mod[:, j * KT + k, v:v + 1].to_broadcast([P, P])
                    last = pe.matmul(c.ps[:, 2 * v + k // 4, (k % 4) * P:(k % 4 + 1) * P], col, eye, start=True, stop=True)
                last.then_inc(spread.sem, 1)

        @b.vector
        def _(dve):
            def scale(t):
                dve.wait_ge(spread.sem, spread.at(t // 2 + 1))
                g = c.ps[:, 2 * (t // 2):2 * (t // 2) + 2, :].rearrange("p b n -> p (b n)")
                dve.tensor_tensor(y[:, t, :], y[:, t, :], g, ALU.mult).then_inc(scaled.sem, 1)

            scale(0)
            for t in range(ntt):
                if t + 1 < ntt:
                    scale(t + 1)
                dve.wait_ge(scaled.sem, scaled.at(t + 1))
                dve.tensor_tensor(x[:, t, :], x[:, t, :], y[:, t, :], ALU.add).then_inc(added.sem, 1)

        @b.scalar
        def _(act):
            for t in range(ntt):
                act.wait_ge(added.sem, added.at(t + 1))
                act.activation(y[:, t, :], x[:, t, :], ACT.Square, accum_out=ss[:, t:t + 1])
    spread.passed(nv)
    scaled.passed(ntt)
    added.passed(ntt)


def attention(c, units, scale, eye, mask=None, pair=None, pool_work=None):
    s_ready, neg_ready, p_ready = c.sig("s_ready"), c.sig("negmax_ready"), c.sig("p_ready")
    w_ready, pt_ready, pt_moved = c.sig("w_ready"), c.sig("pt_ready"), c.sig("pt_moved")
    o_ready, o_moved, step = c.sig("o_ready"), c.sig("o_moved"), c.sig("dve_step")
    n = len(units)
    nk = [sum(k.shape[-1] for k in u["keys"]) for u in units]
    top = max(nk)
    maps = 2 if pair is not None else 1
    with ExitStack() as st:
        sm = c.sb(st, "scores", [P, 2, top]) if mask is not None else None
        p = c.sb(st, "probs", [P, 2, top])
        w = c.sb(st, "mixed", [P, 2, top // 2]) if maps == 2 else None
        pt = c.sb(st, "probs_t", [P, 2, 512])
        neg = c.sb(st, "negmax", [P, 2, 2])
        sums = c.sb(st, "sums", [P, 2, 2])
        inv = c.sb(st, "inv", [P, 2, 2])
        with block(c) as b:
            @b.tensor
            def _(pe):
                def score(u):
                    if u >= 2:
                        pe.wait_ge(p_ready.sem, p_ready.at(u - 1))
                    at, un, bank = 0, units[u], 2 * (u % 2)
                    for i, (q, k) in enumerate(zip(un["q"], un["keys"])):
                        m = k.shape[-1]
                        biased = un.get("bias") is not None and i == 0
                        last = pe.matmul(c.ps[:, bank, at:at + m], q, k, start=True, stop=not biased)
                        if biased:
                            last = pe.matmul(c.ps[:, bank, at:at + m], un["bias"][0], un["bias"][1], start=False, stop=True)
                        if maps == 2:
                            bank += 1
                        else:
                            at += m
                    last.then_inc(s_ready.sem, 1)

                def turns(u):
                    if maps == 2:
                        pe.wait_ge(w_ready.sem, w_ready.at(u + 1))
                    else:
                        pe.wait_ge(p_ready.sem, p_ready.at(u + 1))
                    if u >= 2:
                        pe.wait_ge(pt_moved.sem, pt_moved.at(u - 1))
                    src = w if maps == 2 else p
                    for i in range(nk[u] // maps // P):
                        last = pe.transpose(c.ps[:, 4 + u % 2, i * P:(i + 1) * P], src[:, u % 2, i * P:(i + 1) * P], eye)
                    last.then_inc(pt_ready.sem, 1)

                def values(u):
                    pe.wait_ge(pt_moved.sem, pt_moved.at(u + 1))
                    if u >= 2:
                        pe.wait_ge(o_moved.sem, o_moved.at(u - 1))
                    nv = nk[u] // maps // P
                    dv = units[u]["out"].shape[-1]
                    for i in range(nv):
                        last = pe.matmul(c.ps[:, 6 + u % 2, 0:dv], pt[:, u % 2, i * P:(i + 1) * P], units[u]["v"][i],
                                         start=(i == 0), stop=(i == nv - 1))
                    last.then_inc(o_ready.sem, 1)

                for u in range(n + 3):
                    if u < n:
                        score(u)
                    if 0 <= u - 2 < n:
                        turns(u - 2)
                    if 0 <= u - 3 < n:
                        values(u - 3)

            if pool_work:
                @b.gpsimd
                def _(pool):
                    link = Chain(pool, c.sig("pool_step"))
                    pool_work(pool, link)
                    link.close()

            @b.scalar
            def _(act):
                def exps(u):
                    act.wait_ge(neg_ready.sem, neg_ready.at(u + 1))
                    if u >= 2:
                        if maps == 2:
                            act.wait_ge(w_ready.sem, w_ready.at(u - 1))
                        else:
                            act.wait_ge(pt_ready.sem, pt_ready.at(u - 1))
                    m = nk[u] // maps
                    for i in range(maps):
                        src = c.ps[:, 2 * (u % 2) + i, 0:m] if mask is None else sm[:, u % 2, 0:m]
                        last = act.activation(p[:, u % 2, i * m:(i + 1) * m], src, ACT.Exp, bias=neg[:, u % 2, i:i + 1],
                                              scale=scale if mask is None else 1.0, accum_out=sums[:, u % 2, i:i + 1])
                    last.then_inc(p_ready.sem, 1)

                def move(u):
                    act.wait_ge(pt_ready.sem, pt_ready.at(u + 1))
                    if u >= 2:
                        act.wait_ge(o_ready.sem, o_ready.at(u - 1))
                    m = nk[u] // maps
                    act.activation(pt[:, u % 2, 0:m], c.ps[:, 4 + u % 2, 0:m], ACT.Copy).then_inc(pt_moved.sem, 1)

                for u in range(n + 2):
                    if u < n:
                        exps(u)
                    if u >= 2:
                        move(u - 2)

            @b.vector
            def _(dve):
                link = Chain(dve, step)

                def top_of(u):
                    dve.wait_ge(s_ready.sem, s_ready.at(u + 1))
                    if u >= 2:
                        dve.wait_ge(p_ready.sem, p_ready.at(u - 1))
                    m = nk[u] // maps
                    src = c.ps[:, 2 * (u % 2):2 * (u % 2) + maps, 0:m]
                    if mask is not None:
                        link(dve.scalar_tensor_tensor(out=sm[:, u % 2, 0:m], in0=src[:, 0, :], scalar=scale, in1=mask[:, 0:m],
                                                      op0=ALU.mult, op1=ALU.add))
                        src = sm[:, u % 2:u % 2 + 1, 0:m]
                    link(dve.tensor_reduce(neg[:, u % 2, 0:maps], src, AX, ALU.max))
                    dve.tensor_scalar(neg[:, u % 2, 0:maps], neg[:, u % 2, 0:maps], -1.0 if mask is not None else -scale, None,
                                      ALU.mult).then_inc(neg_ready.sem, 1)

                def mix(u):
                    dve.wait_ge(p_ready.sem, p_ready.at(u + 1))
                    if u >= 2:
                        dve.wait_ge(pt_ready.sem, pt_ready.at(u - 1))
                    m = nk[u] // 2
                    link(dve.reciprocal(inv[:, u % 2, :], sums[:, u % 2, :]))
                    link(dve.tensor_scalar(inv[:, u % 2, 1:2], inv[:, u % 2, 1:2], pair, None, ALU.mult))
                    link(dve.tensor_scalar(w[:, u % 2, :], p[:, u % 2, 0:m], inv[:, u % 2, 0:1], None, ALU.mult))
                    dve.scalar_tensor_tensor(out=w[:, u % 2, :], in0=p[:, u % 2, m:2 * m], scalar=inv[:, u % 2, 1:2],
                                             in1=w[:, u % 2, :], op0=ALU.mult, op1=ALU.add).then_inc(w_ready.sem, 1)

                def recip(u):
                    dve.wait_ge(p_ready.sem, p_ready.at(u + 1))
                    link(dve.reciprocal(inv[:, u % 2, 0:1], sums[:, u % 2, 0:1]))

                def out(u):
                    dve.wait_ge(o_ready.sem, o_ready.at(u + 1))
                    dv = units[u]["out"].shape[-1]
                    src = c.ps[:, 6 + u % 2, 0:dv]
                    if maps == 2:
                        dve.tensor_copy(units[u]["out"], src).then_inc(o_moved.sem, 1)
                    else:
                        dve.tensor_scalar(units[u]["out"], src, inv[:, u % 2, 0:1], None, ALU.mult).then_inc(o_moved.sem, 1)

                for u in range(n + 3):
                    if u < n:
                        top_of(u)
                    if maps == 2 and 0 <= u - 1 < n:
                        mix(u - 1)
                    if 0 <= u - 3 < n:
                        out(u - 3)
                    if maps == 1 and 0 <= u - 1 < n:
                        if u >= 3:
                            dve.wait_ge(o_moved.sem, o_moved.at(u - 2))
                        recip(u - 1)
                link.close()
    for s in (s_ready, neg_ready, p_ready, pt_ready, pt_moved, o_ready, o_moved):
        s.passed(n)
    if maps == 2:
        w_ready.passed(n)


def head_rms(c, v, ntt, h, d, gain, eps, extra=1.0, loads=(), also=None, roots=None):
    squares = c.sig("squares_ready")
    with ExitStack() as st:
        sq = c.sb(st, "sq", [P, ntt, h * d])
        ss, tm = (c.sb(st, n, [P, ntt, h]) for n in ("ss", "root_tmp"))
        r = c.sb(st, "root", [P, ntt, h]) if roots is None else roots
        flat = lambda a: a[:, :, :].rearrange("p t h -> p (t h)")
        with block(c) as b:
            c.ask(b, loads)

            @b.scalar
            def _(act):
                for t in range(ntt):
                    act.activation(sq[:, t, :], v[:, t, :], ACT.Square).then_inc(squares.sem, 1)
                if also:
                    also(act)

            @b.vector
            def _(dve):
                link = Chain(dve, c.sig("dve_step"))
                for t in range(ntt):
                    dve.wait_ge(squares.sem, squares.at(t + 1))
                    link(dve.tensor_reduce(ss[:, t, :], sq[:, t, :].rearrange("p (h d) -> p h d", d=d), AX, ALU.add))
                inverse_root_steps(c, dve, link, flat(ss), 1.0 / d, eps, flat(r), flat(tm))
                if roots is not None:
                    if extra != 1.0:
                        link(dve.tensor_scalar(flat(r), flat(r), extra, None, ALU.mult))
                    link.close()
                    return
                if gain is None:
                    for t in range(ntt):
                        dve.tensor_scalar(v[:, t, :], v[:, t, :], r[:, t, 0:1], None, ALU.mult)
                else:
                    for t in range(ntt):
                        a = v[:, t, :].rearrange("p (h d) -> p h d", d=d)
                        link(dve.tensor_tensor(a, a, r[:, t, :].unsqueeze(2).to_broadcast([P, h, d]), ALU.mult))
                    for t in range(ntt):
                        a = v[:, t, :]
                        if extra == 1.0:
                            dve.tensor_tensor(a, a, gain, ALU.mult)
                        else:
                            dve.scalar_tensor_tensor(out=a, in0=a, scalar=extra, in1=gain, op0=ALU.mult, op1=ALU.mult)
                link.close()
        squares.passed(ntt)


def rotation_scratch(c, st, groups, half):
    return c.sb(st, "rot", [P, len(groups), 4, max(g[0].shape[1] for g in groups), half])


def rotation_products(eng, groups, half, t):
    for i, (x1, x2, co, si) in enumerate(groups):
        h = x1.shape[1]
        cb, sb_ = (a.unsqueeze(1).to_broadcast([P, h, half]) for a in (co, si))
        for m, (a, bb) in enumerate(((x1, cb), (x2, sb_), (x1, sb_), (x2, cb))):
            yield eng.tensor_tensor(t[:, i, m, 0:h, :], a, bb, ALU.mult)


def rotation_sums(eng, groups, half, t):
    for i, (x1, x2, co, si) in enumerate(groups):
        h = x1.shape[1]
        yield eng.tensor_tensor(x1, t[:, i, 0, 0:h, :], t[:, i, 1, 0:h, :], ALU.subtract)
        yield eng.tensor_tensor(x2, t[:, i, 2, 0:h, :], t[:, i, 3, 0:h, :], ALU.add)


def rotate(c, groups, half):
    with ExitStack() as st:
        t = rotation_scratch(c, st, groups, half)
        on_vector(c, lambda dve, link: list(rotation_products(dve, groups, half, t)))
        on_vector(c, lambda dve, link: list(rotation_sums(dve, groups, half, t)))


def fourier(c, u, out, tok, ch, loads=()):
    with ExitStack() as st:
        a = c.sb(st, "dft", [P, 2, 512])
        with block(c) as b:
            c.ask(b, loads)

            @b.tensor
            def _(pe):
                for fg in range(2):
                    for l in range(2):
                        pe.matmul(c.ps[:, fg, :], u[:, l, fg * P:(fg + 1) * P], tok[:, l, :], start=(l == 0), stop=(l == 1))
        with block(c) as b:
            @b.scalar
            def _(act):
                act.activation(a[:, 0, :], c.ps[:, 0, :], ACT.Copy)

            @b.vector
            def _(dve):
                dve.tensor_copy(a[:, 1, :], c.ps[:, 1, :])
        with block(c) as b:
            @b.tensor
            def _(pe):
                for t in range(2):
                    for fg in range(2):
                        for part in range(2):
                            pe.matmul(c.ps[:, 2, t * 256 + fg * P:t * 256 + (fg + 1) * P],
                                      a[:, fg, part * 256 + t * P:part * 256 + (t + 1) * P], ch[:, part, :],
                                      start=(part == 0), stop=(part == 1))
        with block(c) as b:
            @b.vector
            def _(dve):
                dve.tensor_copy(out, c.ps[:, 2, :].rearrange("p (t n) -> p t n", t=2))


def gla_decay(c, g, gate_w, gate_b, a, ones, eye):
    with ExitStack() as st:
        gt = c.sb(st, "gate_t", [32, 1, 4 * P])
        turn(c, lambda t, k: g[:, t, :], gt, 1, 4, 32, eye, split=False)
        pre = c.sb(st, "pre", [P, 4 * 256])
        e = c.sb(st, "gate_e", [P, 4 * 256])
        with block(c) as b:
            @b.tensor
            def _(pe):
                for t in range(4):
                    o = c.ps[:, t // 2, (t % 2) * 256:(t % 2 + 1) * 256]
                    pe.matmul(o, gt[:, 0, t * P:(t + 1) * P], gate_w, start=True, stop=False)
                    pe.matmul(o, ones, gate_b, start=False, stop=True)
        on_vector(c, lambda dve, link: dve.tensor_copy(pre[:, :], c.ps[:, 0:2, :].rearrange("p b n -> p (b n)")))

        def steps(act, link):
            link(act.activation(e[:, :], pre[:, :], ACT.Abs))
            link(act.activation(e[:, :], e[:, :], ACT.Exp, scale=-1.0))
            link(act.activation(e[:, :], e[:, :], ACT.Ln, bias=1.0))
        on_scalar(c, steps)
        on_vector(c, lambda dve, link: dve.scalar_tensor_tensor(
            out=a[:, :, :].rearrange("p t n -> p (t n)"), in0=pre[:, :], scalar=0.0, in1=e[:, :], op0=ALU.min, op1=ALU.subtract))


def decay_sums(pe, ps, a, dec, parts):
    for n, (t, d, tab) in enumerate(parts):
        last = pe.matmul(ps, a[:, t, d * P:(d + 1) * P], dec[:, tab, :], start=(n == 0), stop=(n == len(parts) - 1))
    return last


def gla_state(c, k, v, a, dec, state):
    f = TAB
    with ExitStack() as st:
        e = c.sb(st, "end_decay", [P, 2, 2, P])
        kd = c.sb(st, "k_decayed", [P, 2, 2, P])
        parts = [[[(0, f["gt"]), (1, f["ones"])], [(1, f["gt"])]], [[(0, f["lt"])], [(1, f["lt"]), (0, f["ones"])]]]
        with block(c) as b:
            @b.tensor
            def _(pe):
                for d in range(2):
                    for t in range(2):
                        pp = parts[d][t]
                        for n, (src, tab) in enumerate(pp):
                            pe.matmul(c.ps[:, d, t * P:(t + 1) * P], dec[:, tab, :], a[:, src, d * P:(d + 1) * P],
                                      start=(n == 0), stop=(n == len(pp) - 1))

            @b.vector
            def _(dve):
                dve.memset(state[:, :, :], 0.0)
        on_scalar(c, lambda act, link: [act.activation(e[:, d, :, :].rearrange("p t n -> p (t n)"), c.ps[:, d, 0:256], ACT.Exp)
                                        for d in range(2)])
        on_vector(c, lambda dve, link: [dve.tensor_tensor(kd[:, d, :, :], e[:, d, :, :], k, ALU.mult) for d in range(2)])
        with block(c) as b:
            @b.tensor
            def _(pe):
                for d in range(2):
                    for t in range(2):
                        pe.matmul(c.ps[:, d, 0:256], kd[:, d, t, :], v[:, t, :], start=(t == 0), stop=(t == 1))
        on_vector(c, lambda dve, link: [dve.tensor_copy(state[32 * h:32 * h + 32, d, 64 * h:64 * h + 64],
                                                        c.ps[32 * h:32 * h + 32, d, 64 * h:64 * h + 64])
                                        for d in range(2) for h in range(GLA_HEADS)])


def halves_of(t, at, s, first, second):
    one = t[:, 0:1]
    return bass.AP(tensor=one.tensor, offset=one.offset + at + first,
                   ap=[list(one.ap[0]), [2 * s, 256 // (2 * s)], [s + second - first, 2], [1, s]])


def gla_output(c, qk, at, v, a, dec, levels, state, out, loads=()):
    f = TAB
    span = qk.shape[1] // 2
    e_ready, e_exp, qk_ready = c.sig("decay_ready"), c.sig("decay_exp"), c.sig("qk_ready")
    sc_ready, sc_taken = c.sig("level_ready"), c.sig("level_taken")
    across = GLA_LEVELS
    n = GLA_LEVELS + 1
    with ExitStack() as st:
        near = c.sb(st, "scores_near", [P, GLA_HEADS, 2, P])
        far = c.sb(st, "scores_far", [P, GLA_HEADS, 2, P])
        ex = c.sb(st, "decays", [P, 2, n, 256])
        exi = c.sb(st, "start_decays", [P, 2, 256])
        dq = c.sb(st, "decayed", [P, 2, 512])
        dqi = c.sb(st, "q_since_start", [P, 2, 256])
        with block(c) as b:
            @b.tensor
            def _(pe):
                for d in range(2):
                    for t in range(2):
                        bank = 4 * d + 2 * t
                        l0 = d * GLA_LEVELS
                        at_ = a[:, t, d * P:(d + 1) * P]
                        pe.matmul(c.ps[:, bank, :], at_, dec[:, l0:l0 + 4, :], start=True, stop=True).then_inc(e_ready.sem, 1)
                        pe.matmul(c.ps[:, bank + 1, 0:3 * P], at_, dec[:, l0 + 4:l0 + 7, :], start=True, stop=True)
                        tab = ((f["gt"], f["le"]), (f["ge"], f["lt"]))[d][t]
                        pe.matmul(c.ps[:, bank + 1, 3 * P:4 * P], at_, dec[:, tab, :], start=True, stop=True).then_inc(e_ready.sem, 1)
                if state is not None:
                    pe.wait_ge(e_exp.sem, e_exp.at(1))
                    decay_sums(pe, c.ps[:, 0, 0:P], a, dec, [(0, 0, f["le"])])
                    decay_sums(pe, c.ps[:, 0, P:2 * P], a, dec, [(1, 0, f["le"]), (0, 0, f["ones"])])
                    decay_sums(pe, c.ps[:, 0, 2 * P:3 * P], a, dec, [(0, 1, f["ge"]), (1, 1, f["ones"])])
                    decay_sums(pe, c.ps[:, 0, 3 * P:4 * P], a, dec, [(1, 1, f["ge"])]).then_inc(e_ready.sem, 1)

            @b.scalar
            def _(act):
                for m in range(8):
                    d, t, part = m // 4, m // 2 % 2, m % 2
                    act.wait_ge(e_ready.sem, e_ready.at(m + 1))
                    act.activation(ex[:, d, 4 * part:4 * part + 4, t * P:(t + 1) * P],
                                   c.ps[:, m, :].rearrange("p (l n) -> p l n", l=4), ACT.Exp).then_inc(e_exp.sem, 1)
                if state is not None:
                    act.wait_ge(e_ready.sem, e_ready.at(9))
                    act.activation(exi[:, :, :].rearrange("p d n -> p (d n)"), c.ps[:, 0, :], ACT.Exp)
        e_ready.passed(9 if state is not None else 8)
        e_exp.passed(8)
        units = [(m, pair) for m in range(-1, n) for pair in range(2)]
        with block(c) as b:
            c.ask(b, loads)

            @b.tensor
            def _(pe):
                for u, (m, pair) in enumerate(units):
                    if m >= 0:
                        pe.wait_ge(qk_ready.sem, qk_ready.at(m + 1))
                    if u >= 4:
                        pe.wait_ge(sc_taken.sem, sc_taken.at(u - 3))
                    for t in range(2):
                        jt, it = (t, 1 - t) if m == across else (t, t)
                        for i in range(2):
                            r = slice(32 * (2 * pair + i), 32 * (2 * pair + i) + 32)
                            if m >= 0:
                                k_, q_ = dq[r, m % 2, 256 + jt * P:256 + (jt + 1) * P], dq[r, m % 2, it * P:(it + 1) * P]
                            else:
                                k_, q_ = qk[r, span + at + jt * P:span + at + (jt + 1) * P], qk[r, at + it * P:at + (it + 1) * P]
                            last = pe.matmul(c.ps[:, 2 * (u % 4) + i, t * P:(t + 1) * P], k_, q_, start=True, stop=True)
                    last.then_inc(sc_ready.sem, 1)

            @b.vector
            def _(dve):
                def decayed(m):
                    if m >= 2:
                        dve.wait_ge(sc_ready.sem, sc_ready.at(2 * m))
                    s = 2 ** m
                    buf = dq[:, m % 2, :]
                    for d in range(2):
                        first, second = (1, 0) if d == 0 else (0, 1)
                        last = dve.tensor_tensor(halves_of(buf, 0, s, first * 256, second * 256),
                                                 halves_of(qk, at, s, first * span, second * span),
                                                 halves_of(ex[:, d, m, :], 0, s, 0, 0), ALU.mult)
                    last.then_inc(qk_ready.sem, 1)

                def take(u):
                    m, pair = units[u]
                    dve.wait_ge(sc_ready.sem, sc_ready.at(u + 1))
                    if u >= 2:
                        dve.wait_ge(sc_taken.sem, sc_taken.at(u - 1))
                    b0 = 2 * (u % 4)
                    src = c.ps[:, b0:b0 + 2, 0:2 * P]
                    hs = slice(2 * pair, 2 * pair + 2)
                    if m == -1:
                        last = dve.tensor_scalar(near[:, hs, :, :].rearrange("p h t n -> p h (t n)"), src, 2.0, None, ALU.mult)
                    elif m == across:
                        last = dve.tensor_copy(far[:, hs, :, :].rearrange("p h t n -> p h (t n)"), src)
                    else:
                        last = dve.copy_predicated(near[:, hs, :, :].rearrange("p h t n -> p (h t) n"),
                                                   levels[:, m, :].unsqueeze(1).to_broadcast([P, 4, P]),
                                                   src.rearrange("p h (t n) -> p h t n", t=2))
                    last.then_inc(sc_taken.sem, 1)
                decayed(0)
                for m in range(-1, n):
                    if 0 < m + 1 < n:
                        decayed(m + 1)
                    take(2 * (m + 1))
                    take(2 * (m + 1) + 1)
                if state is not None:
                    for d in range(2):
                        dve.tensor_tensor(dqi[:, d, :], qk[:, at:at + 256], exi[:, d, :], ALU.mult)
        qk_ready.passed(n)
        sc_ready.passed(len(units))
        sc_taken.passed(len(units))
        with block(c) as b:
            @b.tensor
            def _(pe):
                for it in range(2):
                    for h in range(GLA_HEADS):
                        o = c.ps[:, 6 + it, 64 * h:64 * h + 64]
                        if state is not None:
                            for d in range(2):
                                pe.matmul(o, dqi[:, d, it * P:(it + 1) * P], state[:, d, 64 * h:64 * h + 64],
                                          start=(d == 0), stop=False)
                        for jt in range(2):
                            s_t = near[:, h, it, :] if it == jt else far[:, h, jt, :]
                            last = pe.matmul(o, s_t, v[:, jt, 64 * h:64 * h + 64], start=(state is None and jt == 0), stop=(jt == 1))
                    last.then_inc(sc_ready.sem, 1)

            @b.vector
            def _(dve):
                for it in range(2):
                    dve.wait_ge(sc_ready.sem, sc_ready.at(it + 1))
                    dve.tensor_copy(out[:, it, :], c.ps[:, 6 + it, 0:256])
        sc_ready.passed(2)


def encoder_program(nc, A, out, stop=None):
    with ExitStack() as ctx:
        c = Core(nc, ctx)
        sb = lambda name, shape, dt=F32: ctx.enter_context(nc.sbuf_tensor(name, shape, dt))
        dma_in = c.sig("dma_in", 16)

        x = sb("x", [P, 4, D])
        eye = sb("eye", [P, P])
        rope = sb("rope", [P, 2, 2, 32])
        mod = sb("mod", [P, 9 * KT, 2])
        silu4 = sb("silu4", [P, KT, 4], F32R)
        comb = sb("comb", [4, 2])
        b_mod_t = sb("b_mod_t", [P, LAYERS, 9 * KT])
        ones = sb("ones", [1, P])
        ss_x = sb("ss_x", [P, 4])
        angles = sb("angles", [P, 2, 2, 24])

        win = [chunks_of(A["w_in"][l], 0, KT, 0, D_IN) for l in range(LAYERS)]
        wout = [chunks_of(A["w_out"][l], 0, KT, 0, D) for l in range(LAYERS)]
        for l in range(LAYERS):
            c.heads.append(modulation_heads(A["w_mod"][l]))
            c.heads.append(ffn_heads(A["ffn1_w1"][l], A["ffn1_w3"][l], A["ffn1_w2"][l]))
            c.heads.append(project_heads(win[l]))
            c.heads.append(project_heads(wout[l]))
            c.heads.append(ffn_heads(A["ffn2_w1"][l], A["ffn2_w3"][l], A["ffn2_w2"][l]))
        second = []
        for l in range(LAYERS):
            s = dict(
                main=chunks_of(A["w_in_2"][l], 0, KT, 0, OFF2["gate"]),
                uq=chunks_of(A["mla_w_uq_2"][l], 0, 3, 0, MLA_HEADS * MLA_QK),
                ukv=chunks_of(A["mla_w_ukv_2"][l], 0, 2, 0, MLA_HEADS * 2 * MLA_NOPE),
                memkv=chunks_of(A["mem_w_kv_2"][l], 0, KT, 0, 2 * MEM_HEADS * MEM_HD),
                gate=chunks_of(A["w_in_2"][l], 0, KT, OFF2["gate"], 3 * D),
                b0=chunks_of(A["w_branch_2"][l], 0, 4, 0, D),
                b1=chunks_of(A["w_branch_2"][l], 512, 8, 0, D),
                b2=chunks_of(A["w_branch_2"][l], 1536, 4, 0, D),
                out=chunks_of(A["w_out_2"][l], 0, KT, 0, D))
            second.append(s)
            c.heads += [project_heads(s[k]) for k in ("main", "gate", "uq", "ukv", "memkv", "b0", "b1", "b2", "out")]
            c.heads.append(mlp_heads(A["mlp_w1_2"][l], A["mlp_w2_2"][l]))

        def load_all(pairs):
            with block(c) as b:
                @b.sync
                def _(sp):
                    with nc.allow_non_contiguous_dma(reason="small vectors"):
                        for dst, src in pairs:
                            sp.dma_start(dst, src).then_inc(dma_in.sem, 16)
                    sp.wait_ge(dma_in.sem, dma_in.at(len(pairs)))
            dma_in.passed(len(pairs))

        with ExitStack() as st:
            cond = c.sb(st, "cond", [16, P])
            cond_t = c.sb(st, "cond_t", [P, 16])
            bm = c.sb(st, "b_mod", [9 * KT, LAYERS, P])
            small = [(cond[0:8, :], A["c"].rearrange("o (k p) -> (o k) p", p=P)),
                     (cond[8:16, :], A["c_ctx"].rearrange("(k p) -> k p", p=P)), (eye[:, :], A["k_eye"]),
                     (bm[:, :, :], A["b_mod"].rearrange("l (f p) -> f l p", p=P)),
                     (comb[0:2, :], A["k_eye"][0:2, 0:2]), (comb[2:4, :], A["k_eye"][0:2, 0:2])]
            with block(c) as b:
                @b.sync
                def _(sp):
                    with nc.allow_non_contiguous_dma(reason="small vectors"):
                        for dst, src in small:
                            sp.dma_start(dst, src).then_inc(dma_in.sem, 16)
                    c.load_heads(sp, [0] * SLOTS)
                    sp.wait_ge(dma_in.sem, dma_in.at(len(small)))
                dma_in.passed(len(small))

                @b.vector
                def _(dve):
                    dve.memset(ones[:, :], 1.0)
            with block(c) as b:
                c.ask(b, [(x[:, 0:2, :], A["x"][0].rearrange("(t p) d -> p t d", p=P)),
                          (x[:, 2:4, :], A["ctx"][0].rearrange("(t p) d -> p t d", p=P)), (rope[:, :, :, :], A["k_rope"])])

                @b.tensor
                def _(pe):
                    pe.transpose(c.ps[:, 0, 0:16], cond[:, :], eye[0:16, 0:16])
                    for l in range(LAYERS):
                        pe.transpose(c.ps[:, 1 + l, 0:9 * KT], bm[:, l, :], eye[0:9 * KT, 0:9 * KT])
            silu_ready, silu_hi = c.sig("silu_ready"), c.sig("ghi_ready")
            cv = cond_t[:, :].rearrange("p (v k) -> p k v", v=2)
            with block(c) as b:
                @b.scalar
                def _(act):
                    act.activation(cond_t[:, :], c.ps[:, 0, 0:16], ACT.Silu).then_inc(silu_ready.sem, 1)
                    act.wait_ge(silu_ready.sem, silu_ready.at(1))
                    act.activation(silu4[:, :, 0:2], cv, ACT.Copy).then_inc(silu_hi.sem, 1)

                @b.vector
                def _(dve):
                    for l in range(LAYERS):
                        dve.tensor_copy(b_mod_t[:, l, :], c.ps[:, 1 + l, 0:9 * KT])
                    dve.wait_ge(silu_hi.sem, silu_hi.at(1))
                    dve.tensor_tensor(silu4[:, :, 2:4], cv, silu4[:, :, 0:2].bitcast(F32), ALU.subtract)
            silu_ready.passed(1)
            silu_hi.passed(1)

        def mod_cols(j, ntt):
            def cols(k):
                return [(v * TOK, (v + 1) * TOK, mod[:, (j + 1) * KT + k, v:v + 1], mod[:, j * KT + k, v:v + 1])
                        for v in range(ntt // 2)]
            return cols

        def modulated(st, j, ntt, loads=()):
            pair = [c.sb(st, "xt_hi", [P, KT, ntt * P], F32R), c.sb(st, "xt_lo", [P, KT, ntt * P], F32R)]
            turn(c, lambda t, k: x[:, t, k * P:(k + 1) * P], pair, KT, ntt, P, eye[:, :], cols=mod_cols(j, ntt),
                 norm=ss_x, loads=loads)
            return pair

        def feed_forward(l, which, j, ntt):
            with ExitStack() as st:
                pair = modulated(st, j, ntt)
                y = c.sb(st, "y", [P, ntt, D])
                swiglu(c, A[f"ffn{which}_w1"][l], A[f"ffn{which}_w3"][l], A[f"ffn{which}_w2"][l], pair, ntt, y,
                       x, mod, j + 2, eye[:, :], ss_x)

        for l in range(LAYERS):
            final = l == LAYERS - 1
            modulation(c, A["w_mod"][l], silu4, b_mod_t[:, l, :], mod, comb[:, :], (x, ss_x, dma_in) if l == 0 else None)
            if l == 0:
                c.arrived()
            if stop == f"mod{l}":
                return
            feed_forward(l, 1, 0, 4)
            if stop == f"ffn1_{l}":
                return
            nmix = 2 if final else 4
            with ExitStack() as st_mix:
                mix = c.sb(st_mix, "mix", [P, nmix, D])
                with ExitStack() as st:
                    h = c.sb(st, "h", [P, 4, D_IN])
                    dft_tok = c.sb(st, "dft_tok", [P, 2, 512])
                    dft_ch = c.sb(st, "dft_ch", [P, 2, P])
                    with ExitStack() as s2:
                        pair = modulated(s2, 3, 4, loads=[(dft_tok[:, :, :], A["k_dft_tok"]), (dft_ch[:, :, :], A["k_dft_ch"])])
                        project(c, win[l], lhs_of(pair), 4, into(h, 256))
                    if stop == f"win{l}":
                        return
                    first_mixers(c, A, l, final, h, mix, eye, rope, ones, dft_tok, dft_ch)
                if stop == f"mix{l}":
                    return
                with ExitStack() as s2:
                    pair = [c.sb(s2, "mt_hi", [P, KT, nmix * P], F32R), c.sb(s2, "mt_lo", [P, KT, nmix * P], F32R)]
                    turn(c, lambda t, k: mix[:, t, k * P:(k + 1) * P], pair, KT, nmix, P, eye[:, :])
                    y = c.sb(s2, "y", [P, nmix, D])
                    project(c, wout[l], lhs_of(pair), nmix, into(y, 256))
                    residual(c, x, y, nmix, mod, 5, eye[:, :], ss_x)
            feed_forward(l, 2, 6, nmix)
            if stop == f"first{l}":
                return

        rotary_tables(c, A, angles, load_all)
        for l in range(LAYERS):
            second_layer(c, A, l, x, angles, second[l], eye, stop)
            if stop in (f"branches{l}", f"attn2_{l}", f"second{l}"):
                return
        with block(c) as b:
            @b.sync
            def _(sp):
                sp.dma_start(out[0].rearrange("(t p) d -> p t d", p=P), x[:, 0:2, :]).then_inc(dma_in.sem, 16)
                sp.wait_ge(dma_in.sem, dma_in.at(1))


def first_mixers(c, A, l, final, h, mix, eye, rope, ones, tok, ch):
    O = OFF
    nmix = 2 if final else 4
    with ExitStack() as st:
        gain, g_na, mask = ch[:, :, :].rearrange("p a n -> p (a n)"), tok[:, 0, :], tok[:, 1, :]
        g_gqa = c.sb(st, "gqa_gain", [P, 384])
        flip = c.sb(st, "flip", [P, P])
        rep = lambda g, n: g[l:l + 1].unsqueeze(1).to_broadcast([P, n, HD])
        hd = lambda v: v.rearrange("p (h d) -> p h d", d=HD)
        na_loads = [(hd(g_na[:, 0:256]), rep(A["na_q_norm"], 4)), (hd(g_na[:, 256:512]), rep(A["na_k_norm"], 4)),
                    (hd(g_gqa[:, 0:256]), rep(A["gqa_q_norm"], 4)), (hd(g_gqa[:, 256:384]), rep(A["gqa_k_norm"], 2)),
                    (mask, A["k_na_mask"]), (flip[:, :], A["k_flip"]),
                    (gain.rearrange("p (h d) -> p h d", d=HD), A["gla_norm"][l:l + 1].unsqueeze(1).to_broadcast([P, 4, HD]))]
        gla = ExitStack()
        dec = c.sb(gla, "decay_tables", [P, 19, P])
        lev = c.sb(gla, "level_masks", [P, GLA_LEVELS, P], I32)
        gw = c.sb(gla, "gate_w", [32, 256])
        gb = c.sb(gla, "gate_b", [1, 256])
        state = c.sb(gla, "state", [P, 2, 256])
        a = c.sb(gla, "log_decay", [P, 4, 256])
        qk = c.sb(gla, "qk_t", [P, 2 * nmix * P])
        on_vector(c, lambda dve, link: dve.memset(gw[:, :], 0.0))
        loads = [(dec[:, :, :], A["k_decay"]), (lev[:, :, :], A["k_levels"]),
                  (gw[0:16, 0:P], A["gla_w_gate_f"][l]), (gw[16:32, P:2 * P], A["gla_w_gate_b"][l]),
                  (gb[:, 0:P], A["gla_b_gate_f"][l:l + 1]), (gb[:, P:2 * P], A["gla_b_gate_b"][l:l + 1])]
        for s in range(nmix // 2):
            t = slice(2 * s, 2 * s + 2)
            fourier(c, h[:, t, 0:256], mix[:, t, 0:256], tok, ch, loads if s == 0 else ())
        c.arrived()
        gla_decay(c, h[:, :, O["gla_g"]:O["gla_g"] + 32], gw[:, :], gb[:, :], a, ones[:, :], eye[:, :])
        turn(c, lambda tt, k: h[:, tt, O["gla_q"] + k * P:O["gla_q"] + (k + 1) * P], qk[:, :].rearrange("p (k n) -> p k n", k=2),
             2, nmix, P, eye[:, :], split=False, side=lambda k: GLA_DK ** -0.5 if k == 0 else 1.0)
        for s in (1, 0):
            t = slice(2 * s, 2 * s + 2)
            v = h[:, t, O["gla_v"]:O["gla_v"] + 256]
            a_s = a[:, t, :]
            if s == 0 or not final:
                gla_output(c, qk, s * TOK, v, a_s, dec, lev, state if s == 0 else None, mix[:, t, 512:768],
                           na_loads if s == 0 else ())
            if s == 1:
                gla_state(c, h[:, t, O["gla_k"]:O["gla_k"] + P], v, a_s, dec, state)
        gla.close()
        bias = c.sb(st, "na_bias", [P, 2, NA_HEADS, 4, GRID_W])
        rpb = A["na_rpb"]
        loads, later = [], []
        for rq in range(4):
            for hh in range(NA_HEADS):
                at = ((l * NA_HEADS + hh) * RPB_ROWS + 7 - rq) * RPB_COLS + 15 - (GRID_W - 1)
                src = bass.AP(tensor=rpb.tensor, offset=rpb.offset + at, ap=[[1, GRID_W], [RPB_COLS, 4], [1, GRID_W]])
                (loads if rq < 2 else later).append((bias[64 * (rq % 2):64 * (rq % 2) + 64, rq // 2, hh, :, :], src))
        out_gate = h[:, 0:nmix, O["gla_r"]:O["gla_r"] + 256]
        c.arrived()
        gla_roots = c.sb(st, "gla_roots", [P, nmix, 4])
        head_rms(c, mix[:, :, 512:768], nmix, 4, HD, None, EPS, loads=loads, roots=gla_roots,
                 also=lambda act: act.activation(out_gate, out_gate, ACT.Silu))

        def gla_norm(pool, link):
            for t in range(nmix):
                v = mix[:, t, 512:768]
                link(pool.tensor_tensor(hd(v), hd(v), gla_roots[:, t, :].unsqueeze(2).to_broadcast([P, 4, HD]), ALU.mult))
                link(pool.tensor_tensor(v, v, gain[:, :], ALU.mult))
                link(pool.tensor_tensor(v, v, out_gate[:, t, :], ALU.mult))
        head_rms(c, h[:, :, O["na_q"]:O["na_q"] + 512], 4, 8, HD, g_na[:, :], EPS, loads=later)
        roots = c.sb(st, "gqa_roots", [P, 4, 6])
        head_rms(c, h[:, :, O["gqa_q"]:O["gqa_q"] + 384], 4, 6, HD, None, EPS, roots=roots)
        groups = []
        for t in range(2):
            v = h[:, t, O["gqa_q"]:O["gqa_q"] + 384].rearrange("p (h d) -> p h d", d=HD)
            groups.append((v[:, :, 0:32], v[:, :, 32:64], rope[:, t, 0, :], rope[:, t, 1, :]))
        turned = rotation_scratch(c, st, groups, 32)

        def gqa_norm_and_rotation(pool, link):
            for t in range(4):
                v = h[:, t, O["gqa_q"]:O["gqa_q"] + 384]
                link(pool.tensor_tensor(hd(v), hd(v), roots[:, t, :].unsqueeze(2).to_broadcast([P, 6, HD]), ALU.mult))
                link(pool.tensor_tensor(v, v, g_gqa[:, :], ALU.mult))
            for ins in rotation_products(pool, groups, 32, turned):
                link(ins)
            for ins in rotation_sums(pool, groups, 32, turned):
                link(ins)
            gla_norm(pool, link)
        na_t = c.sb(st, "na_t", [P, 4, 512])
        turn(c, lambda t, k: h[:, t, O["na_q"] + k * P:O["na_q"] + (k + 1) * P], na_t, 4, 4, P, eye[:, :], split=False)
        units = []
        for hh in range(NA_HEADS):
            r = slice(64 * (hh % 2), 64 * (hh % 2) + 64)
            for qt in range(2):
                q = na_t[r, hh // 2, qt * P:(qt + 1) * P]
                vs = [h[:, kt, O["na_v"] + 64 * hh:O["na_v"] + 64 * hh + 64] for kt in range(4)]
                units.append(dict(q=[q, q], keys=[na_t[r, 2 + hh // 2, 0:256], na_t[r, 2 + hh // 2, 256:512]], v=vs,
                                  bias=(flip[:, :], bias[:, qt, hh, :, :].rearrange("p r c -> p (r c)")),
                                  out=mix[:, qt, 256 + 64 * hh:256 + 64 * hh + 64]))
        c.arrived()
        attention(c, units, HD ** -0.5, eye[:, :], mask=mask, pool_work=gqa_norm_and_rotation)
        if not final:
            units = []
            for hh in range(NA_HEADS):
                r = slice(64 * (hh % 2), 64 * (hh % 2) + 64)
                for qt in range(2, 4):
                    vs = [h[:, kt, O["na_v"] + 64 * hh:O["na_v"] + 64 * hh + 64] for kt in (2, 3)]
                    units.append(dict(q=[na_t[r, hh // 2, qt * P:(qt + 1) * P]], keys=[na_t[r, 2 + hh // 2, 256:512]], v=vs,
                                      out=mix[:, qt, 256 + 64 * hh:256 + 64 * hh + 64]))
            attention(c, units, HD ** -0.5, eye[:, :])
    with ExitStack() as st:
        g_t = c.sb(st, "gqa_t", [HD, 6, 512])
        turn(c, lambda t, k: h[:, t, O["gqa_q"] + k * HD:O["gqa_q"] + (k + 1) * HD], g_t, 6, 4, HD, eye[:, :], split=False)
        units = []
        for qt in range(nmix):
            for hh in range(4):
                kv = hh // 2
                lo = 0 if qt < 2 else 2
                vs = [h[:, kt, O["gqa_v"] + HD * kv:O["gqa_v"] + HD * kv + HD] for kt in range(lo, 4)]
                units.append(dict(q=[g_t[:, hh, qt * P:(qt + 1) * P]], keys=[g_t[:, 4 + kv, lo * P:512]], v=vs,
                                  out=mix[:, qt, 768 + HD * hh:768 + HD * hh + HD]))
        attention(c, units, HD ** -0.5, eye[:, :])


TWO_PI = 2 * math.pi
PI_A = 6.28125
PI_B = float(np.float32(TWO_PI - PI_A))
PI_C = float(TWO_PI - PI_A - PI_B)
PI_TOP = 3.1415925
ROUND = 12582912.0


def rotary_tables(c, A, angles, load_all):
    with ExitStack() as st:
        pos = c.sb(st, "pos", [P, 2], I32)
        posf = c.sb(st, "posf", [P, 2])
        inv = c.sb(st, "inv", [P, 24])
        ang = c.sb(st, "ang", [P, 2, 24])
        k = c.sb(st, "turns", [P, 2, 24])
        load_all([(pos[:, :], A["positions_2"].rearrange("o (t p) -> p (o t)", p=P)), (inv[:, :], A["k_inv"])])

        def steps(dve, link):
            link(dve.tensor_copy(posf[:, :], pos[:, :]))
            for t in range(2):
                link(dve.tensor_scalar(ang[:, t, :], inv[:, :], posf[:, t:t + 1], None, ALU.mult))
            link(dve.tensor_scalar(k[:, :, :], ang[:, :, :], 1.0 / TWO_PI, None, ALU.mult))
            link(dve.tensor_scalar(k[:, :, :], k[:, :, :], ROUND, None, ALU.add))
            link(dve.tensor_scalar(k[:, :, :], k[:, :, :], -ROUND, None, ALU.add))
            for part in (PI_A, PI_B, PI_C):
                link(dve.scalar_tensor_tensor(out=ang[:, :, :].rearrange("p t n -> p (t n)"),
                                              in0=k[:, :, :].rearrange("p t n -> p (t n)"), scalar=-part,
                                              in1=ang[:, :, :].rearrange("p t n -> p (t n)"), op0=ALU.mult, op1=ALU.add))
            link(dve.tensor_scalar(angles[:, :, 1, :], ang[:, :, :], PI_TOP, -PI_TOP, ALU.min, ALU.max))
            link(dve.tensor_scalar(ang[:, :, :], angles[:, :, 1, :], -1.0, None, ALU.mult))
            link(dve.tensor_tensor(ang[:, :, :], ang[:, :, :], angles[:, :, 1, :], ALU.max))
            link(dve.tensor_scalar(angles[:, :, 0, :], ang[:, :, :], -1.0, math.pi / 2, ALU.mult, ALU.add))
        on_vector(c, steps)
        on_scalar(c, lambda act, link: link(act.activation(angles[:, :, :, :].rearrange("p a b n -> p (a b n)"),
                                                           angles[:, :, :, :].rearrange("p a b n -> p (a b n)"), ACT.Sin)))


def layer_norm(c, x, y, g, b_):
    centered, squared = c.sig("mean_ready"), c.sig("squares_ready")
    with ExitStack() as st:
        sums, mean, ss, r, tm = (c.sb(st, n, [P, 2]) for n in ("sum", "mean", "ss", "root", "root_tmp"))
        with block(c) as b:
            @b.vector
            def _(dve):
                link = Chain(dve, c.sig("dve_step"))

                def times_gain(t):
                    link(dve.scalar_tensor_tensor(out=x[:, t, :], in0=x[:, t, :], scalar=mean[:, t:t + 1], in1=g,
                                                  op0=ALU.add, op1=ALU.mult))

                for t in range(2):
                    link(dve.scalar_tensor_tensor(out=x[:, t, :], in0=x[:, t, :], scalar=ALPHA, in1=y[:, t, :],
                                                  op0=ALU.mult, op1=ALU.add, accum_out=sums[:, t:t + 1]))
                    dve.tensor_scalar(mean[:, t:t + 1], sums[:, t:t + 1], -1.0 / D, None, ALU.mult).then_inc(centered.sem, 1)
                dve.wait_ge(centered.sem, centered.at(2))
                dve.wait_ge(squared.sem, squared.at(1))
                times_gain(0)
                dve.wait_ge(squared.sem, squared.at(2))
                inverse_root_steps(c, dve, link, ss[:, :], 1.0 / D, LN_EPS, r[:, :], tm[:, :])
                dve.scalar_tensor_tensor(out=x[:, 0, :], in0=x[:, 0, :], scalar=r[:, 0:1], in1=b_, op0=ALU.mult, op1=ALU.add)
                times_gain(1)
                dve.scalar_tensor_tensor(out=x[:, 1, :], in0=x[:, 1, :], scalar=r[:, 1:2], in1=b_, op0=ALU.mult, op1=ALU.add)
                link.close()

            @b.scalar
            def _(act):
                for t in range(2):
                    act.wait_ge(centered.sem, centered.at(t + 1))
                    act.activation(y[:, t, :], x[:, t, :], ACT.Square, bias=mean[:, t:t + 1],
                                   accum_out=ss[:, t:t + 1]).then_inc(squared.sem, 1)
        centered.passed(2)
        squared.passed(2)


def second_layer(c, A, l, x, angles, S, eye, stop):
    O = OFF2
    lam0 = 0.8 - 0.6 * math.exp(-0.3 * l)
    ident = eye[:, :]
    with ExitStack() as st_o:
        o = c.sb(st_o, "branches", [P, 2, 2048])
        merged_in = c.sb(st_o, "gates", [P, 2, 3 * D])
        with ExitStack() as st_g:
            with ExitStack() as st:
                h = c.sb(st, "h2", [P, 2, O["gate"]])
                gq = c.sb(st, "gq", [P, 3])
                gk = c.sb(st, "gk", [P, 2])
                lam = c.sb(st, "lam", [P, 4, DIFF_D])
                sub = c.sb(st, "subln", [P, 8 * 128])
                with ExitStack() as sn:
                    bg = c.sb(sn, "b_gate", [P, 3 * D])
                    xt = [c.sb(sn, "x2_hi", [P, KT, TOK], F32R), c.sb(sn, "x2_lo", [P, KT, TOK], F32R)]
                    loads = [(gq[:, :], A["mla_q_norm_2"][l].rearrange("(k p) -> p k", p=P)),
                             (gk[:, :], A["mla_kv_norm_2"][l].rearrange("(k p) -> p k", p=P)),
                             (lam[:, :, :], A["diff_lambda_2"][l:l + 1].to_broadcast([P, 4, DIFF_D])),
                             (bg[:, :], A["b_gate_2"][l:l + 1].rearrange("o a d -> o (a d)").to_broadcast([P, 3 * D])),
                             (sub[:, :].rearrange("p (h d) -> p h d", d=128),
                            A["diff_subln_2"][l:l + 1].unsqueeze(1).to_broadcast([P, 8, 128]))]
                    turn(c, lambda t, k: x[:, t, k * P:(k + 1) * P], xt, KT, 2, P, ident, loads=loads)
                    project(c, S["main"], lhs_of(xt), 2, into(h, 256))
                    c.arrived()
                    at = lambda n: slice(n * 256, (n + 1) * 256) if isinstance(n, int) else bass.ds(n * 256, 256)

                    def biased(dve, n, v):
                        return dve.tensor_tensor(merged_in[:, :, at(n)], v, bg[:, at(n)].unsqueeze(1).to_broadcast([P, 2, 256]),
                                                 ALU.add)

                    def sigmoid(act, n):
                        return act.activation(merged_in[:, :, at(n)], merged_in[:, :, at(n)], ACT.Sigmoid)
                    project(c, S["gate"], lhs_of(xt), 2, biased, on_act=False, act_then=sigmoid)
                with ExitStack() as sm:
                    q = c.sb(sm, "mla_q", [P, 2, MLA_HEADS * MLA_QK])
                    kv = c.sb(sm, "mla_kv", [P, 2, MLA_HEADS * 2 * MLA_NOPE])
                    with ExitStack() as sn:
                        head_rms(c, h[:, :, 0:Q_LORA], 2, 1, Q_LORA, None, EPS)
                        head_rms(c, h[:, :, O["ckv"]:O["ckv"] + KV_LORA], 2, 1, KV_LORA, None, EPS)
                        cq = [c.sb(sn, "cq_hi", [P, 3, TOK], F32R), c.sb(sn, "cq_lo", [P, 3, TOK], F32R)]
                        turn(c, lambda t, k: h[:, t, k * P:(k + 1) * P], cq, 3, 2, P, ident,
                             cols=lambda k: [(0, TOK, gq[:, k:k + 1], None)])
                        project(c, S["uq"], lhs_of(cq), 2, into(q, 512))
                        ck = [c.sb(sn, "ck_hi", [P, 2, TOK], F32R), c.sb(sn, "ck_lo", [P, 2, TOK], F32R)]
                        turn(c, lambda t, k: h[:, t, O["ckv"] + k * P:O["ckv"] + (k + 1) * P], ck, 2, 2, P, ident,
                             cols=lambda k: [(0, TOK, gk[:, k:k + 1], None)])
                        project(c, S["ukv"], lhs_of(ck), 2, into(kv, 512))
                    groups = []
                    for t in range(2):
                        co, si = angles[:, t, 0, 0:16], angles[:, t, 1, 0:16]
                        qv = q[:, t, :].rearrange("p (h d) -> p h d", d=MLA_QK)
                        groups.append((qv[:, :, 64:80], qv[:, :, 80:96], co, si))
                        kp = h[:, t, O["kpe"]:O["kpe"] + 32].unsqueeze(1)
                        groups.append((kp[:, :, 0:16], kp[:, :, 16:32], co, si))
                    rotate(c, groups, 16)
                    qt_ = c.sb(sm, "mla_qt", [MLA_QK, MLA_HEADS, TOK])
                    kt_ = c.sb(sm, "mla_kt", [MLA_QK, MLA_HEADS, TOK])
                    with ExitStack() as sn:
                        kk = c.sb(sn, "mla_k", [P, 2, MLA_HEADS, MLA_QK])

                        def assemble(dve, link):
                            for t in range(2):
                                src = kv[:, t, :].rearrange("p (h d) -> p h d", d=2 * MLA_NOPE)[:, :, 0:MLA_NOPE]
                                dve.tensor_copy(kk[:, t, :, 0:MLA_NOPE], src)
                                pe_ = h[:, t, O["kpe"]:O["kpe"] + 32].unsqueeze(1).to_broadcast([P, MLA_HEADS, MLA_ROPE])
                                dve.tensor_copy(kk[:, t, :, MLA_NOPE:MLA_QK], pe_)
                        on_vector(c, assemble)
                        turn(c, lambda t, k: q[:, t, k * MLA_QK:(k + 1) * MLA_QK], qt_, MLA_HEADS, 2, MLA_QK, ident, split=False)
                        turn(c, lambda t, k: kk[:, t, k, :], kt_, MLA_HEADS, 2, MLA_QK, ident, split=False)
                    units = []
                    for hh in range(MLA_HEADS):
                        for t in range(2):
                            units.append(dict(q=[qt_[:, hh, t * P:(t + 1) * P]], keys=[kt_[:, hh, :]],
                                              v=[kv[:, j, hh * 128 + 64:hh * 128 + 128] for j in range(2)],
                                              out=o[:, t, hh * 64:hh * 64 + 64]))
                    groups = []
                    for t in range(2):
                        for part in ("dq", "dk"):
                            v = h[:, t, O[part]:O[part] + 1024].rearrange("p (h d) -> p h d", d=DIFF_D)
                            groups.append((v[:, :, 0:8], v[:, :, 8:16], angles[:, t, 0, 16:24], angles[:, t, 1, 16:24]))
                    turned = rotation_scratch(c, sm, groups[:1], 8)

                    def diff_rotation(pool, link, groups=groups, turned=turned):
                        for g in groups:
                            for ins in rotation_products(pool, [g], 8, turned):
                                link(ins)
                            for ins in rotation_sums(pool, [g], 8, turned):
                                link(ins)
                    attention(c, units, MLA_QK ** -0.5, ident, pool_work=diff_rotation)
                with ExitStack() as sm:
                    ld = c.sb(sm, "lam_dot", [P, 2])
                    neg = c.sb(sm, "neg_lambda", [P, 1])

                    def dots(dve, link):
                        lv = lam[:, :, :].rearrange("p (a b) d -> p a b d", b=2)
                        link(dve.tensor_tensor(lv[:, :, 0, :], lv[:, :, 0, :], lv[:, :, 1, :], ALU.mult))
                        link(dve.tensor_reduce(ld[:, :], lv[:, :, 0, :], AX, ALU.add))
                    on_vector(c, dots)
                    on_scalar(c, lambda act, link: act.activation(ld[:, :], ld[:, :], ACT.Exp))

                    def lam_full(dve, link):
                        link(dve.tensor_tensor(neg[:, :], ld[:, 1:2], ld[:, 0:1], ALU.subtract))
                        link(dve.tensor_scalar(neg[:, :], neg[:, :], -lam0, None, ALU.add))
                    on_vector(c, lam_full)
                    dt_ = c.sb(sm, "diff_t", [P, 16, TOK])
                    turn(c, lambda t, k: h[:, t, O["dq"] + k * P:O["dq"] + (k + 1) * P], dt_, 16, 2, P, ident, split=False)
                    units = []
                    for hh in range(DIFF_HEADS):
                        for t in range(2):
                            units.append(dict(q=[dt_[64 * m:64 * m + 64, hh, t * P:(t + 1) * P] for m in range(2)],
                                              keys=[dt_[64 * m:64 * m + 64, 8 + hh, :] for m in range(2)],
                                              v=[h[:, j, O["dv"] + hh * 128:O["dv"] + (hh + 1) * 128] for j in range(2)],
                                              out=o[:, t, 512 + hh * 128:512 + (hh + 1) * 128]))
                    attention(c, units, DIFF_D ** -0.5, ident, pair=neg[:, :])
                with ExitStack() as sm:
                    mkv = c.sb(sm, "mem_kv", [P, 2, 1024])
                    diff_roots = c.sb(sm, "diff_roots", [P, 2, 8])
                    with ExitStack() as sn:
                        mem = c.sb(sn, "mem", [P, 2, D])
                        head_rms(c, o[:, :, 512:1536], 2, 8, 128, None, 1e-5, extra=1.0 - lam0, roots=diff_roots,
                                 loads=[(mem[:, :, :], A["mem_2"][0].rearrange("(t p) d -> p t d", p=P))])
                        c.arrived()
                        mt = [c.sb(sn, "mem_hi", [P, KT, TOK], F32R), c.sb(sn, "mem_lo", [P, KT, TOK], F32R)]
                        turn(c, lambda t, k: mem[:, t, k * P:(k + 1) * P], mt, KT, 2, P, ident)
                        project(c, S["memkv"], lhs_of(mt), 2, into(mkv, 256))
                    mq = c.sb(sm, "mem_qt", [P, 4, TOK])
                    mk = c.sb(sm, "mem_kt", [P, 4, TOK])
                    turn(c, lambda t, k: h[:, t, O["mq"] + k * P:O["mq"] + (k + 1) * P], mq, 4, 2, P, ident, split=False)
                    turn(c, lambda t, k: mkv[:, t, k * P:(k + 1) * P], mk, 4, 2, P, ident, split=False)
                    units = []
                    for hh in range(MEM_HEADS):
                        for t in range(2):
                            units.append(dict(q=[mq[:, hh, t * P:(t + 1) * P]], keys=[mk[:, hh, :]],
                                              v=[mkv[:, j, 512 + hh * 128:512 + (hh + 1) * 128] for j in range(2)],
                                              out=o[:, t, 1536 + hh * 128:1536 + (hh + 1) * 128]))

                    def diff_norm(pool, link, roots=diff_roots, sub=sub):
                        for t in range(2):
                            v = o[:, t, 512:1536]
                            vh = v.rearrange("p (h d) -> p h d", d=128)
                            link(pool.tensor_tensor(vh, vh, roots[:, t, :].unsqueeze(2).to_broadcast([P, 8, 128]), ALU.mult))
                            link(pool.tensor_tensor(v, v, sub[:, :], ALU.mult))
                    attention(c, units, MEM_HD ** -0.5, ident, pool_work=diff_norm)
            if stop == f"branches{l}":
                return
            with ExitStack() as sn:
                ot = [c.sb(sn, "o_hi", [P, 16, TOK], F32R), c.sb(sn, "o_lo", [P, 16, TOK], F32R)]
                turn(c, lambda t, k: o[:, t, k * P:(k + 1) * P], ot, 16, 2, P, ident)
                for br, key in enumerate(("b0", "b1", "b2")):
                    k0 = BRANCH_ROWS[br] // P
                    cw = 512 if br != 1 else 256

                    def gated(dve, n, v, br=br, cw=cw):
                        m = merged_in[:, :, br * D + n * cw:br * D + (n + 1) * cw]
                        return dve.tensor_tensor(m, v, m, ALU.mult)
                    def add_up(pool, n, br=br, cw=cw):
                        m0, m = (merged_in[:, :, b_ * D + n * cw:b_ * D + (n + 1) * cw] for b_ in (0, br))
                        return pool.tensor_tensor(m0, m0, m, ALU.add)
                    project(c, S[key], [lambda n, k, a=a, k0=k0: a[:, k0 + k, :] for a in ot], 2, gated, on_act=False,
                            pool_then=add_up if br > 0 else None)
            with ExitStack() as sn:
                mt = [c.sb(sn, "m_hi", [P, KT, TOK], F32R), c.sb(sn, "m_lo", [P, KT, TOK], F32R)]
                y = c.sb(sn, "y2", [P, 2, D])
                gb = c.sb(sn, "ln", [P, 2, D])
                turn(c, lambda t, k: merged_in[:, t, k * P:(k + 1) * P], mt, KT, 2, P, ident,
                     loads=[(gb[:, 0, :], A["ln1_g_2"][l:l + 1].to_broadcast([P, D])),
                            (gb[:, 1, :], A["ln1_b_2"][l:l + 1].to_broadcast([P, D]))])
                project(c, S["out"], lhs_of(mt), 2, into(y, 256))
                c.arrived()
                layer_norm(c, x, y, gb[:, 0, :], gb[:, 1, :])
    if stop == f"attn2_{l}":
        return
    with ExitStack() as sn:
        xt = [c.sb(sn, "x2_hi", [P, KT, TOK], F32R), c.sb(sn, "x2_lo", [P, KT, TOK], F32R)]
        y = c.sb(sn, "y2", [P, 2, D])
        gb = c.sb(sn, "ln", [P, 2, D])
        turn(c, lambda t, k: x[:, t, k * P:(k + 1) * P], xt, KT, 2, P, ident,
             loads=[(gb[:, 0, :], A["ln2_g_2"][l:l + 1].to_broadcast([P, D])),
                    (gb[:, 1, :], A["ln2_b_2"][l:l + 1].to_broadcast([P, D]))])
        relu_squared_mlp(c, A["mlp_w1_2"][l], A["mlp_w2_2"][l], xt, y)
        c.arrived()
        layer_norm(c, x, y, gb[:, 0, :], gb[:, 1, :])


_INS = ["x", "c", "ctx", "c_ctx", "w_mod", "b_mod", "ffn1_w1", "ffn1_w3", "ffn1_w2", "w_in", "na_q_norm", "na_k_norm",
        "na_rpb", "gla_w_gate_f", "gla_b_gate_f", "gla_w_gate_b", "gla_b_gate_b", "gla_norm", "gqa_q_norm", "gqa_k_norm",
        "w_out", "ffn2_w1", "ffn2_w3", "ffn2_w2", "mem_2", "positions_2", "w_in_2", "b_gate_2", "mla_q_norm_2",
        "mla_kv_norm_2", "mla_w_uq_2", "mla_w_ukv_2", "diff_lambda_2", "diff_subln_2", "mem_w_kv_2", "w_branch_2",
        "w_out_2", "ln1_g_2", "ln1_b_2", "mlp_w1_2", "mlp_w2_2", "ln2_g_2", "ln2_b_2"]


def kernel(**inputs):
    import concourse.bacc as _bacc
    from concourse.bass_utils import run_bass_kernel_spmd as _run

    nc = _bacc.Bacc("TRN2", target_bir_lowering=False, num_devices=1)
    arrays, A = {}, {}
    given = {name: np.ascontiguousarray(inputs[name]) for name in _INS}
    given.update(shape_constants())
    for name, a in given.items():
        arrays[f"in_{name}_dram"] = a
        A[name] = nc.dram_tensor(f"in_{name}_dram", a.shape, mybir.dt.from_np(a.dtype), kind="ExternalInput").ap()
    out = nc.dram_tensor("out_0_dram", (1, TOK, D), F32, kind="ExternalOutput").ap()
    encoder_program(nc, A, out)
    r = _run(nc, [arrays], core_ids=[0])
    return r.results[0]["out_0_dram"]
```
